# Optimizing a Trainium2 kernel written in Bass

```python
import math
import jax, jax.numpy as jnp
from jax import lax
import numpy as np

D_MODEL = 1024
BATCH = 1
SEQ = 512
DEPTH = 1

HEAD_DIM = 64
NSA_HEADS = 8
NSA_KV_GROUPS = 2
NSA_GROUP_SIZE = NSA_HEADS // NSA_KV_GROUPS
CMP_BLOCK = 32
CMP_STRIDE = 16
CMP_HIDDEN = 128
SEL_BLOCK = 64
SEL_TOP_N = 16
WINDOW = 512
Q_BLOCK = 128
FORCE_BONUS = 1.0e4
ROPE_THETA = 500000.0
ROPE_DIM = HEAD_DIM // 4

SGU_GROUPS = 4
SGU_CHUNK = 128
SGU_WIDTH = 512
SGU_GROUP_DIM = SGU_WIDTH // SGU_GROUPS

FFN_HIDDEN = -(-(8 * D_MODEL) // (3 * 256)) * 256

Q_WIDTH = NSA_HEADS * HEAD_DIM
KV_WIDTH = NSA_KV_GROUPS * HEAD_DIM
NSA_GATE_WIDTH = 3 * NSA_HEADS
MERGE_GATE_WIDTH = 2 * D_MODEL
IN_PROJ_WIDTH = Q_WIDTH + 6 * KV_WIDTH + NSA_GATE_WIDTH + 2 * SGU_WIDTH + MERGE_GATE_WIDTH

DEEPNORM_ALPHA = (2.0 * DEPTH) ** 0.25
DEEPNORM_BETA = (8.0 * DEPTH) ** -0.25
LN_EPS = 1e-5
NEG_INF = -1e30

kernel_name = "nsa_gmlp_hybrid_deepnorm"

def _split_points():
    sizes = [Q_WIDTH] + [KV_WIDTH] * 6 + [NSA_GATE_WIDTH, SGU_WIDTH, SGU_WIDTH, MERGE_GATE_WIDTH]
    return [int(v) for v in np.cumsum(sizes)[:-1]]

def layer_norm(x, g, b):
    xf = x.astype(jnp.float32)
    mu = jnp.mean(xf, axis=-1, keepdims=True)
    var = jnp.mean(jnp.square(xf - mu), axis=-1, keepdims=True)
    y = (xf - mu) * lax.rsqrt(var + LN_EPS) * g.astype(jnp.float32) + b.astype(jnp.float32)
    return y.astype(x.dtype)

def partial_rope(x, positions):
    half = ROPE_DIM // 2
    freqs = ROPE_THETA ** (-jnp.arange(half, dtype=jnp.float32) / half)
    ang = positions.astype(jnp.float32)[..., None] * freqs
    cos = jnp.cos(ang)[:, :, None, :]
    sin = jnp.sin(ang)[:, :, None, :]
    xr = x[..., :ROPE_DIM].astype(jnp.float32)
    x1, x2 = xr[..., :half], xr[..., half:]
    rot = jnp.concatenate([x1 * cos - x2 * sin, x2 * cos + x1 * sin], axis=-1).astype(x.dtype)
    return jnp.concatenate([rot, x[..., ROPE_DIM:]], axis=-1)

def masked_softmax(s, mask):
    s = jnp.where(mask, s.astype(jnp.float32), NEG_INF)
    p = jax.nn.softmax(s, axis=-1)
    return jnp.where(mask, p, 0.0)

def compress(tokens, pe, w1, w2):
    B, S, G, dh = tokens.shape
    c = tokens.reshape(B, S // CMP_STRIDE, CMP_STRIDE, G, dh)
    blocks = jnp.concatenate([c[:, :-1], c[:, 1:]], axis=2)
    blocks = blocks + pe[None, None, :, None, :]
    nc = blocks.shape[1]
    flat = blocks.transpose(0, 1, 3, 2, 4).reshape(B, nc, G, CMP_BLOCK * dh)
    return jax.nn.silu(flat @ w1) @ w2

def native_sparse_attention(q, k_cmp, v_cmp, k_sel, v_sel, k_win, v_win, gates,
                            pe_ck, w_ck1, w_ck2, pe_cv, w_cv1, w_cv2):
    B, S, H, dh = q.shape
    G, R = NSA_KV_GROUPS, NSA_GROUP_SIZE
    kc = compress(k_cmp, pe_ck, w_ck1, w_ck2)
    vc = compress(v_cmp, pe_cv, w_cv1, w_cv2)
    NC = kc.shape[1]
    NS = S // SEL_BLOCK
    n_sel = min(SEL_TOP_N, NS)
    NQ = S // Q_BLOCK
    cmp_end = jnp.arange(NC) * CMP_STRIDE + CMP_BLOCK - 1
    cs = jnp.arange(NC)[:, None] * CMP_STRIDE
    ss = jnp.arange(NS)[None, :] * SEL_BLOCK
    overlap = jnp.clip(jnp.minimum(cs + CMP_BLOCK, ss + SEL_BLOCK) - jnp.maximum(cs, ss), 0, None).astype(jnp.float32) / CMP_BLOCK
    ks_blocks = k_sel.reshape(B, NS, SEL_BLOCK, G, dh).transpose(0, 3, 1, 2, 4)
    vs_blocks = v_sel.reshape(B, NS, SEL_BLOCK, G, dh).transpose(0, 3, 1, 2, 4)
    kw_pad = jnp.pad(k_win, ((0, 0), (WINDOW, 0), (0, 0), (0, 0)))
    vw_pad = jnp.pad(v_win, ((0, 0), (WINDOW, 0), (0, 0), (0, 0)))
    b_idx = jnp.arange(B)[:, None, None, None]
    g_idx = jnp.arange(G)[None, :, None, None]
    scale = HEAD_DIM ** -0.5
    sel_j = jnp.arange(NS)

    def one_block(c):
        start = c * Q_BLOCK
        t = start + jnp.arange(Q_BLOCK)
        qb = lax.dynamic_slice_in_dim(q, start, Q_BLOCK, axis=1).reshape(B, Q_BLOCK, G, R, dh) * scale
        gb = lax.dynamic_slice_in_dim(gates, start, Q_BLOCK, axis=1).reshape(B, Q_BLOCK, G, R, 3)
        s_c = jnp.einsum('bqgrd,bngd->bgrqn', qb, kc)
        p_c = masked_softmax(s_c, cmp_end[None, :] <= t[:, None])
        o_cmp = jnp.einsum('bgrqn,bngd->bqgrd', p_c.astype(vc.dtype), vc)
        imp = jnp.einsum('bgrqn,nj->bgqj', p_c, overlap)
        cur = t // SEL_BLOCK
        valid = sel_j[None, :] <= cur[:, None]
        forced = (sel_j[None, :] == 0) | (sel_j[None, :] == cur[:, None]) | (sel_j[None, :] == cur[:, None] - 1)
        score = jnp.where(valid, imp + jnp.where(forced, FORCE_BONUS, 0.0), NEG_INF)
        top_val, top_idx = lax.top_k(score, n_sel)
        top_ok = top_val > 0.5 * NEG_INF
        gk = ks_blocks[b_idx, g_idx, top_idx]
        gv = vs_blocks[b_idx, g_idx, top_idx]
        kpos = top_idx[..., None] * SEL_BLOCK + jnp.arange(SEL_BLOCK)
        m_s = top_ok[..., None] & (kpos <= t[None, None, :, None, None])
        s_s = jnp.einsum('bqgrd,bgqnkd->bgrqnk', qb, gk).reshape(B, G, R, Q_BLOCK, n_sel * SEL_BLOCK)
        p_s = masked_softmax(s_s, m_s.reshape(B, G, 1, Q_BLOCK, n_sel * SEL_BLOCK))
        o_sel = jnp.einsum('bgrqm,bgqmd->bqgrd', p_s.astype(gv.dtype), gv.reshape(B, G, Q_BLOCK, n_sel * SEL_BLOCK, dh))
        kw = lax.dynamic_slice_in_dim(kw_pad, start, WINDOW + Q_BLOCK, axis=1)
        vw = lax.dynamic_slice_in_dim(vw_pad, start, WINDOW + Q_BLOCK, axis=1)
        wpos = start - WINDOW + jnp.arange(WINDOW + Q_BLOCK)
        m_w = (wpos[None, :] <= t[:, None]) & (wpos[None, :] > t[:, None] - WINDOW) & (wpos[None, :] >= 0)
        s_w = jnp.einsum('bqgrd,bkgd->bgrqk', qb, kw)
        p_w = masked_softmax(s_w, m_w)
        o_win = jnp.einsum('bgrqk,bkgd->bqgrd', p_w.astype(vw.dtype), vw)
        out = gb[..., 0:1] * o_cmp + gb[..., 1:2] * o_sel + gb[..., 2:3] * o_win
        return out.reshape(B, Q_BLOCK, H * dh)

    outs = lax.map(one_block, jnp.arange(NQ))
    return outs.transpose(1, 0, 2, 3).reshape(B, S, H * dh)

def spatial_gating(u, v, ln_g, ln_b, w_s, b_s):
    B, S, _ = u.shape
    u = jax.nn.gelu(u)
    v = layer_norm(jax.nn.gelu(v), ln_g, ln_b)
    vc = v.reshape(B, S // SGU_CHUNK, SGU_CHUNK, SGU_GROUPS, SGU_GROUP_DIM)
    causal = jnp.tril(jnp.ones((SGU_CHUNK, SGU_CHUNK), dtype=bool))
    w = jnp.where(causal, w_s, 0.0).astype(v.dtype)
    mixed = jnp.einsum('gts,bnsgc->bntgc', w, vc) + b_s.T[None, None, :, :, None]
    return u * mixed.reshape(B, S, SGU_WIDTH)

def setup_inputs(seed: int = 0) -> dict:
    key = jax.random.key(seed)
    ks = jax.random.split(key, 24)
    L = DEPTH

    def nrm(k, shape, scale):
        return jax.random.normal(k, shape, jnp.float32) * scale

    x = nrm(ks[0], (BATCH, SEQ, D_MODEL), 1.0)
    positions = jnp.arange(SEQ, dtype=jnp.int32)[None, :] + jax.random.randint(ks[1], (BATCH, 1), 0, 1024, dtype=jnp.int32)
    return {
        'x': x,
        'positions': positions,
        'w_in': nrm(ks[2], (L, D_MODEL, IN_PROJ_WIDTH), D_MODEL ** -0.5),
        'pe_ck': nrm(ks[3], (L, CMP_BLOCK, HEAD_DIM), 0.1),
        'w_ck1': nrm(ks[4], (L, CMP_BLOCK * HEAD_DIM, CMP_HIDDEN), (CMP_BLOCK * HEAD_DIM) ** -0.5),
        'w_ck2': nrm(ks[5], (L, CMP_HIDDEN, HEAD_DIM), CMP_HIDDEN ** -0.5),
        'pe_cv': nrm(ks[6], (L, CMP_BLOCK, HEAD_DIM), 0.1),
        'w_cv1': nrm(ks[7], (L, CMP_BLOCK * HEAD_DIM, CMP_HIDDEN), (CMP_BLOCK * HEAD_DIM) ** -0.5),
        'w_cv2': nrm(ks[8], (L, CMP_HIDDEN, HEAD_DIM), CMP_HIDDEN ** -0.5),
        'ln_sgu_g': 1.0 + nrm(ks[9], (L, SGU_WIDTH), 0.1),
        'ln_sgu_b': nrm(ks[10], (L, SGU_WIDTH), 0.1),
        'w_spatial': nrm(ks[11], (L, SGU_GROUPS, SGU_CHUNK, SGU_CHUNK), SGU_CHUNK ** -0.5),
        'b_spatial': 1.0 + nrm(ks[12], (L, SGU_GROUPS, SGU_CHUNK), 0.1),
        'w_branch_nsa': nrm(ks[13], (L, Q_WIDTH, D_MODEL), DEEPNORM_BETA * Q_WIDTH ** -0.5),
        'w_branch_sgu': nrm(ks[14], (L, SGU_WIDTH, D_MODEL), DEEPNORM_BETA * SGU_WIDTH ** -0.5),
        'w_out': nrm(ks[15], (L, D_MODEL, D_MODEL), DEEPNORM_BETA * D_MODEL ** -0.5),
        'ln1_g': 1.0 + nrm(ks[16], (L, D_MODEL), 0.1),
        'ln1_b': nrm(ks[17], (L, D_MODEL), 0.1),
        'w_ffn_gate': nrm(ks[18], (L, D_MODEL, FFN_HIDDEN), DEEPNORM_BETA * D_MODEL ** -0.5),
        'w_ffn_up': nrm(ks[19], (L, D_MODEL, FFN_HIDDEN), DEEPNORM_BETA * D_MODEL ** -0.5),
        'w_ffn_down': nrm(ks[20], (L, FFN_HIDDEN, D_MODEL), DEEPNORM_BETA * FFN_HIDDEN ** -0.5),
        'ln2_g': 1.0 + nrm(ks[21], (L, D_MODEL), 0.1),
        'ln2_b': nrm(ks[22], (L, D_MODEL), 0.1),
    }

def reference(x, positions, w_in, pe_ck, w_ck1, w_ck2, pe_cv, w_cv1, w_cv2, ln_sgu_g, ln_sgu_b,
              w_spatial, b_spatial, w_branch_nsa, w_branch_sgu, w_out, ln1_g, ln1_b,
              w_ffn_gate, w_ffn_up, w_ffn_down, ln2_g, ln2_b):
    B, S, _ = x.shape
    splits = _split_points()
    h = x
    for l in range(DEPTH):
        proj = h @ w_in[l]
        q, k_c, v_c, k_s, v_s, k_w, v_w, nsa_gl, u, v, merge_gl = jnp.split(proj, splits, axis=-1)
        q = partial_rope(q.reshape(B, S, NSA_HEADS, HEAD_DIM), positions)
        kv = lambda a: a.reshape(B, S, NSA_KV_GROUPS, HEAD_DIM)
        k_c = partial_rope(kv(k_c), positions)
        k_s = partial_rope(kv(k_s), positions)
        k_w = partial_rope(kv(k_w), positions)
        nsa_gates = jax.nn.sigmoid(nsa_gl).reshape(B, S, NSA_HEADS, 3)
        o_nsa = native_sparse_attention(q, k_c, kv(v_c), k_s, kv(v_s), k_w, kv(v_w), nsa_gates,
                                        pe_ck[l], w_ck1[l], w_ck2[l], pe_cv[l], w_cv1[l], w_cv2[l])
        o_sgu = spatial_gating(u, v, ln_sgu_g[l], ln_sgu_b[l], w_spatial[l], b_spatial[l])
        g_nsa, g_sgu = jnp.split(jax.nn.sigmoid(merge_gl), 2, axis=-1)
        merged = g_nsa * (o_nsa @ w_branch_nsa[l]) + g_sgu * (o_sgu @ w_branch_sgu[l])
        mix = merged @ w_out[l]
        h = layer_norm(DEEPNORM_ALPHA * h + mix, ln1_g[l], ln1_b[l])
        ffn = (jax.nn.silu(h @ w_ffn_gate[l]) * (h @ w_ffn_up[l])) @ w_ffn_down[l]
        h = layer_norm(DEEPNORM_ALPHA * h + ffn, ln2_g[l], ln2_b[l])
    return h


_drawn_inputs = setup_inputs


def setup_inputs(seed=0):
    import zlib

    import numpy as np

    out = dict(_drawn_inputs(seed))
    spreads = {}
    factors = {'pe_ck': 8.0,
     'w_ck1': 7.271,
     'w_ck2': 7.353,
     'pe_cv': 8.0,
     'w_cv1': 3.005,
     'ln_sgu_g': 7.799,
     'ln_sgu_b': 7.562,
     'b_spatial': 5.558}
    for name, (base, spread) in spreads.items():
        noise = np.random.default_rng([zlib.crc32(name.encode()), seed]).standard_normal(out[name].shape)
        drawn = base * np.exp(spread * noise) if base else spread * noise
        out[name] = __import__('jax').numpy.asarray(drawn.astype(out[name].dtype))
    for name, factor in factors.items():
        out[name] = (out[name] * factor).astype(out[name].dtype)
    return out
```

```python
def build_layer(nc, T):
    import math
    from contextlib import ExitStack

    import numpy as np

    import concourse.bass as bass
    from concourse import mybir

    fp32 = mybir.dt.float32
    f32r = mybir.dt.float32r
    i32 = mybir.dt.int32
    ALU = mybir.AluOpType
    ACT = mybir.ActivationFunctionType
    AX = mybir.AxisListType
    ds = bass.ds

    P = 128
    SEQ, D = T["x"].shape[1:]
    MT = SEQ // P
    KD = D // P
    DH = 64
    G, R = 2, 4
    PAIRS = R
    NCB = 31
    NB = 32
    STRIDE, BLOCK = 16, 32
    HID = T["w_ck2"].shape[1]
    SG = 512
    F = T["w_ffn_gate"].shape[2]
    FT = F // P
    HALF = 8
    SCALE = DH ** -0.5
    NEG = -1e30
    ALPHA = 2.0 ** 0.25
    EPS = 1e-5
    GATE_W = 3 * G * R

    C_Q, C_KVA, C_KVB = 0, 512, 1024
    N_KVB = 2 * P + GATE_W
    C_U = C_KVB + N_KVB
    C_V = C_U + SG
    C_MERGE = C_V + SG

    U_Q, U_KVA, U_KVB, U_V, U_U = 0, 2, 4, 6, 8
    U_MERGE0 = 10
    U_CK, U_CV = 11, 12
    U_MERGE = 13
    N_MERGE = 2 * D // 256
    U_BRANCH = U_MERGE + N_MERGE - 1
    U_OUT = U_BRANCH + 4
    U_FFN = U_OUT + 4
    U_DOWN = U_FFN + FT
    N_DOWN = FT // 2

    x_d = T["x"][0].rearrange("(m p) c -> p m c", p=P)
    out_d = T["out"][0].rearrange("(m p) c -> p m c", p=P)
    w_in_d = T["w_in"][0].rearrange("(k p) n -> p k n", p=P)
    ck1_d = T["w_ck1"][0].rearrange("(j p) h -> p j h", p=P)
    cv1_d = T["w_cv1"][0].rearrange("(j p) h -> p j h", p=P)
    nsa_d = T["w_branch_nsa"][0].rearrange("(g k d) n -> g d k n", g=G, k=PAIRS)
    sgu_d = T["w_branch_sgu"][0].rearrange("(k p) n -> p k n", p=P)
    wout_d = T["w_out"][0].rearrange("(k p) n -> p k n", p=P)
    gate_d = T["w_ffn_gate"][0].rearrange("(k p) n -> p k n", p=P)
    up_d = T["w_ffn_up"][0].rearrange("(k p) n -> p k n", p=P)
    down_d = T["w_ffn_down"][0].rearrange("(f p) n -> p f n", p=P)

    def as_rows(v):
        return v.rearrange("n -> () n").broadcast_to([P, v.shape[0]])

    FREQ = [float(np.float32(500000.0 ** (-j / HALF))) for j in range(HALF)]
    MAGIC = 1.5 * 2.0 ** 23
    PI_1 = 6.28125
    PI_2 = round((2 * math.pi - PI_1) * 2.0 ** 20) / 2.0 ** 20
    PI_3 = 2 * math.pi - PI_1 - PI_2
    PI_IN = 3.1415925

    with ExitStack() as ctx:
        def sb(name, shape, dt, scope=ctx):
            return scope.enter_context(nc.sbuf_tensor(name, shape, dt))

        def sem(name):
            return ctx.enter_context(nc.semaphore(name))

        stage = sb("stage", [P, 2, 2048], fp32)
        wh = sb("wh", [P, 2, 2048], f32r)
        wl = sb("wl", [P, 2, 2048], f32r)
        xh = sb("xh", [P, KD, SEQ], f32r)
        xl = sb("xl", [P, KD, SEQ], f32r)
        ath = sb("ath", [P, 4096], f32r)
        atl = sb("atl", [P, 4096], f32r)
        ident = sb("ident", [P, P], fp32)
        stat = sb("stat", [P, 2, 6], fp32)
        mv = sb("mv", [P, 2], fp32)
        nrm = sb("nrm", [P, 8], fp32)

        first = ExitStack()
        prob = sb("prob", [P, 2, G, SEQ], fp32, first)
        pcmp = sb("pcmp", [P, G, MT, PAIRS, NB], fp32, first)
        pth = sb("pth", [P, 1024], f32r, first)
        ptl = sb("ptl", [P, 1024], f32r, first)
        arena = sb("arena", [P, 10240], fp32, first)
        oth = sb("oth", [P, PAIRS, SEQ], f32r, first)
        otl = sb("otl", [P, PAIRS, SEQ], f32r, first)
        ln_g = sb("ln_g", [P, SG], fp32, first)
        ln_b = sb("ln_b", [P, SG], fp32, first)
        wsp = sb("wsp", [P, 4, P], fp32, first)
        wth = sb("wth", [P, 4, P], f32r, first)
        wtl = sb("wtl", [P, 4, P], f32r, first)
        bsp = sb("bsp", [P, 4], fp32, first)
        causal = sb("causal", [P, P], fp32, first)
        cbias = sb("cbias", [P, MT, NB], fp32, first)
        cmask = sb("cmask", [P, MT, NB], fp32, first)
        pos_i = sb("pos_i", [P, MT], i32, first)
        pos_f = sb("pos_f", [P, MT], fp32, first)
        freq = sb("freq", [P, HALF], fp32, first)
        ang = sb("ang", [P, 2, MT, HALF], fp32, first)
        turns = sb("turns", [P, 2, MT, HALF], fp32, first)
        tmp_b = sb("tmp_b", [P, 2, MT, HALF], fp32, first)
        trig = sb("trig", [P, 2, MT, HALF], fp32, first)
        gates = sb("gates", [P, MT, G, R, 3], fp32, first)
        pe_in = sb("pe_in", [16, 2, P], fp32, first)
        pe_t = sb("pe_t", [P, 2, 16], fp32, first)
        w2 = sb("w2", [P, 3, DH], fp32, first)
        w2h = sb("w2h", [P, 3, DH], f32r, first)
        w2l = sb("w2l", [P, 3, DH], f32r, first)
        hidh = sb("hidh", [P, 2, G * NB], f32r, first)
        hidl = sb("hidl", [P, 2, G * NB], f32r, first)
        kch = sb("kch", [P, NB], f32r, first)
        kcl = sb("kcl", [P, NB], f32r, first)
        vch = sb("vch", [NB, P], f32r, first)
        vcl = sb("vcl", [NB, P], f32r, first)
        nmax = sb("nmax", [P, 2, G], fp32, first)
        rsum = sb("rsum", [P, 2, G], fp32, first)
        rinv = sb("rinv", [P, 2, G], fp32, first)
        vstat = sb("vstat", [P, MT, 6], fp32, first)
        vmv = sb("vmv", [P, MT, 2], fp32, first)
        vrs = sb("vrs", [P, 4, MT], fp32, first)
        first.close()

        second = ExitStack()
        hid_sg = sb("hid_sg", [P, 2, SEQ], fp32, second)
        y = sb("y", [P, MT, D], fp32, second)
        fact = sb("fact", [P, FT, SEQ], fp32, second)
        lng = sb("lng", [P, 2, D], fp32, second)
        lnb = sb("lnb", [P, 2, D], fp32, second)
        second.close()

        raw = arena[:, :].rearrange("p (c m n) -> p c m n", c=5, m=MT)
        q_raw, kva, v_raw, u_raw = raw[:, 0], raw[:, 1], raw[:, 2], raw[:, 4]
        kvb = arena[:, 6144:6144 + MT * N_KVB].rearrange("p (m n) -> p m n", m=MT)
        kvb_end = 6144 + MT * N_KVB
        hid = arena[:, kvb_end:kvb_end + 2 * G * NB].rearrange("p (c e) -> p c e", c=2)
        cmax = arena[:, kvb_end + 128:kvb_end + 160]
        csum_f = arena[:, kvb_end + 160:kvb_end + 192]
        csum = csum_f.rearrange("p (g m k) -> p g m k", g=G, m=MT)
        x_sb = arena[:, 4096:8192].rearrange("p (m c) -> p m c", m=MT)
        merge = arena[:, 0:16 * SEQ].rearrange("p (f t) -> p f t", f=16)
        q_perm = prob[:, :, :, :].rearrange("p a b c -> p (a b c)").rearrange("p (m n) -> p m n", m=MT)
        q_view = q_perm.rearrange("p m (k g d) -> p m g k d", k=PAIRS, g=G)
        pc_flat = pcmp[:, :, :, :, :].rearrange("p a b c d -> p (a b c d)")
        rope_t = pc_flat.rearrange("p (t m h j) -> p t m h j", t=4, m=MT, h=8)
        tok2 = pc_flat.rearrange("p (c g t) -> p c g t", c=2, g=G)
        flat = prob[:, :, :, :].rearrange("p a b c -> p a (b c)").rearrange(
            "p c (j g n) -> p c j g n", j=16, g=G)
        flath = oth[:, :, :].rearrange("p a b -> p (a b)").rearrange("p (c e) -> p c e", c=2)
        flatl = otl[:, :, :].rearrange("p a b -> p (a b)").rearrange("p (c e) -> p c e", c=2)

        def att(t, off, n):
            return t[:, off:off + n]

        def q_t(t):
            return att(t, 0, 2048).rearrange("p (k s) -> p k s", k=PAIRS)

        def k_t(t, br):
            return att(t, 2048 + 512 * br, 512)

        def v_t(t, br):
            return att(t, 3072 + 512 * br, 512).rearrange("p (m n) -> p m n", m=MT)

        sgh = att(ath, 0, 2048).rearrange("p (k s) -> p k s", k=4)
        sgl = att(atl, 0, 2048).rearrange("p (k s) -> p k s", k=4)
        hth = ath[:, :].rearrange("p (k s) -> p k s", k=KD)
        htl = atl[:, :].rearrange("p (k s) -> p k s", k=KD)
        ah = xh[:, :, :].rearrange("p (r f) s -> p r f s", f=2)
        al = xl[:, :, :].rearrange("p (r f) s -> p r f s", f=2)

        ps = ctx.enter_context(nc.psum_tensor("ps", [P, 8, 512], fp32))
        PT0, O0, M0 = 2, 4, 6

        def w4(t, slot, n=512):
            return t[:, slot, 0:4 * n].rearrange("p (k n) -> p k n", k=4)

        def w8(t, slot):
            return t[:, slot, :].rearrange("p (k n) -> p k n", k=8)

        def w2d(t, slot):
            return t[:, slot, :].rearrange("p (f n) -> p f n", f=2)

        def w16(t, slot):
            return t[:, slot, :].rearrange("p (j h) -> p j h", j=16)

        w_arrived = [sem("w_arrived0"), sem("w_arrived1")]
        w_hi, w_lo, w_used = sem("w_hi"), sem("w_lo"), sem("w_used")
        x_arrived = [sem("x_arrived0"), sem("x_arrived1")]
        small_arrived = sem("small_arrived")
        xt_done, xt_hi, xt_lo = sem("xt_done"), sem("xt_hi"), sem("xt_lo")
        rows_done = sem("rows_done")
        raw_act, raw_dve = sem("raw_act"), sem("raw_dve")
        pool_step, act_step, dve_step = sem("pool_step"), sem("act_step"), sem("dve_step")
        masks_ready, ang_ready, trig_ready = sem("masks_ready"), sem("ang_ready"), sem("trig_ready")
        roped = sem("roped")
        tr_done = sem("tr_done")
        tok_k, tok_v = sem("tok_k"), sem("tok_v")
        op_hi, op_lo = sem("op_hi"), sem("op_lo")
        pe_tr, pe_ok = sem("pe_tr"), sem("pe_ok")
        flat_ok = sem("flat_ok")
        w2_hi, w2_lo = sem("w2_hi"), sem("w2_lo")
        hid_ok, hid_hi, hid_lo = sem("hid_ok"), sem("hid_hi"), sem("hid_lo")
        cmp_done, cmp_hi, cmp_lo = sem("cmp_done"), sem("cmp_hi"), sem("cmp_lo")
        sc_done, sc_max, sc_exp, pcmp_ok = sem("sc_done"), sem("sc_max"), sem("sc_exp"), sem("pcmp_ok")
        gates_ok = sem("gates_ok")
        gelu_ok, vsq_in, vsq_ok, vln_ok = sem("gelu_ok"), sem("vsq_in"), sem("vsq_ok"), sem("vln_ok")
        vh_ok, vl_ok = sem("vh_ok"), sem("vl_ok")
        wt_done, wt_hi, wt_lo = sem("wt_done"), sem("wt_hi"), sem("wt_lo")
        mix_done, sgu_ok = sem("mix_done"), sem("sgu_ok")
        merge_half = sem("merge_half")
        merge_out = sem("merge_out")
        s_done, s_max, s_exp, p_ok = sem("s_done"), sem("s_max"), sem("s_exp"), sem("p_ok")
        pt_done, pt_hi, pt_lo = sem("pt_done"), sem("pt_hi"), sem("pt_lo")
        pv_done, o_hi, o_lo = sem("pv_done"), sem("o_hi"), sem("o_lo")
        st_done, st_hi, st_lo = sem("st_done"), sem("st_hi"), sem("st_lo")
        sig_ok = sem("sig_ok")
        br_done, br_prod = sem("br_done"), sem("br_prod")
        mg_ok, mg_hi, mg_lo = sem("mg_ok"), sem("mg_hi"), sem("mg_lo")
        x2_arrived, ln_arrived = sem("x2_arrived"), sem("ln_arrived")
        var_ok, sq_ok, h_ok = sem("var_ok"), sem("sq_ok"), sem("h_ok")
        ht_done, ht_hi, ht_lo = sem("ht_done"), sem("ht_hi"), sem("ht_lo")
        ffn_half, silu_ok, fact_ok = sem("ffn_half"), sem("silu_ok"), sem("fact_ok")
        a_hi, a_lo = sem("a_hi"), sem("a_lo")
        rows_out = sem("rows_out")
        stored = sem("stored")

        block = ctx.enter_context(nc.Block())

        STEPS = [(qt, pp, br) for qt in range(MT) for pp in range(PAIRS) for br in range(3)]
        N_STEPS = len(STEPS)
        SOFT = []
        for a in range(N_STEPS + 1):
            SOFT.append(sum(1 for s in STEPS[:a] if s[2] < 2))
        U_FILL0, N_FILL = U_MERGE + 1, N_MERGE - 2
        PIECES = N_FILL * 2 * KD
        FILL_AT = [PIECES * i // (N_STEPS + 2) for i in range(N_STEPS + 3)]

        def fills_done(i):
            return FILL_AT[i + 1] // KD

        class Steps:

            def __init__(self, eng, s):
                self.eng, self.s, self.n = eng, s, 0

            def __call__(self, ins):
                ins.then_inc(self.s, 1)
                self.n = self.n + 1
                self.eng.wait_ge(self.s, self.n)

        @block.sync
        def _(sp):
            def load(u, slot, parts, free=True):
                if free:
                    sp.wait_ge(w_lo, u - 1)
                for dst, src in parts:
                    sp.dma_start(dst, src).then_inc(w_arrived[slot], 16)

            def rows4(d, slot, kh, col, n):
                s = w4(stage, slot, n)
                return [(s[:, 2 * i:2 * i + 2, :], d[:, 4 * kh + 2 * i:4 * kh + 2 * i + 2, ds(col, n)])
                        for i in range(2)]

            def rows8(d, slot, col):
                s = w8(stage, slot)
                return [(s[:, 4 * i:4 * i + 4, :], d[:, 4 * i:4 * i + 4, ds(col, 256)]) for i in range(2)]

            for half in range(2):
                sp.dma_start(x_sb[:, :, 512 * half:512 * half + 512],
                             x_d[:, :, 512 * half:512 * half + 512]).then_inc(x_arrived[half], 16)
                load(half, half, rows4(w_in_d, half, half, C_Q, 512), free=False)
            smalls = [(pos_i[:, :], T["positions"][0].rearrange("(m p) -> p m", p=P)),
                      (pe_in[:, 0, :], T["pe_ck"][0].rearrange("(j a) d -> j (a d)", a=2)),
                      (pe_in[:, 1, :], T["pe_cv"][0].rearrange("(j a) d -> j (a d)", a=2)),
                      (w2[:, 0, :], T["w_ck2"][0]), (w2[:, 1, :], T["w_ck2"][0]), (w2[:, 2, :], T["w_cv2"][0]),
                      (ln_g[:, :], as_rows(T["ln_sgu_g"][0])), (ln_b[:, :], as_rows(T["ln_sgu_b"][0])),
                      (wsp[:, :, :], T["w_spatial"][0].rearrange("g t s -> t g s")),
                      (bsp[:, :], T["b_spatial"][0].rearrange("g t -> t g"))]
            for dst, src in smalls:
                sp.dma_start(dst, src, allow_slow_non_contiguous=True).then_inc(small_arrived, 16)
            for kh in range(2):
                load(U_KVA + kh, kh, rows4(w_in_d, kh, kh, C_KVA, 512))
            for kh in range(2):
                load(U_KVB + kh, kh, rows4(w_in_d, kh, kh, C_KVB, N_KVB))
            for u, col in ((U_V, C_V), (U_U, C_U)):
                for kh in range(2):
                    load(u + kh, kh, rows4(w_in_d, kh, kh, col, SG))
            load(U_MERGE0, 0, rows8(w_in_d, 0, C_MERGE))
            for u, d in ((U_CK, ck1_d), (U_CV, cv1_d)):
                s = w16(stage, u % 2)
                load(u, u % 2, [(s[:, 8 * i:8 * i + 8, :], d[:, 8 * i:8 * i + 8, :]) for i in range(2)])
            with sp.Fori(0, (N_MERGE - 2) // 2) as i:
                for b in range(2):
                    load(2 * i + U_MERGE + b, (U_MERGE + b) % 2,
                         rows8(w_in_d, (U_MERGE + b) % 2, 512 * i + C_MERGE + 256 * (1 + b)))
            load(U_BRANCH - 1, (U_BRANCH - 1) % 2, rows8(w_in_d, (U_BRANCH - 1) % 2, C_MERGE + 256 * (N_MERGE - 1)))
            with sp.Fori(0, 2) as c:
                s = w4(stage, 0)
                load(2 * c + U_BRANCH, 0,
                     [(s[DH * g:DH * g + DH, :, :], nsa_d[g][:, :, ds(512 * c, 512)]) for g in range(G)])
                load(2 * c + U_BRANCH + 1, 1, rows4(sgu_d, 1, 0, 512 * c, 512))
            sp.wait_ge(o_lo, MT * PAIRS)
            sp.dma_start(y[:, :, :], x_d).then_inc(x2_arrived, 16)
            with sp.Fori(0, 2) as c:
                for kh in range(2):
                    load(2 * c + U_OUT + kh, kh, rows4(wout_d, kh, kh, 512 * c, 512))
            sp.wait_ge(mg_lo, KD)
            for i, (g_, b_) in enumerate((("ln1_g", "ln1_b"), ("ln2_g", "ln2_b"))):
                sp.dma_start(lng[:, i, :], as_rows(T[g_][0])).then_inc(ln_arrived, 16)
                sp.dma_start(lnb[:, i, :], as_rows(T[b_][0])).then_inc(ln_arrived, 16)
            with sp.Fori(0, FT // 2) as i:
                load(2 * i + U_FFN, 0, rows8(gate_d, 0, 256 * i))
                load(2 * i + U_FFN + 1, 1, rows8(up_d, 1, 256 * i))

            def down(j, slot):
                s = w2d(stage, slot)
                load(U_DOWN + j, slot, [(s[:, f:f + 1, :], down_d[:, ds(2 * j + f, 1), :]) for f in range(2)])

            with sp.Fori(0, N_DOWN // 2) as i:
                for b in range(2):
                    down(2 * i + b, b)
            if N_DOWN % 2:
                down(N_DOWN - 1, (N_DOWN - 1) % 2)
            for m in range(MT):
                sp.wait_ge(h_ok, MT + m + 1)
                sp.dma_start(out_d[:, m, :], y[:, m, :]).then_inc(stored, 16)
            sp.wait_ge(stored, 16 * MT)

        @block.gpsimd
        def _(pool):
            step = Steps(pool, pool_step)
            step(pool.memset(ident[:, :], 0.0))
            step(pool.affine_select(out=ident[:, :], in_=ident[:, :], compare_op=ALU.not_equal, fill=1.0, base=0,
                                    pattern=[[-1, P]], channel_multiplier=1))
            step(pool.memset(causal[:, :], 0.0))
            step(pool.memset(cbias[:, :, :], 0.0))
            step(pool.memset(cmask[:, :, :], 1.0))
            pool.affine_select(out=causal[:, :], in_=causal[:, :], compare_op=ALU.is_ge, fill=NEG, base=0,
                               pattern=[[-1, P]], channel_multiplier=1).then_inc(masks_ready, 1)
            for t, fill in ((cbias, NEG), (cmask, 0.0)):
                pool.affine_select(out=t[:, :, :], in_=t[:, :, :], compare_op=ALU.is_ge, fill=fill,
                                   base=-(BLOCK - 1), pattern=[[P, MT], [-STRIDE, NB]],
                                   channel_multiplier=1).then_inc(masks_ready, 1)
            for j in range(HALF):
                step(pool.memset(freq[:, j:j + 1], FREQ[j]))
            pool.wait_ge(small_arrived, 160)
            step(pool.tensor_copy(pos_f[:, :], pos_i[:, :]))
            for i in range(2):
                for m in range(MT):
                    step(pool.tensor_scalar(ang[:, i, m, :], freq[:, :], pos_f[:, m:m + 1], None, ALU.mult))
                step(pool.tensor_scalar(turns[:, i], ang[:, i], 1.0 / (2 * math.pi), 0.25 * i, ALU.mult, ALU.add))
            step(pool.tensor_scalar(turns[:, :], turns[:, :], MAGIC, None, ALU.add))
            step(pool.tensor_scalar(turns[:, :], turns[:, :], -MAGIC, None, ALU.add))
            for part in (PI_1, PI_2, PI_3):
                step(pool.tensor_scalar(tmp_b[:, :], turns[:, :], -part, None, ALU.mult))
                step(pool.tensor_tensor(ang[:, :], ang[:, :], tmp_b[:, :], ALU.add))
            step(pool.tensor_scalar(ang[:, 1], ang[:, 1], math.pi / 2, None, ALU.add))
            pool.tensor_scalar(ang[:, :], ang[:, :], PI_IN, -PI_IN, ALU.min, ALU.max).then_inc(ang_ready, 1)
            pool.affine_select(out=wsp[:, :, :], in_=wsp[:, :, :], compare_op=ALU.is_ge, fill=0.0, base=0,
                               pattern=[[0, 4], [-1, P]], channel_multiplier=1).then_inc(masks_ready, 1)

            pool.wait_ge(trig_ready, 1)

            def rotate(src, dst, heads):
                t = [rope_t[:, i, :, 0:heads, :] for i in range(4)]
                x1, x2 = src[..., 0:HALF], src[..., HALF:2 * HALF]
                sn, cs = [trig[:, i, :, :].rearrange("p m (h j) -> p m h j", h=1).broadcast_to([P, MT, heads, HALF])
                          for i in range(2)]
                pool.tensor_tensor(t[0], x1, cs, ALU.mult).then_inc(pool_step, 1)
                pool.tensor_tensor(t[1], x2, sn, ALU.mult).then_inc(pool_step, 1)
                pool.tensor_tensor(t[2], x2, cs, ALU.mult).then_inc(pool_step, 1)
                pool.tensor_tensor(t[3], x1, sn, ALU.mult).then_inc(pool_step, 1)
                step.n += 4
                pool.wait_ge(pool_step, step.n)
                return t

            pool.wait_ge(raw_act, 4)
            pool.wait_ge(raw_dve, 4)
            for col in (0, 2 * P):
                k = kva[:, :, col:col + P].rearrange("p m (g d) -> p m g d", g=G)
                t = rotate(k, k, G)
                step(pool.tensor_tensor(k[..., 0:HALF], t[0], t[1], ALU.subtract))
                step(pool.tensor_tensor(k[..., HALF:2 * HALF], t[2], t[3], ALU.add))
            for m in range(MT):
                step(pool.tensor_copy(q_view[:, m], q_raw[:, m, :].rearrange("p (g k d) -> p g k d", g=G, k=PAIRS)))
            q_heads = q_raw[:, :, :].rearrange("p m (h d) -> p m h d", h=G * R)
            t = rotate(q_heads, None, G * R)
            for m in range(MT):
                tv = [t_[:, m].rearrange("p (g k) j -> p g k j", g=G) for t_ in t]
                step(pool.tensor_tensor(q_view[:, m][..., 0:HALF], tv[0], tv[1], ALU.subtract))
                step(pool.tensor_tensor(q_view[:, m][..., HALF:2 * HALF], tv[2], tv[3], ALU.add))
            pool.wait_ge(raw_act, 6)
            pool.wait_ge(raw_dve, 6)
            k = kvb[:, :, 0:P].rearrange("p m (g d) -> p m g d", g=G)
            t = rotate(k, k, G)
            step(pool.tensor_tensor(k[..., 0:HALF], t[0], t[1], ALU.subtract))
            pool.tensor_tensor(k[..., HALF:2 * HALF], t[2], t[3], ALU.add).then_inc(roped, 1)
            for br, v in ((0, kva[:, :, 3 * P:4 * P]), (1, kvb[:, :, P:2 * P])):
                step(pool.tensor_copy(v_t(ath, br), v))
                pool.tensor_tensor(v_t(atl, br), v, v_t(ath, br).bitcast(fp32), ALU.subtract).then_inc(roped, 1)
            pool.wait_ge(pe_ok, 1)
            pool.wait_ge(tr_done, 8)
            for c, tok in ((0, tok_k), (1, tok_v)):
                step(pool.memset(flat[:, c, :, :, NCB:NB], 0.0))
                pool.wait_ge(tok, 4)
                for g in range(G):
                    src = tok2[:, c, g, :].rearrange("p (n j) -> p j n", j=8)
                    for jh in range(2):
                        step(pool.tensor_tensor(
                            flat[:, c, 8 * jh:8 * jh + 8, g, 0:NCB], src[:, :, jh:jh + NCB],
                            pe_t[:, c, 8 * jh:8 * jh + 8].rearrange("p (j n) -> p j n", n=1).broadcast_to([P, 8, NCB]),
                            ALU.add))
                src = flat[:, c].rearrange("p j g n -> p (j g n)")
                step(pool.tensor_copy(flath[:, c, :], src))
                pool.tensor_tensor(flatl[:, c, :], src, flath[:, c, :].bitcast(fp32),
                                   ALU.subtract).then_inc(flat_ok, 1)

        @block.scalar
        def _(act):
            def split(u, slot, n=2048):
                act.wait_ge(w_arrived[slot], (16 * (u - slot) + 32) if not isinstance(u, int) else 32 * (u // 2 + 1))
                if not isinstance(u, int) or u >= 2:
                    act.wait_ge(w_used, u - 1)
                act.copy(wh[:, slot, 0:n], stage[:, slot, 0:n]).then_inc(w_hi, 1)

            def hi(dst, src):
                return act.copy(dst, src)

            for k in range(KD):
                act.wait_ge(xt_done, k + 1)
                hi(xh[:, k, :], ps[:, 4 + k % 2, :]).then_inc(xt_hi, 1)
                if k == 1:
                    split(0, 0)
                if k == 3:
                    split(1, 1)

            def chunk(u, c, dst, n, n_next=2048):
                split(u + 2, 0, n_next)
                for m in (0, 2):
                    act.wait_ge(rows_done, 3 * c + m + 1)
                    act.copy(dst[:, m, :], ps[:, m, 0:n]).then_inc(raw_act, 1)
                split(u + 3, 1, n_next)

            chunk(U_Q, 0, q_raw, 512)
            act.wait_ge(ang_ready, 1)
            act.activation(trig[:, :, :, :], ang[:, :, :, :], ACT.Sin).then_inc(trig_ready, 1)
            chunk(U_KVA, 1, kva, 512, 4 * N_KVB)
            chunk(U_KVB, 2, kvb, N_KVB)
            with act.Fori(0, 2) as c:
                u = 2 * c + U_V
                split(u + 2, 0)
                for m in (0, 2):
                    act.wait_ge(rows_done, 3 * c + 9 + m + 1)
                    act.copy(raw[:, ds(2 * c + 2, 1), m, :], ps[:, m:m + 1, :]).then_inc(raw_act, 1)
                split(u + 3, 1)

            act.wait_ge(pe_tr, 1)
            act.copy(pe_t[:, :, :], ps[:, 0, 0:32].rearrange("p (c j) -> p c j", c=2)).then_inc(pe_ok, 1)
            act.wait_ge(tr_done, 1)
            for g in range(G):
                for par in range(2):
                    act.copy(tok2[DH * par:DH * par + DH, 0, g, :],
                             ps[DH * g:DH * g + DH, 4, par:SEQ:2]).then_inc(tok_k, 1)
            for t in range(2, 8):
                act.wait_ge(tr_done, t + 1)
                if t < 4:
                    hi(k_t(ath, t - 2), ps[:, 4 + t % 4, :]).then_inc(op_hi, 1)
                else:
                    act.mul(q_t(ath)[:, t - 4, :], ps[:, 4 + t % 4, :], SCALE).then_inc(op_hi, 1)
            act.wait_ge(small_arrived, 160)
            hi(w2h[:, :, :], w2[:, :, :]).then_inc(w2_hi, 1)
            act.wait_ge(raw_dve, 6)
            act.wait_ge(raw_act, 6)
            act.activation(gates[:, :, :, :, :].rearrange("p m g r b -> p m (g r b)"),
                           kvb[:, :, 2 * P:2 * P + GATE_W], ACT.Sigmoid).then_inc(gates_ok, 1)
            act.wait_ge(raw_dve, 10)
            act.wait_ge(raw_act, 10)
            act.activation(v_raw, v_raw, ACT.Gelu_apprx_tanh).then_inc(gelu_ok, 1)
            act.activation(u_raw, u_raw, ACT.Gelu_apprx_tanh).then_inc(gelu_ok, 1)
            split(U_CV, 0)

            def take_merge(f, u, second):
                if second:
                    act.wait_ge(w_used, u + 1)
                else:
                    act.wait_ge(merge_half, f // 2 + 1)
                act.copy(merge[:, f, :], ps[:, M0 + f % 2, :]).then_inc(merge_out, 1)

            act.wait_ge(vsq_in, 1)
            act.activation(vrs[:, 1, :], vrs[:, 0, :], ACT.Sqrt).then_inc(vsq_ok, 1)
            take_merge(0, U_MERGE0, False)
            take_merge(1, U_MERGE0, True)
            split(U_MERGE, 1)
            for c in range(2):
                act.wait_ge(w_used, U_CK + c + 1)
                act.activation(hid[:, c, :], ps[:, 4 + c, 0:G * NB], ACT.Silu).then_inc(hid_ok, 1)
                act.wait_ge(hid_ok, c + 1)
                hi(hidh[:, c, :], hid[:, c, :]).then_inc(hid_hi, 1)
            split(U_MERGE + 1, 0)
            act.wait_ge(vln_ok, MT)
            act.wait_ge(w_used, U_CV + 1)
            hi(oth[:, :, :], v_raw).then_inc(vh_ok, 1)
            take_merge(2, U_MERGE, False)
            take_merge(3, U_MERGE, True)
            split(U_MERGE + 2, 1)
            act.wait_ge(cmp_done, 1)
            for g in range(G):
                hi(kch[DH * g:DH * g + DH, :], ps[DH * g:DH * g + DH, 2, NB * g:NB * g + NB]).then_inc(cmp_hi, 1)
            act.wait_ge(cmp_done, 2)
            hi(vch[:, :], ps[0:NB, 3, 0:P]).then_inc(cmp_hi, 1)
            act.wait_ge(wt_done, 1)
            hi(wth[:, :, :].rearrange("p g t -> p (g t)"), ps[:, 4, :]).then_inc(wt_hi, 1)
            act.wait_ge(sc_max, 1)
            act.activation(pc_flat, pc_flat, ACT.Exp).then_inc(sc_exp, 1)

            def take_o(w):
                qt, pp, _ = STEPS[3 * w]
                act.wait_ge(pv_done, 3 * w + 3)
                for g in range(G):
                    hi(oth[DH * g:DH * g + DH, pp, P * qt:P * qt + P],
                       ps[DH * g:DH * g + DH, O0 + w % 2, P * g:P * g + P]).then_inc(o_hi, 1)

            f_out = 0
            act.wait_ge(mix_done, 4)
            for i in range(N_STEPS + 3):
                if 2 <= i < N_STEPS + 2:
                    a = i - 2
                    n = G * P * (STEPS[a][0] + 1) if STEPS[a][2] < 2 else G * P
                    rows = P if STEPS[a][2] < 2 else NB
                    act.wait_ge(pt_done, a + 1)
                    if a >= 1:
                        act.wait_ge(pv_done, a)
                    hi(pth[0:rows, 0:n], ps[0:rows, PT0:PT0 + 2, :].rearrange("p b c -> p (b c)")[:, 0:n]).then_inc(pt_hi, 1)
                if i < N_STEPS and STEPS[i][2] < 2:
                    a = SOFT[i]
                    act.wait_ge(s_max, a + 1)
                    if a >= 2:
                        act.wait_ge(pt_done, [j for j in range(N_STEPS) if STEPS[j][2] < 2][a - 2] + 1)
                    n = P * (STEPS[i][0] + 1)
                    for g in range(G):
                        act.activation(prob[:, a % 2, g, 0:n], ps[:, g, 0:n], ACT.Exp, bias=nmax[:, a % 2, g:g + 1],
                                       accum_out=rsum[:, a % 2, g:g + 1]).then_inc(s_exp, 1)
                if i >= 3 and (i - 3) % 3 == 2:
                    take_o((i - 3) // 3)
                while i < N_STEPS + 2 and f_out < fills_done(i):
                    u = U_FILL0 + f_out // 2
                    take_merge(4 + f_out, u, f_out % 2 == 1)
                    if f_out % 2 == 1:
                        split(u + 2, u % 2)
                    f_out += 1

            for k in range(4):
                act.wait_ge(st_done, k + 1)
                hi(sgh[:, k, :], ps[:, 4 + k, :]).then_inc(st_hi, 1)
            act.wait_ge(merge_out, 16)
            for f in (0, 8, 4, 12):
                act.activation(merge[:, f:f + 4, :], merge[:, f:f + 4, :], ACT.Sigmoid).then_inc(sig_ok, 1)
            with act.Fori(0, 2) as c:
                split(2 * c + U_BRANCH + 2, 0)
                for f in range(4):
                    act.wait_ge(mg_ok, 4 * c + f + 1)
                    act.copy(xh[:, ds(4 * c + f, 1), :], merge[:, ds(4 * c + f, 1), :]).then_inc(mg_hi, 1)
                split(2 * c + U_BRANCH + 3, 1)
            with act.Fori(0, 2) as c:
                split(2 * c + U_OUT + 2, 0)
                split(2 * c + U_OUT + 3, 1)

            def root(k):
                act.wait_ge(var_ok, k + 1)
                act.activation(nrm[:, 1:2], nrm[:, 0:1], ACT.Sqrt).then_inc(sq_ok, 1)

            for m in range(MT):
                root(m)
                act.wait_ge(ht_done, m + 1)
                hi(hth[:, :, P * m:P * m + P],
                   ps[:, 4 + 2 * (m % 2):6 + 2 * (m % 2), :].rearrange("p b (k t) -> p (b k) t", k=4)).then_inc(ht_hi, 1)

            with act.Fori(0, FT // 2) as i:
                u = 2 * i + U_FFN
                for f in range(2):
                    if f == 0:
                        act.wait_ge(ffn_half, 2 * i + 1)
                    else:
                        act.wait_ge(w_used, u + 1)
                    act.activation(hid_sg[:, f, :], ps[:, f, :], ACT.Silu).then_inc(silu_ok, 1)
                split(u + 2, 0)
                split(u + 3, 1)
                act.wait_ge(fact_ok, 2 * i + 2)

            def tiles_hi(j, slot, wait=True):
                if wait:
                    act.wait_ge(w_used, U_DOWN + j - 1)
                act.copy(ah[:, slot, :, :], fact[:, ds(2 * j, 2), :]).then_inc(a_hi, 1)

            tiles_hi(0, 0, False)
            tiles_hi(1, 1, False)
            with act.Fori(0, (N_DOWN - 3) // 2) as i:
                for b in range(2):
                    split(2 * i + U_DOWN + b + 2, b)
                    tiles_hi(2 * i + b + 2, b)
            split(U_DOWN + N_DOWN - 1, 0)
            tiles_hi(N_DOWN - 1, 0)
            for m in range(MT):
                root(MT + m)

        @block.vector
        def _(dve):
            step = Steps(dve, dve_step)

            def split(u, slot, n=2048):
                dve.wait_ge(w_hi, u + 1)
                dve.tensor_tensor(wl[:, slot, 0:n], stage[:, slot, 0:n], wh[:, slot, 0:n].bitcast(fp32),
                                  ALU.subtract).then_inc(w_lo, 1)

            def lo(dst, src, h):
                return dve.tensor_tensor(dst, src, h.bitcast(fp32), ALU.subtract)

            for k in range(KD):
                dve.wait_ge(xt_hi, k + 1)
                lo(xl[:, k, :], ps[:, 4 + k % 2, :], xh[:, k, :]).then_inc(xt_lo, 1)
                if k == 1:
                    split(0, 0)
                if k == 3:
                    split(1, 1)

            def chunk(u, c, dst, n, n_next=2048):
                split(u + 2, 0, n_next)
                dve.wait_ge(rows_done, 3 * c + 2)
                dve.tensor_copy(dst[:, 1, :], ps[:, 1, 0:n]).then_inc(raw_dve, 1)
                dve.wait_ge(w_used, u + 2)
                dve.tensor_copy(dst[:, 3, :], ps[:, 3, 0:n]).then_inc(raw_dve, 1)
                split(u + 3, 1, n_next)

            chunk(U_Q, 0, q_raw, 512)
            chunk(U_KVA, 1, kva, 512, 4 * N_KVB)
            chunk(U_KVB, 2, kvb, N_KVB)
            with dve.Fori(0, 2) as c:
                u = 2 * c + U_V
                split(u + 2, 0)
                dve.wait_ge(rows_done, 3 * c + 11)
                dve.tensor_copy(raw[:, ds(2 * c + 2, 1), 1, :], ps[:, 1:2, :]).then_inc(raw_dve, 1)
                dve.wait_ge(w_used, u + 2)
                dve.tensor_copy(raw[:, ds(2 * c + 2, 1), 3, :], ps[:, 3:4, :]).then_inc(raw_dve, 1)
                split(u + 3, 1)

            dve.wait_ge(tr_done, 2)
            for g in range(G):
                for par in range(2):
                    dve.tensor_copy(tok2[DH * par:DH * par + DH, 1, g, :],
                                    ps[DH * g:DH * g + DH, 5, par:SEQ:2]).then_inc(tok_v, 1)
            for t in range(2, 8):
                dve.wait_ge(op_hi, t - 1)
                if t < 4:
                    lo(k_t(atl, t - 2), ps[:, 4 + t % 4, :], k_t(ath, t - 2)).then_inc(op_lo, 1)
                else:
                    dve.scalar_tensor_tensor(out=q_t(atl)[:, t - 4, :], in0=ps[:, 4 + t % 4, :], scalar=SCALE,
                                             in1=q_t(ath)[:, t - 4, :].bitcast(fp32), op0=ALU.mult,
                                             op1=ALU.subtract).then_inc(op_lo, 1)
            dve.wait_ge(w2_hi, 1)
            lo(w2l[:, :, :], w2[:, :, :], w2h[:, :, :]).then_inc(w2_lo, 1)
            dve.wait_ge(gelu_ok, 1)
            for m in range(MT):
                step(dve.bn_stats(vstat[:, m, :], v_raw[:, m, :]))
                step(dve.bn_aggr(vmv[:, m, :], vstat[:, m, :]))
            dve.tensor_scalar(vrs[:, 0, :], vmv[:, :, 1], EPS, None, ALU.add).then_inc(vsq_in, 1)
            split(U_CV, 0)
            dve.wait_ge(vsq_ok, 1)
            step(dve.reciprocal(vrs[:, 2, :], vrs[:, 1, :]))
            step(dve.tensor_tensor(vrs[:, 3, :], vrs[:, 2, :], vrs[:, 2, :], ALU.mult))
            step(dve.tensor_tensor(vrs[:, 3, :], vrs[:, 3, :], vrs[:, 0, :], ALU.mult))
            step(dve.tensor_scalar(vrs[:, 3, :], vrs[:, 3, :], -0.5, 1.5, ALU.mult, ALU.add))
            step(dve.tensor_tensor(vrs[:, 3, :], vrs[:, 3, :], vrs[:, 2, :], ALU.mult))
            for m in range(MT):
                step(dve.scalar_tensor_tensor(out=v_raw[:, m, :], in0=v_raw[:, m, :], scalar=vmv[:, m, 0:1],
                                              in1=ln_g[:, :], op0=ALU.subtract, op1=ALU.mult))
                dve.scalar_tensor_tensor(out=v_raw[:, m, :], in0=v_raw[:, m, :], scalar=vrs[:, 3, m:m + 1],
                                         in1=ln_b[:, :], op0=ALU.mult, op1=ALU.add).then_inc(vln_ok, 1)
            split(U_MERGE, 1)
            for c in range(2):
                dve.wait_ge(hid_hi, c + 1)
                lo(hidl[:, c, :], hid[:, c, :], hidh[:, c, :]).then_inc(hid_lo, 1)
            split(U_MERGE + 1, 0)
            dve.wait_ge(vh_ok, 1)
            lo(otl[:, :, :], v_raw, oth[:, :, :]).then_inc(vl_ok, 1)
            split(U_MERGE + 2, 1)
            for g in range(G):
                dve.wait_ge(cmp_hi, g + 1)
                lo(kcl[DH * g:DH * g + DH, :], ps[DH * g:DH * g + DH, 2, NB * g:NB * g + NB],
                   kch[DH * g:DH * g + DH, :]).then_inc(cmp_lo, 1)
            dve.wait_ge(cmp_hi, 3)
            lo(vcl[:, :], ps[0:NB, 3, 0:P], vch[:, :]).then_inc(cmp_lo, 1)
            dve.wait_ge(wt_hi, 1)
            lo(wtl[:, :, :].rearrange("p g t -> p (g t)"), ps[:, 4, :],
               wth[:, :, :].rearrange("p g t -> p (g t)")).then_inc(wt_lo, 1)

            dve.wait_ge(masks_ready, 4)
            for g in range(G):
                dve.wait_ge(sc_done, g + 1)
                step(dve.tensor_tensor(pcmp[:, g], ps[:, g, :].rearrange("p (m k n) -> p m k n", m=MT, k=PAIRS),
                                       cbias[:, :, :].rearrange("p m (k n) -> p m k n", k=1).broadcast_to(
                                           [P, MT, PAIRS, NB]), ALU.add))
            rows = pc_flat.rearrange("p (r n) -> p r n", n=NB)

            def per_row(v):
                return v.rearrange("p (r n) -> p r n", n=1).broadcast_to([P, G * MT * PAIRS, NB])

            step(dve.tensor_reduce(cmax, rows, AX.X, ALU.max))
            dve.tensor_tensor(rows, rows, per_row(cmax), ALU.subtract).then_inc(sc_max, 1)
            dve.wait_ge(gelu_ok, 2)
            for gs in range(4):
                dve.wait_ge(mix_done, gs + 1)
                uv = u_raw[:, :, P * gs:P * gs + P]
                dve.scalar_tensor_tensor(out=uv, in0=ps[:, 2 + gs, :].rearrange("p (n c) -> p n c", n=MT),
                                         scalar=bsp[:, gs:gs + 1], in1=uv, op0=ALU.add,
                                         op1=ALU.mult).then_inc(sgu_ok, 1)
            dve.wait_ge(sc_exp, 1)
            step(dve.tensor_reduce(csum_f, rows, AX.X, ALU.add))
            step(dve.reciprocal(csum_f, csum_f))
            dve.wait_ge(gates_ok, 1)
            for g in range(G):
                step(dve.tensor_tensor(csum[:, g], csum[:, g], gates[:, :, g, :, 0], ALU.mult))
                step(dve.tensor_tensor(pcmp[:, g], pcmp[:, g], cmask[:, :, :].rearrange(
                    "p m (k n) -> p m k n", k=1).broadcast_to([P, MT, PAIRS, NB]), ALU.mult))
            dve.tensor_tensor(rows, rows, per_row(csum_f), ALU.mult).then_inc(pcmp_ok, 1)

            f_out = 0
            for i in range(N_STEPS + 3):
                if 2 <= i < N_STEPS + 2:
                    a = i - 2
                    n = G * P * (STEPS[a][0] + 1) if STEPS[a][2] < 2 else G * P
                    rws = P if STEPS[a][2] < 2 else NB
                    dve.wait_ge(pt_hi, a + 1)
                    lo(ptl[0:rws, 0:n], ps[0:rws, PT0:PT0 + 2, :].rearrange("p b c -> p (b c)")[:, 0:n],
                       pth[0:rws, 0:n]).then_inc(pt_lo, 1)
                if i < N_STEPS and STEPS[i][2] < 2:
                    a = SOFT[i]
                    qt, pp, br = STEPS[i]
                    n = P * (qt + 1)
                    dve.wait_ge(s_done, a + 1)
                    diag = ps[:, 0:G, n - P:n]
                    step(dve.tensor_tensor(diag, diag, causal[:, :].rearrange(
                        "p (g n) -> p g n", g=1).broadcast_to([P, G, P]), ALU.add))
                    dve.tensor_reduce(nmax[:, a % 2, :], ps[:, 0:G, 0:n], AX.X, ALU.max, negate=True).then_inc(s_max, 1)
                    dve.wait_ge(s_exp, 2 * a + 2)
                    step(dve.reciprocal(rinv[:, a % 2, :], rsum[:, a % 2, :]))
                    step(dve.tensor_tensor(rinv[:, a % 2, :], rinv[:, a % 2, :], gates[:, qt, :, pp, 1 + br], ALU.mult))
                    for g in range(G):
                        dve.tensor_scalar(prob[:, a % 2, g, 0:n], prob[:, a % 2, g, 0:n], rinv[:, a % 2, g:g + 1],
                                          None, ALU.mult).then_inc(p_ok, 1)
                if i >= 3 and (i - 3) % 3 == 2:
                    w = (i - 3) // 3
                    qt, pp, _ = STEPS[3 * w]
                    dve.wait_ge(o_hi, 2 * w + 2)
                    for g in range(G):
                        o = lo(otl[DH * g:DH * g + DH, pp, P * qt:P * qt + P],
                               ps[DH * g:DH * g + DH, O0 + w % 2, P * g:P * g + P],
                               oth[DH * g:DH * g + DH, pp, P * qt:P * qt + P])
                        if g == G - 1:
                            o.then_inc(o_lo, 1)
                while i < N_STEPS + 2 and f_out < fills_done(i):
                    if f_out % 2 == 1:
                        u = U_FILL0 + f_out // 2
                        split(u + 2, u % 2)
                    f_out += 1

            for k in range(4):
                dve.wait_ge(st_hi, k + 1)
                lo(sgl[:, k, :], ps[:, 4 + k, :], sgh[:, k, :]).then_inc(st_lo, 1)

            with dve.Fori(0, 2) as c:
                dve.wait_ge(sig_ok, 2 * c + 2)
                for f in range(4):
                    if f < 3:
                        dve.wait_ge(br_done, 6 * c + f + 1)
                    else:
                        dve.wait_ge(w_used, 2 * c + U_BRANCH + 1)
                    gt = merge[:, ds(4 * c + f, 1), :]
                    dve.tensor_tensor(gt, gt, ps[:, f:f + 1, :], ALU.mult).then_inc(br_prod, 1)
                split(2 * c + U_BRANCH + 2, 0)
                for f in range(4):
                    if f < 3:
                        dve.wait_ge(br_done, 6 * c + 3 + f + 1)
                    else:
                        dve.wait_ge(w_used, 2 * c + U_BRANCH + 2)
                    gn, gt = merge[:, ds(4 * c + f, 1), :], merge[:, ds(4 * c + f + 8, 1), :]
                    dve.tensor_tensor(gt, gt, ps[:, 4 + f:5 + f, :], ALU.mult).then_inc(br_prod, 1)
                    dve.wait_ge(br_prod, 8 * c + 4 + f + 1)
                    dve.tensor_tensor(gn, gn, gt, ALU.add).then_inc(mg_ok, 1)
                    dve.wait_ge(mg_hi, 4 * c + f + 1)
                    dve.tensor_tensor(xl[:, ds(4 * c + f, 1), :], gn, xh[:, ds(4 * c + f, 1), :].bitcast(fp32),
                                      ALU.subtract).then_inc(mg_lo, 1)
                split(2 * c + U_BRANCH + 3, 1)

            dve.wait_ge(x2_arrived, 16)
            with dve.Fori(0, 2) as c:
                split(2 * c + U_OUT + 2, 0)
                for m in range(MT):
                    if m < 3:
                        dve.wait_ge(rows_done, 3 * c + 15 + m + 1)
                    else:
                        dve.wait_ge(w_used, 2 * c + U_OUT + 2)
                    ym = y[:, m:m + 1, ds(512 * c, 512)]
                    dve.scalar_tensor_tensor(out=ym, in0=ym, scalar=ALPHA, in1=ps[:, m:m + 1, :], op0=ALU.mult,
                                             op1=ALU.add).then_inc(mg_lo, 1)
                split(2 * c + U_OUT + 3, 1)

            def norm(k, m):
                ln = k // MT
                for s in range(2):
                    step(dve.bn_stats(stat[:, s, :], y[:, m, 512 * s:512 * s + 512]))
                step(dve.bn_aggr(mv[:, :], stat[:, :, :].rearrange("p a b -> p (a b)")))
                dve.tensor_scalar(nrm[:, 0:1], mv[:, 1:2], EPS, None, ALU.add).then_inc(var_ok, 1)
                dve.wait_ge(sq_ok, k + 1)
                step(dve.reciprocal(nrm[:, 2:3], nrm[:, 1:2]))
                step(dve.scalar_tensor_tensor(out=nrm[:, 3:4], in0=nrm[:, 2:3], scalar=nrm[:, 0:1], in1=nrm[:, 2:3],
                                              op0=ALU.mult, op1=ALU.mult))
                step(dve.tensor_scalar(nrm[:, 3:4], nrm[:, 3:4], -0.5, 1.5, ALU.mult, ALU.add))
                step(dve.tensor_tensor(nrm[:, 3:4], nrm[:, 3:4], nrm[:, 2:3], ALU.mult))
                step(dve.scalar_tensor_tensor(out=y[:, m, :], in0=y[:, m, :], scalar=mv[:, 0:1], in1=lng[:, ln, :],
                                              op0=ALU.subtract, op1=ALU.mult))
                dve.scalar_tensor_tensor(out=y[:, m, :], in0=y[:, m, :], scalar=nrm[:, 3:4], in1=lnb[:, ln, :],
                                         op0=ALU.mult, op1=ALU.add).then_inc(h_ok, 1)

            dve.wait_ge(ln_arrived, 64)
            dve.wait_ge(mg_lo, KD + 2 * MT)
            for m in range(MT):
                norm(m, m)
                if m:
                    dve.wait_ge(ht_hi, m)
                    lo(htl[:, :, P * (m - 1):P * m],
                       ps[:, 4 + 2 * ((m - 1) % 2):6 + 2 * ((m - 1) % 2), :].rearrange("p b (k t) -> p (b k) t", k=4),
                       hth[:, :, P * (m - 1):P * m]).then_inc(ht_lo, 1)
            dve.wait_ge(ht_hi, MT)
            lo(htl[:, :, P * 3:P * 4], ps[:, 6:8, :].rearrange("p b (k t) -> p (b k) t", k=4),
               hth[:, :, P * 3:P * 4]).then_inc(ht_lo, 1)

            with dve.Fori(0, FT // 2) as i:
                u = 2 * i + U_FFN
                split(u + 2, 0)
                for f in range(2):
                    dve.wait_ge(silu_ok, 2 * i + f + 1)
                    if f == 0:
                        dve.wait_ge(ffn_half, 2 * i + 2)
                    else:
                        dve.wait_ge(w_used, u + 2)
                    dve.tensor_tensor(fact[:, ds(2 * i + f, 1), :], hid_sg[:, f:f + 1, :], ps[:, 2 + f:3 + f, :],
                                      ALU.mult).then_inc(fact_ok, 1)
                split(u + 3, 1)

            def tiles_lo(j, slot):
                dve.wait_ge(a_hi, j + 1)
                dve.tensor_tensor(al[:, slot, :, :], fact[:, ds(2 * j, 2), :], ah[:, slot, :, :].bitcast(fp32),
                                  ALU.subtract).then_inc(a_lo, 1)

            tiles_lo(0, 0)
            tiles_lo(1, 1)
            with dve.Fori(0, (N_DOWN - 3) // 2) as i:
                for b in range(2):
                    split(2 * i + U_DOWN + b + 2, b)
                    tiles_lo(2 * i + b + 2, b)
            split(U_DOWN + N_DOWN - 1, 0)
            tiles_lo(N_DOWN - 1, 0)
            for m in range(MT):
                if m < 3:
                    dve.wait_ge(rows_out, m + 1)
                else:
                    dve.wait_ge(w_used, U_DOWN + N_DOWN)
                step(dve.scalar_tensor_tensor(out=y[:, m, :], in0=y[:, m, :], scalar=ALPHA,
                                              in1=ps[:, 2 * m:2 * m + 2, :].rearrange("p b c -> p (b c)"),
                                              op0=ALU.mult, op1=ALU.add))
                norm(MT + m, m)

        @block.tensor
        def _(pe):
            def mm3(out, sh, sl, mh, ml, start, stop):
                pe.matmul(out, sh, mh, start=start, stop=False)
                pe.matmul(out, sh, ml, start=False, stop=False)
                return pe.matmul(out, sl, mh, start=False, stop=stop)

            def transpose(out, in_, k=P):
                return pe.transpose(out, in_, ident[0:k, 0:k])

            def x_tile(k):
                pe.wait_ge(x_arrived[k // 4], 16)
                if k >= 2:
                    pe.wait_ge(xt_lo, k - 1)
                for m in range(MT):
                    last = transpose(ps[:, 4 + k % 2, P * m:P * m + P], x_sb[:, m, P * k:P * k + P])
                last.then_inc(xt_done, 1)

            pe.wait_ge(masks_ready, 1)
            for k in range(4):
                x_tile(k)

            def tokens(u, lh, ll, n, before):
                for kh in range(2):
                    pe.wait_ge(w_lo, u + kh + 1)
                    before(kh, None)
                    for m in range(MT):
                        before(kh, m)
                        for k in range(4):
                            kk = 4 * kh + k
                            tok = slice(P * m, P * m + P)
                            last = mm3(ps[:, m, 0:n], lh[:, kk, tok], ll[:, kk, tok], w4(wh, kh, n)[:, k, :],
                                       w4(wl, kh, n)[:, k, :], kk == 0, kk == KD - 1)
                        if kh == 1 and m < MT - 1:
                            last.then_inc(rows_done, 1)
                    last.then_inc(w_used, 1)

            def bank_free(c):
                def before(kh, m):
                    if kh == 0 and m is not None:
                        pe.wait_ge(raw_dve if m % 2 else raw_act, 2 * (c - 1) + m // 2 + 1)
                return before

            def first_chunk(kh, m):
                if m is None and kh == 0:
                    pe.wait_ge(xt_lo, 4)
                if m is None and kh == 1:
                    for k in range(4, KD):
                        x_tile(k)
                    pe.wait_ge(xt_lo, KD)

            tokens(U_Q, xh, xl, 512, first_chunk)
            tokens(U_KVA, xh, xl, 512, bank_free(1))
            tokens(U_KVB, xh, xl, N_KVB, bank_free(2))
            with pe.Fori(0, 2) as c:
                tokens(2 * c + U_V, xh, xl, SG, bank_free(c + 3))

            pe.wait_ge(small_arrived, 160)
            pe.wait_ge(raw_act, 9)
            for c in range(2):
                last = transpose(ps[:, 0, 16 * c:16 * c + 16], pe_in[:, c, :], 16)
            last.then_inc(pe_tr, 1)
            pe.wait_ge(roped, 1)
            for t in range(8):
                if t == 4:
                    pe.wait_ge(tok_k, 4)
                if t == 5:
                    pe.wait_ge(tok_v, 4)
                if t >= 6:
                    pe.wait_ge(op_lo, t - 5)
                for m in range(MT):
                    src = (kva[:, m, P * t:P * t + P] if t < 3 else
                           kvb[:, m, 0:P] if t == 3 else q_perm[:, m, P * (t - 4):P * (t - 4) + P])
                    last = transpose(ps[:, 4 + t % 4, P * m:P * m + P], src)
                last.then_inc(tr_done, 1)

            def merge_piece(u, piece, f):
                half, k = piece // KD, piece % KD
                if piece == 0:
                    pe.wait_ge(w_lo, u + 1)
                if k == 0 and f >= 2:
                    pe.wait_ge(merge_out, f - 1)
                col = slice(P * half, P * half + P)
                last = mm3(ps[:, M0 + half, :], w8(wh, u % 2)[:, k, col], w8(wl, u % 2)[:, k, col],
                           xh[:, k, :], xl[:, k, :], k == 0, k == KD - 1)
                if k == KD - 1:
                    last.then_inc(w_used if half else merge_half, 1)

            pe.wait_ge(op_lo, 6)
            for piece in range(2 * KD):
                merge_piece(U_MERGE0, piece, piece // KD)

            for c, u in enumerate((U_CK, U_CV)):
                pe.wait_ge(w_lo, u + 1)
                pe.wait_ge(flat_ok, c + 1)
                for j in range(16):
                    cols = slice(G * NB * j, G * NB * (j + 1))
                    last = mm3(ps[:, 4 + c, 0:G * NB], w16(wh, u % 2)[:, j, :], w16(wl, u % 2)[:, j, :],
                               flath[:, c, cols], flatl[:, c, cols], j == 0, j == 15)
                last.then_inc(w_used, 1)
            for piece in range(2 * KD):
                merge_piece(U_MERGE, piece, 2 + piece // KD)

            pe.wait_ge(w2_lo, 1)
            pe.wait_ge(hid_lo, 1)
            dup = slice(0, 2 * DH)
            k2h, k2l = [t[:, :, :].rearrange("p a b -> p (a b)")[:, dup] for t in (w2h, w2l)]
            mm3(ps[:, 2, 0:G * NB], k2h, k2l, hidh[:, 0, :], hidl[:, 0, :], True, True).then_inc(cmp_done, 1)
            pe.wait_ge(hid_lo, 2)
            for g in range(G):
                n = slice(NB * g, NB * g + NB)
                last = mm3(ps[0:NB, 3, DH * g:DH * g + DH], hidh[:, 1, n], hidl[:, 1, n], w2h[:, 2, :], w2l[:, 2, :],
                           True, True)
            last.then_inc(cmp_done, 1)
            pe.wait_ge(masks_ready, 4)
            pe.wait_ge(hid_ok, 1)
            for gs in range(4):
                last = transpose(ps[:, 4, P * gs:P * gs + P], wsp[:, gs, :])
            last.then_inc(wt_done, 1)
            pe.wait_ge(cmp_lo, 2)
            pe.wait_ge(pe_ok, 1)
            for g in range(G):
                r = slice(DH * g, DH * g + DH)
                for m in range(MT):
                    for pp in range(PAIRS):
                        at = NB * (PAIRS * m + pp)
                        tok = slice(P * m, P * m + P)
                        last = mm3(ps[:, g, at:at + NB], q_t(ath)[r, pp, tok], q_t(atl)[r, pp, tok], kch[r, :],
                                   kcl[r, :], True, True)
                last.then_inc(sc_done, 1)
            pe.wait_ge(vl_ok, 1)
            pe.wait_ge(wt_lo, 1)
            pe.wait_ge(cmp_lo, 3)
            for gs in range(4):
                cols = slice(P * gs, P * gs + P)
                mm3(ps[:, 2 + gs, :], wth[:, gs, :], wtl[:, gs, :], oth[:, :, cols], otl[:, :, cols],
                    True, True).then_inc(mix_done, 1)

            pe.wait_ge(sgu_ok, 4)
            pe.wait_ge(sc_max, 1)
            pe.wait_ge(roped, 3)
            pe.wait_ge(merge_out, 4)
            piece = 0
            soft_of = [j for j in range(N_STEPS) if STEPS[j][2] < 2]

            def fill(until):
                nonlocal piece
                while piece < until:
                    merge_piece(U_FILL0 + piece // (2 * KD), piece % (2 * KD), 4 + piece // KD)
                    piece += 1

            for i in range(N_STEPS + 2):
                if i < N_STEPS and STEPS[i][2] < 2:
                    qt, pp, br = STEPS[i]
                    a = SOFT[i]
                    if a:
                        pe.wait_ge(s_exp, 2 * a)
                    n = P * (qt + 1)
                    for g in range(G):
                        r = slice(DH * g, DH * g + DH)
                        tok = slice(P * qt, P * qt + P)
                        last = mm3(ps[:, g, 0:n], q_t(ath)[r, pp, tok], q_t(atl)[r, pp, tok], k_t(ath, br)[r, 0:n],
                                   k_t(atl, br)[r, 0:n], True, True)
                    last.then_inc(s_done, 1)
                mid = (FILL_AT[i] + FILL_AT[i + 1]) // 2
                fill(mid)
                if i >= 2:
                    a = i - 2
                    qt, pp, br = STEPS[a]
                    w = a // 3
                    pe.wait_ge(pt_lo, a + 1)
                    if br == 0 and w >= 2:
                        pe.wait_ge(o_lo, w - 1)
                    out = ps[:, O0 + w % 2, 0:G * P]
                    if br < 2:
                        for kt in range(qt + 1):
                            c = slice(G * P * kt, G * P * (kt + 1))
                            last = mm3(out, v_t(ath, br)[:, kt, :], v_t(atl, br)[:, kt, :], pth[:, c], ptl[:, c],
                                       br == 0 and kt == 0, False)
                    else:
                        last = mm3(out, vch[:, :], vcl[:, :], pth[0:NB, 0:G * P], ptl[0:NB, 0:G * P], False, True)
                    last.then_inc(pv_done, 1)
                fill(FILL_AT[i + 1])
                if 1 <= i <= N_STEPS:
                    a = i - 1
                    qt, pp, br = STEPS[a]
                    if a:
                        pe.wait_ge(pt_lo, a)
                    if br < 2:
                        s = SOFT[a]
                        pe.wait_ge(p_ok, 2 * s + 2)
                        for kt in range(qt + 1):
                            for g in range(G):
                                last = transpose(ps[:, PT0 + kt // 2, G * P * (kt % 2) + P * g:G * P * (kt % 2) + P * g + P],
                                                 prob[:, s % 2, g, P * kt:P * kt + P])
                    else:
                        if a == 2:
                            pe.wait_ge(pcmp_ok, 1)
                        for g in range(G):
                            last = transpose(ps[0:NB, PT0, P * g:P * g + P], pcmp[:, g, qt, pp, :])
                    last.then_inc(pt_done, 1)

            pe.wait_ge(o_lo, MT * PAIRS)
            pe.wait_ge(merge_out, 2 * N_MERGE)
            for k in range(4):
                for m in range(MT):
                    last = transpose(ps[:, 4 + k, P * m:P * m + P], u_raw[:, m, P * k:P * k + P])
                last.then_inc(st_done, 1)

            pe.wait_ge(st_lo, 4)
            with pe.Fori(0, 2) as c:
                for b, (oh, ol) in enumerate(((oth, otl), (sgh, sgl))):
                    pe.wait_ge(w_lo, 2 * c + U_BRANCH + b + 1)
                    if b:
                        pe.wait_ge(br_prod, 8 * c + 1)
                    for f in range(4):
                        for k in range(4):
                            col = slice(P * f, P * f + P)
                            last = mm3(ps[:, 4 * b + f, :], w4(wh, b)[:, k, col], w4(wl, b)[:, k, col], oh[:, k, :],
                                       ol[:, k, :], k == 0, k == 3)
                        if f < 3:
                            last.then_inc(br_done, 1)
                    last.then_inc(w_used, 1)
                pe.wait_ge(br_prod, 8 * c + 4)

            with pe.Fori(0, 2) as c:
                def before(kh, m):
                    if m is None:
                        pe.wait_ge(mg_lo, 4 * kh + 4)
                    elif kh == 0:
                        pe.wait_ge(mg_lo, 4 * c + 5 + m)
                tokens(2 * c + U_OUT, xh, xl, 512, before)

            for m in range(MT):
                pe.wait_ge(h_ok, m + 1)
                if m >= 2:
                    pe.wait_ge(ht_lo, m - 1)
                for k in range(KD):
                    last = transpose(ps[:, 4 + 2 * (m % 2) + k // 4, P * (k % 4):P * (k % 4) + P],
                                     y[:, m, P * k:P * k + P])
                last.then_inc(ht_done, 1)

            pe.wait_ge(ht_lo, MT)
            with pe.Fori(0, FT // 2) as i:
                for b in range(2):
                    pe.wait_ge(w_lo, 2 * i + U_FFN + b + 1)
                    for f in range(2):
                        for k in range(KD):
                            col = slice(P * f, P * f + P)
                            last = mm3(ps[:, 2 * b + f, :], w8(wh, b)[:, k, col], w8(wl, b)[:, k, col], hth[:, k, :],
                                       htl[:, k, :], k == 0, k == KD - 1)
                        if f == 0:
                            last.then_inc(ffn_half, 1)
                    last.then_inc(w_used, 1)
                pe.wait_ge(silu_ok, 2 * i + 2)

            def down(slot, m, start, stop):
                for f in range(2):
                    tok = slice(P * m, P * m + P)
                    for half in range(2):
                        c = slice(512 * half, 512 * half + 512)
                        last = mm3(ps[:, 2 * m + half, :], ah[:, slot, f, tok], al[:, slot, f, tok],
                                   w2d(wh, slot)[:, f, c], w2d(wl, slot)[:, f, c], start and f == 0, stop and f == 1)
                return last

            def down_unit(j, slot, start=False):
                pe.wait_ge(w_lo, U_DOWN + 1 + j)
                pe.wait_ge(a_lo, j + 1)
                for m in range(MT):
                    last = down(slot, m, start, False)
                last.then_inc(w_used, 1)

            pe.wait_ge(fact_ok, FT)
            down_unit(0, 0, True)
            down_unit(1, 1)
            with pe.Fori(1, (N_DOWN - 3) // 2) as i:
                for b in range(2):
                    down_unit(2 * i + b, b)
            down_unit(N_DOWN - 3, 0)
            pe.wait_ge(w_lo, U_DOWN + N_DOWN)
            pe.wait_ge(a_lo, N_DOWN)
            for m in range(MT):
                last = down(1, m, False, False)
                if m == MT - 1:
                    last.then_inc(w_used, 1)
                last = down(0, m, False, True)
                last.then_inc(rows_out if m < MT - 1 else w_used, 1)


_INS = ["x", "positions", "w_in", "pe_ck", "w_ck1", "w_ck2", "pe_cv", "w_cv1", "w_cv2", "ln_sgu_g", "ln_sgu_b",
        "w_spatial", "b_spatial", "w_branch_nsa", "w_branch_sgu", "w_out", "ln1_g", "ln1_b", "w_ffn_gate",
        "w_ffn_up", "w_ffn_down", "ln2_g", "ln2_b"]


def kernel(**inputs):
    import numpy as np
    import concourse.bacc as bacc
    from concourse import mybir
    from concourse.bass_utils import run_bass_kernel_spmd

    nc = bacc.Bacc("TRN2", target_bir_lowering=False, num_devices=1)
    arrays, tensors = {}, {}
    for name in _INS:
        a = np.ascontiguousarray(inputs[name])
        arrays[f"in_{name}"] = a
        tensors[name] = nc.dram_tensor(f"in_{name}", a.shape, mybir.dt.from_np(a.dtype), kind="ExternalInput").ap()
    tensors["out"] = nc.dram_tensor("out", inputs["x"].shape, mybir.dt.float32, kind="ExternalOutput").ap()
    build_layer(nc, tensors)
    result = run_bass_kernel_spmd(nc, [arrays], core_ids=[0])
    return result.results[0]["out"]
```

```python
def build_layer(nc, T):
    import math
    from contextlib import ExitStack

    import numpy as np

    import concourse.bass as bass
    from concourse import mybir

    fp32 = mybir.dt.float32
    f32r = mybir.dt.float32r
    i32 = mybir.dt.int32
    ALU = mybir.AluOpType
    ACT = mybir.ActivationFunctionType
    AX = mybir.AxisListType
    ds = bass.ds

    P = 128
    SEQ, D = T["x"].shape[1:]
    MT = SEQ // P
    KD = D // P
    DH = 64
    G, R = 2, 4
    PAIRS = R
    NCB = 31
    NB = 32
    STRIDE, BLOCK = 16, 32
    HID = T["w_ck2"].shape[1]
    SG = 512
    F = T["w_ffn_gate"].shape[2]
    FT = F // P
    HALF = 8
    SCALE = DH ** -0.5
    NEG = -1e30
    ALPHA = 2.0 ** 0.25
    EPS = 1e-5
    GATE_W = 3 * G * R

    C_Q, C_KVA, C_KVB = 0, 512, 1024
    N_KVB = 2 * P + GATE_W
    C_U = C_KVB + N_KVB
    C_V = C_U + SG
    C_MERGE = C_V + SG

    U_Q, U_KVA, U_KVB, U_V, U_U = 0, 2, 4, 6, 8
    U_MERGE0 = 10
    U_CK, U_CV = 11, 12
    U_MERGE = 13
    N_MERGE = 2 * D // 256
    U_BRANCH = U_MERGE + N_MERGE - 1
    U_OUT = U_BRANCH + 4
    U_FFN = U_OUT + 4
    U_DOWN = U_FFN + FT
    N_DOWN = FT // 2

    TILE_ORDER = (0, 1, 2, 3)
    FILL_SHARE = {0: 0.8, 1: 0.9, 2: 1.1, 3: 1.3, -1: 1.0}
    FILL_BRANCH = (2.3, 0.5, 3.0)
    LATE_PIECE = 9
    FILL_FIRST = 8

    BIAS_COLS = 704

    x_d = T["x"][0].rearrange("(m p) c -> p m c", p=P)
    out_d = T["out"][0].rearrange("(m p) c -> p m c", p=P)
    w_in_d = T["w_in"][0].rearrange("(k p) n -> p k n", p=P)
    ck1_d = T["w_ck1"][0].rearrange("(j p) h -> p j h", p=P)
    cv1_d = T["w_cv1"][0].rearrange("(j p) h -> p j h", p=P)
    nsa_d = T["w_branch_nsa"][0].rearrange("(g k d) n -> g d k n", g=G, k=PAIRS)
    sgu_d = T["w_branch_sgu"][0].rearrange("(k p) n -> p k n", p=P)
    wout_d = T["w_out"][0].rearrange("(k p) n -> p k n", p=P)
    gate_d = T["w_ffn_gate"][0].rearrange("(k p) n -> p k n", p=P)
    up_d = T["w_ffn_up"][0].rearrange("(k p) n -> p k n", p=P)
    down_d = T["w_ffn_down"][0].rearrange("(f p) n -> p f n", p=P)

    def as_rows(v):
        return v.rearrange("n -> () n").broadcast_to([P, v.shape[0]])

    FREQ = [float(np.float32(500000.0 ** (-j / HALF))) for j in range(HALF)]
    MAGIC = 1.5 * 2.0 ** 23
    PI_1 = 6.28125
    PI_2 = round((2 * math.pi - PI_1) * 2.0 ** 20) / 2.0 ** 20
    PI_3 = 2 * math.pi - PI_1 - PI_2
    PI_IN = 3.1415925

    with ExitStack() as ctx:
        def sb(name, shape, dt, scope=ctx):
            return scope.enter_context(nc.sbuf_tensor(name, shape, dt))

        def sem(name):
            return ctx.enter_context(nc.semaphore(name))

        stage = sb("stage", [P, 2, 2048], fp32)
        wh = sb("wh", [P, 2, 2048], f32r)
        wl = sb("wl", [P, 2, 2048], f32r)
        xh = sb("xh", [P, KD, SEQ], f32r)
        xl = sb("xl", [P, KD, SEQ], f32r)
        ath = sb("ath", [P, 4096], f32r)
        atl = sb("atl", [P, 4096], f32r)
        ident = sb("ident", [P, P], fp32)

        first = ExitStack()
        prob = sb("prob", [P, 2, G, SEQ], fp32, first)
        pcmp = sb("pcmp", [P, G, MT, PAIRS, NB], fp32, first)
        pth = sb("pth", [P, 1024], f32r, first)
        ptl = sb("ptl", [P, 1024], f32r, first)
        arena = sb("arena", [P, 10240], fp32, first)
        oth = sb("oth", [P, PAIRS, SEQ], f32r, first)
        otl = sb("otl", [P, PAIRS, SEQ], f32r, first)
        ln_g = sb("ln_g", [P, SG], fp32, first)
        ln_b = sb("ln_b", [P, SG], fp32, first)
        wsp = sb("wsp", [P, 4, P], fp32, first)
        wth = sb("wth", [P, 4, P], f32r, first)
        wtl = sb("wtl", [P, 4, P], f32r, first)
        bsp = sb("bsp", [P, 4], fp32, first)
        causal = sb("causal", [P, P], f32r, first)
        ident_r = sb("ident_r", [P, P], f32r, first)
        cbias = sb("cbias", [P, MT, NB], fp32, first)
        any_block = sb("any_block", [P, MT], fp32, first)
        pos_i = sb("pos_i", [P, MT], i32, first)
        pos_f = sb("pos_f", [P, MT], fp32, first)
        freq = sb("freq", [P, HALF], fp32, first)
        ang = sb("ang", [P, 2, MT, HALF], fp32, first)
        trig = sb("trig", [P, 2, MT, HALF], fp32, first)
        gates = sb("gates", [P, MT, G, R, 3], fp32, first)
        pe_in = sb("pe_in", [16, 2, P], fp32, first)
        pe_t = sb("pe_t", [P, 2, 16], fp32, first)
        w2 = sb("w2", [P, 3, DH], fp32, first)
        w2h = sb("w2h", [P, 3, DH], f32r, first)
        w2l = sb("w2l", [P, 3, DH], f32r, first)
        hidh = sb("hidh", [P, 2, G * NB], f32r, first)
        hidl = sb("hidl", [P, 2, G * NB], f32r, first)
        kch = sb("kch", [P, NB], f32r, first)
        kcl = sb("kcl", [P, NB], f32r, first)
        vch = sb("vch", [NB, P], f32r, first)
        vcl = sb("vcl", [NB, P], f32r, first)
        nmax = sb("nmax", [P, 2, G], fp32, first)
        rsum = sb("rsum", [P, 2, G], fp32, first)
        rinv = sb("rinv", [P, 2, G], fp32, first)
        vstat = sb("vstat", [P, MT, 6], fp32, first)
        vmv = sb("vmv", [P, MT, 2], fp32, first)
        vrs = sb("vrs", [P, 4, MT], fp32, first)
        first.close()

        second = ExitStack()
        hid_sg = sb("hid_sg", [P, 2, SEQ], fp32, second)
        y = sb("y", [P, MT, D], fp32, second)
        lng = sb("lng", [P, 2, D], fp32, second)
        lnb = sb("lnb", [P, 2, D], fp32, second)
        stat = sb("stat", [P, MT, 2, 6], fp32, second)
        mv = sb("mv", [P, MT, 2], fp32, second)
        nrm = sb("nrm", [P, MT, 5], fp32, second)
        early = ExitStack()
        sb("fact_before", [P, FT - 8, SEQ], fp32, early)
        first_h = sb("first_h", [P, 2048], f32r, early)
        first_l = sb("first_l", [P, 2048], f32r, early)
        early.close()
        fact = sb("fact", [P, FT, SEQ], fp32, second)
        second.close()

        raw = arena[:, :].rearrange("p (c m n) -> p c m n", c=5, m=MT)
        q_raw, kva, v_raw, u_raw = raw[:, 0], raw[:, 1], raw[:, 2], raw[:, 4]
        kvb = arena[:, 6144:6144 + MT * N_KVB].rearrange("p (m n) -> p m n", m=MT)
        kvb_end = 6144 + MT * N_KVB
        hid = arena[:, kvb_end:kvb_end + 2 * G * NB].rearrange("p (c e) -> p c e", c=2)
        cmax = arena[:, kvb_end + 128:kvb_end + 160]
        csum_f = arena[:, kvb_end + 160:kvb_end + 192]
        csum = csum_f.rearrange("p (g m k) -> p g m k", g=G, m=MT)
        x_sb = arena[:, 4096:8192].rearrange("p (m c) -> p m c", m=MT)
        merge = arena[:, 0:16 * SEQ].rearrange("p (f t) -> p f t", f=16)
        q_perm = prob[:, :, :, :].rearrange("p a b c -> p (a b c)").rearrange("p (m n) -> p m n", m=MT)
        q_view = q_perm.rearrange("p m (k g d) -> p m g k d", k=PAIRS, g=G)
        pc_flat = pcmp[:, :, :, :, :].rearrange("p a b c d -> p (a b c d)")
        turns, tmp_b = [pc_flat[:, P + 64 * i:P + 64 * i + 64].rearrange("p (a m j) -> p a m j", a=2, m=MT)
                        for i in range(2)]
        rope_t = pc_flat.rearrange("p (t m h j) -> p t m h j", t=4, m=MT, h=8)
        tok2 = pc_flat.rearrange("p (c g t) -> p c g t", c=2, g=G)
        flat = prob[:, :, :, :].rearrange("p a b c -> p a (b c)").rearrange(
            "p c (j g n) -> p c j g n", j=16, g=G)
        flath = oth[:, :, :].rearrange("p a b -> p (a b)").rearrange("p (c e) -> p c e", c=2)
        flatl = otl[:, :, :].rearrange("p a b -> p (a b)").rearrange("p (c e) -> p c e", c=2)

        def att(t, off, n):
            return t[:, off:off + n]

        def q_t(t):
            return att(t, 0, 2048).rearrange("p (k s) -> p k s", k=PAIRS)

        def k_t(t, br):
            return att(t, 2048 + 512 * br, 512)

        def v_t(t, br):
            return att(t, 3072 + 512 * br, 512).rearrange("p (m n) -> p m n", m=MT)

        sgh = att(ath, 0, 2048).rearrange("p (k s) -> p k s", k=4)
        sgl = att(atl, 0, 2048).rearrange("p (k s) -> p k s", k=4)
        hth = ath[:, :].rearrange("p (k s) -> p k s", k=KD)
        htl = atl[:, :].rearrange("p (k s) -> p k s", k=KD)
        late_h, late_l = ath[:, 0:2048], atl[:, 0:2048]
        ah = xh[:, :, :].rearrange("p (r f) s -> p r f s", f=2)
        al = xl[:, :, :].rearrange("p (r f) s -> p r f s", f=2)

        ps = ctx.enter_context(nc.psum_tensor("ps", [P, 8, 512], fp32))
        PT0, O0, M0 = 2, 4, 6

        def w4(t, slot, n=512):
            return t[:, slot, 0:4 * n].rearrange("p (k n) -> p k n", k=4)

        def w8(t, slot):
            return t[:, slot, :].rearrange("p (k n) -> p k n", k=8)

        def w2d(t, slot):
            return t[:, slot, :].rearrange("p (f n) -> p f n", f=2)

        def w16(t, slot):
            return t[:, slot, :].rearrange("p (j h) -> p j h", j=16)

        w_arrived = [sem("w_arrived0"), sem("w_arrived1")]
        w_hi, w_lo, w_used = sem("w_hi"), sem("w_lo"), sem("w_used")
        quarter_hi = sem("quarter_hi")
        x_arrived = [sem("x_arrived0"), sem("x_arrived1")]
        small_arrived = sem("small_arrived")
        xt_done, xt_hi, xt_lo = sem("xt_done"), sem("xt_hi"), sem("xt_lo")
        rows_done = sem("rows_done")
        raw_act, raw_dve = sem("raw_act"), sem("raw_dve")
        pool_step, act_step, dve_step = sem("pool_step"), sem("act_step"), sem("dve_step")
        masks_ready, ang_ready, trig_ready = sem("masks_ready"), sem("ang_ready"), sem("trig_ready")
        roped = sem("roped")
        tr_done = sem("tr_done")
        tok_k, tok_v = sem("tok_k"), sem("tok_v")
        op_hi, op_lo = sem("op_hi"), sem("op_lo")
        pe_tr, pe_ok = sem("pe_tr"), sem("pe_ok")
        flat_ok = sem("flat_ok")
        w2_hi, w2_lo = sem("w2_hi"), sem("w2_lo")
        hid_ok, hid_hi, hid_lo = sem("hid_ok"), sem("hid_hi"), sem("hid_lo")
        cmp_done, cmp_hi, cmp_lo = sem("cmp_done"), sem("cmp_hi"), sem("cmp_lo")
        sc_done, sc_max, sc_exp, pcmp_ok = sem("sc_done"), sem("sc_max"), sem("sc_exp"), sem("pcmp_ok")
        gates_ok = sem("gates_ok")
        gelu_ok, vsq_in, vsq_ok, vln_ok = sem("gelu_ok"), sem("vsq_in"), sem("vsq_ok"), sem("vln_ok")
        vh_ok, vl_ok = sem("vh_ok"), sem("vl_ok")
        wt_done, wt_hi, wt_lo = sem("wt_done"), sem("wt_hi"), sem("wt_lo")
        mix_done, sgu_ok = sem("mix_done"), sem("sgu_ok")
        merge_half = sem("merge_half")
        merge_out = sem("merge_out")
        s_done, s_max, s_exp, rinv_ok = sem("s_done"), sem("s_max"), sem("s_exp"), sem("rinv_ok")
        p_ok = [sem("p_ok0"), sem("p_ok1")]
        pt_done, pt_hi, pt_lo = sem("pt_done"), sem("pt_hi"), sem("pt_lo")
        pv_done, o_hi, o_lo = sem("pv_done"), sem("o_hi"), sem("o_lo")
        st_done, st_hi, st_lo = sem("st_done"), sem("st_hi"), sem("st_lo")
        sig_ok = sem("sig_ok")
        br_done, br_prod = sem("br_done"), sem("br_prod")
        mg_ok, mg_hi, mg_lo = sem("mg_ok"), sem("mg_hi"), sem("mg_lo")
        x2_arrived, ln_arrived = sem("x2_arrived"), sem("ln_arrived")
        var_ok, sq_ok, centred, scaled = sem("var_ok"), sem("sq_ok"), sem("centred"), sem("scaled")
        h_ok = [sem("h_ok0"), sem("h_ok1")]
        ht_done, ht_hi, ht_lo = sem("ht_done"), sem("ht_hi"), sem("ht_lo")
        ffn_half, silu_ok, fact_ok = sem("ffn_half"), sem("silu_ok"), sem("fact_ok")
        a_hi, a_lo = sem("a_hi"), sem("a_lo")
        rows_out = sem("rows_out")
        stored = sem("stored")

        block = ctx.enter_context(nc.Block())

        STEPS = [(qt, pp, br) for qt in TILE_ORDER for pp in range(PAIRS) for br in range(3)]
        N_STEPS = len(STEPS)
        SOFT_STEPS = [a for a in range(N_STEPS) if STEPS[a][2] < 2]
        SOFT = {a: s for s, a in enumerate(SOFT_STEPS)}
        U_FILL0, N_FILL = U_MERGE + 1, N_MERGE - 2
        PIECES = N_FILL * 2 * KD
        share = [FILL_SHARE[STEPS[i][0] if i < N_STEPS else -1] * FILL_BRANCH[i % 3] for i in range(N_STEPS + 3)]
        FILL_AT = [FILL_FIRST + round((PIECES - FILL_FIRST) * sum(share[:i]) / sum(share)) for i in range(N_STEPS + 4)]

        def fills_done(i):
            return FILL_AT[i] // KD

        QUARTERS = [[] for _ in range(N_STEPS + 3)]
        for v in range(N_FILL):
            end = next(i for i in range(N_STEPS + 3) if fills_done(i + 1) >= 2 * v + 2)
            for quarter in range(4):
                at = end - end % 3 + 2 + 3 * (quarter // 2)
                QUARTERS[min(at, N_STEPS + 2)].append((U_FILL0 + v + 2, quarter))

        class Steps:

            def __init__(self, eng, s):
                self.eng, self.s, self.n = eng, s, 0

            def __call__(self, ins):
                ins.then_inc(self.s, 1)
                self.n = self.n + 1
                self.eng.wait_ge(self.s, self.n)

        @block.sync
        def _(sp):
            def load(u, slot, parts, free=True):
                if free:
                    sp.wait_ge(w_lo, u - 1)
                for dst, src in parts:
                    sp.dma_start(dst, src).then_inc(w_arrived[slot], 16)

            def rows4(d, slot, kh, col, n):
                s = w4(stage, slot, n)
                return [(s[:, 2 * i:2 * i + 2, :], d[:, 4 * kh + 2 * i:4 * kh + 2 * i + 2, ds(col, n)])
                        for i in range(2)]

            def rows8(d, slot, col):
                s = w8(stage, slot)
                return [(s[:, 4 * i:4 * i + 4, :], d[:, 4 * i:4 * i + 4, ds(col, 256)]) for i in range(2)]

            for half in range(2):
                sp.dma_start(x_sb[:, :, 512 * half:512 * half + 512],
                             x_d[:, :, 512 * half:512 * half + 512]).then_inc(x_arrived[half], 16)
                load(half, half, rows4(w_in_d, half, half, C_Q, 512), free=False)
            smalls = [(pos_i[:, :], T["positions"][0].rearrange("(m p) -> p m", p=P)),
                      (pe_in[:, 0, :], T["pe_ck"][0].rearrange("(j a) d -> j (a d)", a=2)),
                      (pe_in[:, 1, :], T["pe_cv"][0].rearrange("(j a) d -> j (a d)", a=2)),
                      (w2[:, 0, :], T["w_ck2"][0]), (w2[:, 1, :], T["w_ck2"][0]), (w2[:, 2, :], T["w_cv2"][0]),
                      (ln_g[:, :], as_rows(T["ln_sgu_g"][0])), (ln_b[:, :], as_rows(T["ln_sgu_b"][0])),
                      (wsp[:, :, :], T["w_spatial"][0].rearrange("g t s -> t g s")),
                      (bsp[:, :], T["b_spatial"][0].rearrange("g t -> t g"))]
            for dst, src in smalls:
                sp.dma_start(dst, src, allow_slow_non_contiguous=True).then_inc(small_arrived, 16)
            for kh in range(2):
                load(U_KVA + kh, kh, rows4(w_in_d, kh, kh, C_KVA, 512))
            for kh in range(2):
                load(U_KVB + kh, kh, rows4(w_in_d, kh, kh, C_KVB, N_KVB))
            for u, col in ((U_V, C_V), (U_U, C_U)):
                for kh in range(2):
                    load(u + kh, kh, rows4(w_in_d, kh, kh, col, SG))
            load(U_MERGE0, 0, rows8(w_in_d, 0, C_MERGE))
            for u, d in ((U_CK, ck1_d), (U_CV, cv1_d)):
                s = w16(stage, u % 2)
                load(u, u % 2, [(s[:, 8 * i:8 * i + 8, :], d[:, 8 * i:8 * i + 8, :]) for i in range(2)])
            with sp.Fori(0, (N_MERGE - 2) // 2) as i:
                for b in range(2):
                    load(2 * i + U_MERGE + b, (U_MERGE + b) % 2,
                         rows8(w_in_d, (U_MERGE + b) % 2, 512 * i + C_MERGE + 256 * (1 + b)))
            load(U_BRANCH - 1, (U_BRANCH - 1) % 2, rows8(w_in_d, (U_BRANCH - 1) % 2, C_MERGE + 256 * (N_MERGE - 1)))
            with sp.Fori(0, 2) as c:
                s = w4(stage, 0)
                load(2 * c + U_BRANCH, 0,
                     [(s[DH * g:DH * g + DH, :, :], nsa_d[g][:, :, ds(512 * c, 512)]) for g in range(G)])
                load(2 * c + U_BRANCH + 1, 1, rows4(sgu_d, 1, 0, 512 * c, 512))
            sp.wait_ge(o_lo, MT * PAIRS)
            sp.dma_start(y[:, :, :], x_d).then_inc(x2_arrived, 16)
            with sp.Fori(0, 2) as c:
                for kh in range(2):
                    load(2 * c + U_OUT + kh, kh, rows4(wout_d, kh, kh, 512 * c, 512))
            sp.wait_ge(mg_lo, KD)
            for i, (g_, b_) in enumerate((("ln1_g", "ln1_b"), ("ln2_g", "ln2_b"))):
                sp.dma_start(lng[:, i, :], as_rows(T[g_][0])).then_inc(ln_arrived, 16)
                sp.dma_start(lnb[:, i, :], as_rows(T[b_][0])).then_inc(ln_arrived, 16)
            with sp.Fori(0, FT // 2) as i:
                load(2 * i + U_FFN, 0, rows8(gate_d, 0, 256 * i))
                load(2 * i + U_FFN + 1, 1, rows8(up_d, 1, 256 * i))

            def down(j, slot):
                s = w2d(stage, slot)
                load(U_DOWN + j, slot, [(s[:, f:f + 1, :], down_d[:, ds(2 * j + f, 1), :]) for f in range(2)])

            with sp.Fori(0, N_DOWN // 2) as i:
                for b in range(2):
                    down(2 * i + b, b)
            if N_DOWN % 2:
                down(N_DOWN - 1, (N_DOWN - 1) % 2)
            for m in range(MT):
                for h in h_ok:
                    sp.wait_ge(h, MT + m + 1)
                sp.dma_start(out_d[:, m, :], y[:, m, :]).then_inc(stored, 16)
            sp.wait_ge(stored, 16 * MT)

        @block.gpsimd
        def _(pool):
            step = Steps(pool, pool_step)
            step(pool.memset(ident[:, :], 0.0))
            step(pool.affine_select(out=ident[:, :], in_=ident[:, :], compare_op=ALU.not_equal, fill=1.0, base=0,
                                    pattern=[[-1, P]], channel_multiplier=1))
            step(pool.tensor_copy(ident_r[:, :], ident[:, :]))
            step(pool.memset(pc_flat[:, 0:P], 0.0))
            step(pool.memset(cbias[:, :, :], 0.0))
            step(pool.memset(any_block[:, :], 1.0))
            step(pool.affine_select(out=pc_flat[:, 0:P], in_=pc_flat[:, 0:P], compare_op=ALU.is_ge, fill=NEG, base=0,
                                    pattern=[[-1, P]], channel_multiplier=1))
            pool.tensor_copy(causal[:, :], pc_flat[:, 0:P]).then_inc(masks_ready, 1)
            pool.affine_select(out=cbias[:, :, :], in_=cbias[:, :, :], compare_op=ALU.is_ge, fill=NEG,
                               base=-(BLOCK - 1), pattern=[[P, MT], [-STRIDE, NB]],
                               channel_multiplier=1).then_inc(masks_ready, 1)
            pool.affine_select(out=any_block[:, :], in_=any_block[:, :], compare_op=ALU.is_ge, fill=0.0,
                               base=-(BLOCK - 1), pattern=[[P, MT]], channel_multiplier=1).then_inc(masks_ready, 1)
            for j in range(HALF):
                step(pool.memset(freq[:, j:j + 1], FREQ[j]))
            pool.wait_ge(small_arrived, 160)
            step(pool.tensor_copy(pos_f[:, :], pos_i[:, :]))
            for i in range(2):
                for m in range(MT):
                    step(pool.tensor_scalar(ang[:, i, m, :], freq[:, :], pos_f[:, m:m + 1], None, ALU.mult))
                step(pool.tensor_scalar(turns[:, i], ang[:, i], 1.0 / (2 * math.pi), 0.25 * i, ALU.mult, ALU.add))
            step(pool.tensor_scalar(turns[:, :], turns[:, :], MAGIC, None, ALU.add))
            step(pool.tensor_scalar(turns[:, :], turns[:, :], -MAGIC, None, ALU.add))
            for part in (PI_1, PI_2, PI_3):
                step(pool.tensor_scalar(tmp_b[:, :], turns[:, :], -part, None, ALU.mult))
                step(pool.tensor_tensor(ang[:, :], ang[:, :], tmp_b[:, :], ALU.add))
            step(pool.tensor_scalar(ang[:, 1], ang[:, 1], math.pi / 2, None, ALU.add))
            pool.tensor_scalar(ang[:, :], ang[:, :], PI_IN, -PI_IN, ALU.min, ALU.max).then_inc(ang_ready, 1)
            pool.affine_select(out=wsp[:, :, :], in_=wsp[:, :, :], compare_op=ALU.is_ge, fill=0.0, base=0,
                               pattern=[[0, 4], [-1, P]], channel_multiplier=1).then_inc(masks_ready, 1)

            pool.wait_ge(trig_ready, 1)

            def rotate(src, dst, heads):
                t = [rope_t[:, i, :, 0:heads, :] for i in range(4)]
                x1, x2 = src[..., 0:HALF], src[..., HALF:2 * HALF]
                sn, cs = [trig[:, i, :, :].rearrange("p m (h j) -> p m h j", h=1).broadcast_to([P, MT, heads, HALF])
                          for i in range(2)]
                pool.tensor_tensor(t[0], x1, cs, ALU.mult).then_inc(pool_step, 1)
                pool.tensor_tensor(t[1], x2, sn, ALU.mult).then_inc(pool_step, 1)
                pool.tensor_tensor(t[2], x2, cs, ALU.mult).then_inc(pool_step, 1)
                pool.tensor_tensor(t[3], x1, sn, ALU.mult).then_inc(pool_step, 1)
                step.n += 4
                pool.wait_ge(pool_step, step.n)
                return t

            pool.wait_ge(raw_act, 4)
            pool.wait_ge(raw_dve, 4)
            for col in (0, 2 * P):
                k = kva[:, :, col:col + P].rearrange("p m (g d) -> p m g d", g=G)
                t = rotate(k, k, G)
                step(pool.tensor_tensor(k[..., 0:HALF], t[0], t[1], ALU.subtract))
                step(pool.tensor_tensor(k[..., HALF:2 * HALF], t[2], t[3], ALU.add))
            for m in range(MT):
                step(pool.tensor_copy(q_view[:, m], q_raw[:, m, :].rearrange("p (g k d) -> p g k d", g=G, k=PAIRS)))
            q_heads = q_raw[:, :, :].rearrange("p m (h d) -> p m h d", h=G * R)
            t = rotate(q_heads, None, G * R)
            for m in range(MT):
                tv = [t_[:, m].rearrange("p (g k) j -> p g k j", g=G) for t_ in t]
                step(pool.tensor_tensor(q_view[:, m][..., 0:HALF], tv[0], tv[1], ALU.subtract))
                step(pool.tensor_tensor(q_view[:, m][..., HALF:2 * HALF], tv[2], tv[3], ALU.add))
            pool.wait_ge(raw_act, 6)
            pool.wait_ge(raw_dve, 6)
            k = kvb[:, :, 0:P].rearrange("p m (g d) -> p m g d", g=G)
            t = rotate(k, k, G)
            step(pool.tensor_tensor(k[..., 0:HALF], t[0], t[1], ALU.subtract))
            pool.tensor_tensor(k[..., HALF:2 * HALF], t[2], t[3], ALU.add).then_inc(roped, 1)
            for br, v in ((0, kva[:, :, 3 * P:4 * P]), (1, kvb[:, :, P:2 * P])):
                step(pool.tensor_copy(v_t(ath, br), v))
                pool.tensor_tensor(v_t(atl, br), v, v_t(ath, br).bitcast(fp32), ALU.subtract).then_inc(roped, 1)
            pool.wait_ge(pe_ok, 1)
            pool.wait_ge(tr_done, 8)
            for c, tok in ((0, tok_k), (1, tok_v)):
                step(pool.memset(flat[:, c, :, :, NCB:NB], 0.0))
                pool.wait_ge(tok, 4)
                for g in range(G):
                    src = tok2[:, c, g, :].rearrange("p (n j) -> p j n", j=8)
                    for jh in range(2):
                        step(pool.tensor_tensor(
                            flat[:, c, 8 * jh:8 * jh + 8, g, 0:NCB], src[:, :, jh:jh + NCB],
                            pe_t[:, c, 8 * jh:8 * jh + 8].rearrange("p (j n) -> p j n", n=1).broadcast_to([P, 8, NCB]),
                            ALU.add))
                src = flat[:, c].rearrange("p j g n -> p (j g n)")
                step(pool.tensor_copy(flath[:, c, :], src))
                pool.tensor_tensor(flatl[:, c, :], src, flath[:, c, :].bitcast(fp32),
                                   ALU.subtract).then_inc(flat_ok, 1)
            for a, i in enumerate(SOFT_STEPS):
                n = P * (STEPS[i][0] + 1)
                pool.wait_ge(rinv_ok, a + 1)
                pool.tensor_scalar(prob[:, a % 2, 1, 0:n], prob[:, a % 2, 1, 0:n], rinv[:, a % 2, 1:2], None,
                                   ALU.mult).then_inc(p_ok[1], 1)
            for k in range(2 * MT):
                ln, m = divmod(k, MT)
                pool.wait_ge(scaled, k + 1)
                pool.tensor_tensor(y[:, m, BIAS_COLS:D], y[:, m, BIAS_COLS:D], lnb[:, ln, BIAS_COLS:D],
                                   ALU.add).then_inc(h_ok[1], 1)

        @block.scalar
        def _(act):
            def split(u, slot, n=2048):
                act.wait_ge(w_arrived[slot], (16 * (u - slot) + 32) if not isinstance(u, int) else 32 * (u // 2 + 1))
                if not isinstance(u, int) or u >= 2:
                    act.wait_ge(w_used, u - 1)
                act.copy(wh[:, slot, 0:n], stage[:, slot, 0:n]).then_inc(w_hi, 1)

            def hi(dst, src):
                return act.copy(dst, src)

            for k in range(KD):
                act.wait_ge(xt_done, k + 1)
                hi(xh[:, k, :], ps[:, 4 + k % 2, :]).then_inc(xt_hi, 1)
                if k == 1:
                    split(0, 0)
                if k == 3:
                    split(1, 1)

            def chunk(u, c, dst, n, n_next=2048):
                split(u + 2, 0, n_next)
                for m in (0, 2):
                    act.wait_ge(rows_done, 3 * c + m + 1)
                    act.copy(dst[:, m, :], ps[:, m, 0:n]).then_inc(raw_act, 1)
                split(u + 3, 1, n_next)

            chunk(U_Q, 0, q_raw, 512)
            act.wait_ge(ang_ready, 1)
            act.activation(trig[:, :, :, :], ang[:, :, :, :], ACT.Sin).then_inc(trig_ready, 1)
            chunk(U_KVA, 1, kva, 512, 4 * N_KVB)
            chunk(U_KVB, 2, kvb, N_KVB)
            with act.Fori(0, 2) as c:
                u = 2 * c + U_V
                split(u + 2, 0)
                for m in (0, 2):
                    act.wait_ge(rows_done, 3 * c + 9 + m + 1)
                    act.copy(raw[:, ds(2 * c + 2, 1), m, :], ps[:, m:m + 1, :]).then_inc(raw_act, 1)
                split(u + 3, 1)

            act.wait_ge(pe_tr, 1)
            act.copy(pe_t[:, :, :], ps[:, 0, 0:32].rearrange("p (c j) -> p c j", c=2)).then_inc(pe_ok, 1)
            act.wait_ge(tr_done, 1)
            for g in range(G):
                for par in range(2):
                    act.copy(tok2[DH * par:DH * par + DH, 0, g, :],
                             ps[DH * g:DH * g + DH, 4, par:SEQ:2]).then_inc(tok_k, 1)
            for t in range(2, 8):
                act.wait_ge(tr_done, t + 1)
                if t < 4:
                    hi(k_t(ath, t - 2), ps[:, 4 + t % 4, :]).then_inc(op_hi, 1)
                else:
                    act.mul(q_t(ath)[:, t - 4, :], ps[:, 4 + t % 4, :], SCALE).then_inc(op_hi, 1)
            act.wait_ge(small_arrived, 160)
            hi(w2h[:, :, :], w2[:, :, :]).then_inc(w2_hi, 1)
            act.wait_ge(raw_dve, 6)
            act.wait_ge(raw_act, 6)
            act.activation(gates[:, :, :, :, :].rearrange("p m g r b -> p m (g r b)"),
                           kvb[:, :, 2 * P:2 * P + GATE_W], ACT.Sigmoid).then_inc(gates_ok, 1)
            act.wait_ge(raw_dve, 10)
            act.wait_ge(raw_act, 10)
            act.activation(v_raw, v_raw, ACT.Gelu_apprx_tanh).then_inc(gelu_ok, 1)
            act.activation(u_raw, u_raw, ACT.Gelu_apprx_tanh).then_inc(gelu_ok, 1)
            split(U_CV, 0)

            def take_merge(f, u, second):
                if second:
                    act.wait_ge(w_used, u + 1)
                else:
                    act.wait_ge(merge_half, f // 2 + 1)
                act.copy(merge[:, f, :], ps[:, M0 + f % 2, :]).then_inc(merge_out, 1)

            act.wait_ge(vsq_in, 1)
            act.activation(vrs[:, 1, :], vrs[:, 0, :], ACT.Sqrt).then_inc(vsq_ok, 1)
            take_merge(0, U_MERGE0, False)
            take_merge(1, U_MERGE0, True)
            split(U_MERGE, 1)
            for c in range(2):
                act.wait_ge(w_used, U_CK + c + 1)
                act.activation(hid[:, c, :], ps[:, 4 + c, 0:G * NB], ACT.Silu).then_inc(hid_ok, 1)
                act.wait_ge(hid_ok, c + 1)
                hi(hidh[:, c, :], hid[:, c, :]).then_inc(hid_hi, 1)
            split(U_MERGE + 1, 0)
            act.wait_ge(vln_ok, MT)
            act.wait_ge(w_used, U_CV + 1)
            hi(oth[:, :, :], v_raw).then_inc(vh_ok, 1)
            take_merge(2, U_MERGE, False)
            act.wait_ge(cmp_done, 1)
            for g in range(G):
                hi(kch[DH * g:DH * g + DH, :], ps[DH * g:DH * g + DH, 2, NB * g:NB * g + NB]).then_inc(cmp_hi, 1)
            act.wait_ge(cmp_done, 2)
            hi(vch[:, :], ps[0:NB, 3, 0:P]).then_inc(cmp_hi, 1)
            act.wait_ge(wt_done, 1)
            hi(wth[:, :, :].rearrange("p g t -> p (g t)"), ps[:, 4, :]).then_inc(wt_hi, 1)
            take_merge(3, U_MERGE, True)
            split(U_MERGE + 2, 1)
            act.wait_ge(sc_max, 1)
            act.activation(pc_flat, pc_flat, ACT.Exp).then_inc(sc_exp, 1)

            def take_o(w):
                qt, pp, _ = STEPS[3 * w]
                act.wait_ge(pv_done, 3 * w + 3)
                for g in range(G):
                    hi(oth[DH * g:DH * g + DH, pp, P * qt:P * qt + P],
                       ps[DH * g:DH * g + DH, O0 + w % 2, P * g:P * g + P]).then_inc(o_hi, 1)

            f_out = 0
            act.wait_ge(mix_done, 4)
            for i in range(N_STEPS + 3):
                if 2 <= i < N_STEPS + 2:
                    a = i - 2
                    n = G * P * (STEPS[a][0] + 1) if STEPS[a][2] < 2 else G * P
                    rows = P if STEPS[a][2] < 2 else NB
                    act.wait_ge(pt_done, a + 1)
                    if a >= 1:
                        act.wait_ge(pv_done, a)
                    hi(pth[0:rows, 0:n], ps[0:rows, PT0:PT0 + 2, :].rearrange("p b c -> p (b c)")[:, 0:n]).then_inc(pt_hi, 1)
                if i in SOFT:
                    a = SOFT[i]
                    act.wait_ge(s_max, a + 1)
                    if a >= 2:
                        act.wait_ge(pt_done, SOFT_STEPS[a - 2] + 1)
                    n = P * (STEPS[i][0] + 1)
                    for g in range(G):
                        act.activation(prob[:, a % 2, g, 0:n], ps[:, g, 0:n], ACT.Exp, bias=nmax[:, a % 2, g:g + 1],
                                       accum_out=rsum[:, a % 2, g:g + 1]).then_inc(s_exp, 1)
                if i >= 5 and i % 3 == 2:
                    take_o((i - 5) // 3)
                while f_out < fills_done(i + 1):
                    u = U_FILL0 + f_out // 2
                    take_merge(4 + f_out, u, f_out % 2 == 1)
                    f_out += 1
                for u, quarter in QUARTERS[i]:
                    if quarter == 0:
                        act.wait_ge(w_arrived[u % 2], 32 * (u // 2 + 1))
                        act.wait_ge(w_used, u - 1)
                    part = slice(512 * quarter, 512 * quarter + 512)
                    last = act.copy(wh[:, u % 2, part], stage[:, u % 2, part])
                    last.then_inc(quarter_hi if quarter < 3 else w_hi, 1)

            for k in range(4):
                act.wait_ge(st_done, k + 1)
                hi(sgh[:, k, :], ps[:, 4 + k, :]).then_inc(st_hi, 1)
            act.wait_ge(merge_out, 16)
            for f in (0, 8, 4, 12):
                act.activation(merge[:, f:f + 4, :], merge[:, f:f + 4, :], ACT.Sigmoid).then_inc(sig_ok, 1)
            with act.Fori(0, 2) as c:
                split(2 * c + U_BRANCH + 2, 0)
                for f in range(4):
                    act.wait_ge(mg_ok, 4 * c + f + 1)
                    act.copy(xh[:, ds(4 * c + f, 1), :], merge[:, ds(4 * c + f, 1), :]).then_inc(mg_hi, 1)
                split(2 * c + U_BRANCH + 3, 1)
            def split_to(dst, u, slot, used):
                act.wait_ge(w_arrived[slot], 32 * (u // 2 + 1))
                act.wait_ge(w_used, used)
                act.copy(dst, stage[:, slot, :]).then_inc(w_hi, 1)

            split(U_OUT + 2, 0)
            split(U_OUT + 3, 1)
            split_to(first_h[:, :], U_FFN, 0, U_BRANCH)

            def root(k):
                m = k % MT
                act.wait_ge(var_ok, k + 1)
                act.activation(nrm[:, m, 1:2], nrm[:, m, 0:1], ACT.Sqrt).then_inc(sq_ok, 1)
                act.activation(y[:, m, :], y[:, m, :], ACT.Identity, bias=nrm[:, m, 4:5]).then_inc(centred, 1)

            def ht_hi_of(m):
                act.wait_ge(ht_done, m + 1)
                hi(hth[:, :, P * m:P * m + P],
                   ps[:, 4 + 2 * (m % 2):6 + 2 * (m % 2), :].rearrange("p b (k t) -> p (b k) t", k=4)).then_inc(ht_hi, 1)

            root(0)
            root(1)
            ht_hi_of(0)
            root(2)
            ht_hi_of(1)
            split(U_FFN + 1, 1)
            root(3)
            ht_hi_of(2)
            ht_hi_of(3)

            def ffn(i):
                u = 2 * i + U_FFN
                for f in range(2):
                    if f == 0:
                        act.wait_ge(ffn_half, 2 * i + 1)
                    else:
                        act.wait_ge(w_used, u + 1)
                    act.activation(hid_sg[:, f, :], ps[:, f, :], ACT.Silu).then_inc(silu_ok, 1)
                split(u + 2, 0)
                split(u + 3, 1)
                act.wait_ge(fact_ok, 2 * i + 2)

            def tiles_hi(j, slot):
                act.copy(ah[:, slot, :, :], fact[:, ds(2 * j, 2), :]).then_inc(a_hi, 1)

            with act.Fori(0, FT // 2 - 1) as i:
                ffn(i)
            tiles_hi(0, 0)
            tiles_hi(1, 1)
            ffn(FT // 2 - 1)
            with act.Fori(0, (N_DOWN - 5) // 2) as i:
                for b in range(2):
                    split(2 * i + U_DOWN + b + 2, b)
                    tiles_hi(2 * i + b + 2, b)
            split(U_DOWN + N_DOWN - 3, 0)
            tiles_hi(N_DOWN - 3, 0)
            split_to(late_h, U_DOWN + N_DOWN - 2, 1, U_DOWN)
            tiles_hi(N_DOWN - 2, 2)
            tiles_hi(N_DOWN - 1, 3)
            split_to(wh[:, 1, :], U_DOWN + N_DOWN - 1, 0, U_DOWN + N_DOWN - 3)
            for m in range(MT):
                root(MT + m)

        @block.vector
        def _(dve):
            step = Steps(dve, dve_step)

            def split(u, slot, n=2048):
                dve.wait_ge(w_hi, u + 1)
                dve.tensor_tensor(wl[:, slot, 0:n], stage[:, slot, 0:n], wh[:, slot, 0:n].bitcast(fp32),
                                  ALU.subtract).then_inc(w_lo, 1)

            def lo(dst, src, h):
                return dve.tensor_tensor(dst, src, h.bitcast(fp32), ALU.subtract)

            for k in range(KD):
                dve.wait_ge(xt_hi, k + 1)
                lo(xl[:, k, :], ps[:, 4 + k % 2, :], xh[:, k, :]).then_inc(xt_lo, 1)
                if k == 1:
                    split(0, 0)
                if k == 3:
                    split(1, 1)

            def chunk(u, c, dst, n, n_next=2048):
                split(u + 2, 0, n_next)
                dve.wait_ge(rows_done, 3 * c + 2)
                dve.tensor_copy(dst[:, 1, :], ps[:, 1, 0:n]).then_inc(raw_dve, 1)
                dve.wait_ge(w_used, u + 2)
                dve.tensor_copy(dst[:, 3, :], ps[:, 3, 0:n]).then_inc(raw_dve, 1)
                split(u + 3, 1, n_next)

            chunk(U_Q, 0, q_raw, 512)
            chunk(U_KVA, 1, kva, 512, 4 * N_KVB)
            chunk(U_KVB, 2, kvb, N_KVB)
            with dve.Fori(0, 2) as c:
                u = 2 * c + U_V
                split(u + 2, 0)
                dve.wait_ge(rows_done, 3 * c + 11)
                dve.tensor_copy(raw[:, ds(2 * c + 2, 1), 1, :], ps[:, 1:2, :]).then_inc(raw_dve, 1)
                dve.wait_ge(w_used, u + 2)
                dve.tensor_copy(raw[:, ds(2 * c + 2, 1), 3, :], ps[:, 3:4, :]).then_inc(raw_dve, 1)
                split(u + 3, 1)

            dve.wait_ge(tr_done, 2)
            for g in range(G):
                for par in range(2):
                    dve.tensor_copy(tok2[DH * par:DH * par + DH, 1, g, :],
                                    ps[DH * g:DH * g + DH, 5, par:SEQ:2]).then_inc(tok_v, 1)
            for t in range(2, 8):
                dve.wait_ge(op_hi, t - 1)
                if t < 4:
                    lo(k_t(atl, t - 2), ps[:, 4 + t % 4, :], k_t(ath, t - 2)).then_inc(op_lo, 1)
                else:
                    dve.scalar_tensor_tensor(out=q_t(atl)[:, t - 4, :], in0=ps[:, 4 + t % 4, :], scalar=SCALE,
                                             in1=q_t(ath)[:, t - 4, :].bitcast(fp32), op0=ALU.mult,
                                             op1=ALU.subtract).then_inc(op_lo, 1)
            dve.wait_ge(w2_hi, 1)
            lo(w2l[:, :, :], w2[:, :, :], w2h[:, :, :]).then_inc(w2_lo, 1)
            dve.wait_ge(gelu_ok, 1)
            for m in range(MT):
                step(dve.bn_stats(vstat[:, m, :], v_raw[:, m, :]))
                step(dve.bn_aggr(vmv[:, m, :], vstat[:, m, :]))
            dve.tensor_scalar(vrs[:, 0, :], vmv[:, :, 1], EPS, None, ALU.add).then_inc(vsq_in, 1)
            split(U_CV, 0)
            dve.wait_ge(vsq_ok, 1)
            step(dve.reciprocal(vrs[:, 2, :], vrs[:, 1, :]))
            step(dve.tensor_tensor(vrs[:, 3, :], vrs[:, 2, :], vrs[:, 2, :], ALU.mult))
            step(dve.tensor_tensor(vrs[:, 3, :], vrs[:, 3, :], vrs[:, 0, :], ALU.mult))
            step(dve.tensor_scalar(vrs[:, 3, :], vrs[:, 3, :], -0.5, 1.5, ALU.mult, ALU.add))
            step(dve.tensor_tensor(vrs[:, 3, :], vrs[:, 3, :], vrs[:, 2, :], ALU.mult))
            for m in range(MT):
                step(dve.scalar_tensor_tensor(out=v_raw[:, m, :], in0=v_raw[:, m, :], scalar=vmv[:, m, 0:1],
                                              in1=ln_g[:, :], op0=ALU.subtract, op1=ALU.mult))
                dve.scalar_tensor_tensor(out=v_raw[:, m, :], in0=v_raw[:, m, :], scalar=vrs[:, 3, m:m + 1],
                                         in1=ln_b[:, :], op0=ALU.mult, op1=ALU.add).then_inc(vln_ok, 1)
            split(U_MERGE, 1)
            for c in range(2):
                dve.wait_ge(hid_hi, c + 1)
                lo(hidl[:, c, :], hid[:, c, :], hidh[:, c, :]).then_inc(hid_lo, 1)
            split(U_MERGE + 1, 0)
            dve.wait_ge(vh_ok, 1)
            lo(otl[:, :, :], v_raw, oth[:, :, :]).then_inc(vl_ok, 1)
            for g in range(G):
                dve.wait_ge(cmp_hi, g + 1)
                lo(kcl[DH * g:DH * g + DH, :], ps[DH * g:DH * g + DH, 2, NB * g:NB * g + NB],
                   kch[DH * g:DH * g + DH, :]).then_inc(cmp_lo, 1)
            dve.wait_ge(cmp_hi, 3)
            lo(vcl[:, :], ps[0:NB, 3, 0:P], vch[:, :]).then_inc(cmp_lo, 1)
            dve.wait_ge(wt_hi, 1)
            lo(wtl[:, :, :].rearrange("p g t -> p (g t)"), ps[:, 4, :],
               wth[:, :, :].rearrange("p g t -> p (g t)")).then_inc(wt_lo, 1)
            split(U_MERGE + 2, 1)

            dve.wait_ge(masks_ready, 4)
            for g in range(G):
                dve.wait_ge(sc_done, g + 1)
                step(dve.tensor_tensor(pcmp[:, g], ps[:, g, :].rearrange("p (m k n) -> p m k n", m=MT, k=PAIRS),
                                       cbias[:, :, :].rearrange("p m (k n) -> p m k n", k=1).broadcast_to(
                                           [P, MT, PAIRS, NB]), ALU.add))
            rows = pc_flat.rearrange("p (r n) -> p r n", n=NB)

            def per_row(v):
                return v.rearrange("p (r n) -> p r n", n=1).broadcast_to([P, G * MT * PAIRS, NB])

            step(dve.tensor_reduce(cmax, rows, AX.X, ALU.max))
            dve.tensor_tensor(rows, rows, per_row(cmax), ALU.subtract).then_inc(sc_max, 1)
            dve.wait_ge(gelu_ok, 2)
            for gs in range(4):
                dve.wait_ge(mix_done, gs + 1)
                uv = u_raw[:, :, P * gs:P * gs + P]
                dve.scalar_tensor_tensor(out=uv, in0=ps[:, 2 + gs, :].rearrange("p (n c) -> p n c", n=MT),
                                         scalar=bsp[:, gs:gs + 1], in1=uv, op0=ALU.add,
                                         op1=ALU.mult).then_inc(sgu_ok, 1)

            def weigh_cmp():
                dve.wait_ge(sc_exp, 1)
                step(dve.tensor_reduce(csum_f, rows, AX.X, ALU.add))
                step(dve.reciprocal(csum_f, csum_f))
                step(dve.tensor_tensor(csum, csum, any_block[:, :].rearrange(
                    "p (g m k) -> p g m k", g=1, k=1).broadcast_to([P, G, MT, PAIRS]), ALU.mult))
                dve.wait_ge(gates_ok, 1)
                for g in range(G):
                    step(dve.tensor_tensor(csum[:, g], csum[:, g], gates[:, :, g, :, 0], ALU.mult))
                dve.tensor_tensor(rows, rows, per_row(csum_f), ALU.mult).then_inc(pcmp_ok, 1)

            def norm_prob(i):
                a = SOFT[i]
                qt, pp, br = STEPS[i]
                n = P * (qt + 1)
                dve.wait_ge(s_exp, 2 * a + 2)
                step(dve.reciprocal(rinv[:, a % 2, :], rsum[:, a % 2, :]))
                dve.tensor_tensor(rinv[:, a % 2, :], rinv[:, a % 2, :], gates[:, qt, :, pp, 1 + br],
                                  ALU.mult).then_inc(rinv_ok, 1)
                dve.wait_ge(rinv_ok, a + 1)
                dve.tensor_scalar(prob[:, a % 2, 0, 0:n], prob[:, a % 2, 0, 0:n], rinv[:, a % 2, 0:1],
                                  None, ALU.mult).then_inc(p_ok[0], 1)

            def lo_prob(a):
                n = G * P * (STEPS[a][0] + 1) if STEPS[a][2] < 2 else G * P
                rws = P if STEPS[a][2] < 2 else NB
                dve.wait_ge(pt_hi, a + 1)
                lo(ptl[0:rws, 0:n], ps[0:rws, PT0:PT0 + 2, :].rearrange("p b c -> p (b c)")[:, 0:n],
                   pth[0:rws, 0:n]).then_inc(pt_lo, 1)

            def lo_quarter(u, quarter):
                if quarter < 3:
                    dve.wait_ge(quarter_hi, 3 * (u - U_FILL0 - 2) + quarter + 1)
                else:
                    dve.wait_ge(w_hi, u + 1)
                part = slice(512 * quarter, 512 * quarter + 512)
                last = lo(wl[:, u % 2, part], stage[:, u % 2, part], wh[:, u % 2, part])
                if quarter == 3:
                    last.then_inc(w_lo, 1)

            for i in range(N_STEPS + 3):
                if i - 1 in SOFT:
                    norm_prob(i - 1)
                if 2 <= i < N_STEPS + 2:
                    lo_prob(i - 2)
                if i in SOFT:
                    a = SOFT[i]
                    dve.wait_ge(s_done, a + 1)
                    dve.tensor_reduce(nmax[:, a % 2, :], ps[:, 0:G, 0:P * (STEPS[i][0] + 1)], AX.X, ALU.max,
                                      negate=True).then_inc(s_max, 1)
                if i == 2:
                    weigh_cmp()
                if i >= 5 and i % 3 == 2:
                    w = (i - 5) // 3
                    qt, pp, _ = STEPS[3 * w]
                    dve.wait_ge(o_hi, 2 * w + 2)
                    for g in range(G):
                        o = lo(otl[DH * g:DH * g + DH, pp, P * qt:P * qt + P],
                               ps[DH * g:DH * g + DH, O0 + w % 2, P * g:P * g + P],
                               oth[DH * g:DH * g + DH, pp, P * qt:P * qt + P])
                        if g == G - 1:
                            o.then_inc(o_lo, 1)
                if i >= 1:
                    for u, quarter in QUARTERS[i - 1]:
                        lo_quarter(u, quarter)
            for u, quarter in QUARTERS[N_STEPS + 2]:
                lo_quarter(u, quarter)

            for k in range(4):
                dve.wait_ge(st_hi, k + 1)
                lo(sgl[:, k, :], ps[:, 4 + k, :], sgh[:, k, :]).then_inc(st_lo, 1)

            with dve.Fori(0, 2) as c:
                dve.wait_ge(sig_ok, 2 * c + 2)
                for f in range(4):
                    if f < 3:
                        dve.wait_ge(br_done, 6 * c + f + 1)
                    else:
                        dve.wait_ge(w_used, 2 * c + U_BRANCH + 1)
                    gt = merge[:, ds(4 * c + f, 1), :]
                    dve.tensor_tensor(gt, gt, ps[:, f:f + 1, :], ALU.mult).then_inc(br_prod, 1)
                split(2 * c + U_BRANCH + 2, 0)
                for f in range(4):
                    if f < 3:
                        dve.wait_ge(br_done, 6 * c + 3 + f + 1)
                    else:
                        dve.wait_ge(w_used, 2 * c + U_BRANCH + 2)
                    gn, gt = merge[:, ds(4 * c + f, 1), :], merge[:, ds(4 * c + f + 8, 1), :]
                    dve.tensor_tensor(gt, gt, ps[:, 4 + f:5 + f, :], ALU.mult).then_inc(br_prod, 1)
                    dve.wait_ge(br_prod, 8 * c + 4 + f + 1)
                    dve.tensor_tensor(gn, gn, gt, ALU.add).then_inc(mg_ok, 1)
                    dve.wait_ge(mg_hi, 4 * c + f + 1)
                    dve.tensor_tensor(xl[:, ds(4 * c + f, 1), :], gn, xh[:, ds(4 * c + f, 1), :].bitcast(fp32),
                                      ALU.subtract).then_inc(mg_lo, 1)
                split(2 * c + U_BRANCH + 3, 1)

            def split_to(dst, src_h, u, slot):
                dve.wait_ge(w_hi, u + 1)
                lo(dst, stage[:, slot, :], src_h).then_inc(w_lo, 1)

            def moments(m, half):
                return dve.bn_stats(stat[:, m, half, :], y[:, m, 512 * half:512 * half + 512])

            def add_rows(m, half, bank):
                ym = y[:, m, 512 * half:512 * half + 512]
                return dve.scalar_tensor_tensor(out=ym, in0=ym, scalar=ALPHA, in1=ps[:, bank, :], op0=ALU.mult,
                                                op1=ALU.add)

            def variance(m):
                step(dve.bn_aggr(mv[:, m, :], stat[:, m, :, :].rearrange("p a b -> p (a b)")))
                dve.tensor_scalar(nrm[:, m, 4:5], mv[:, m, 0:1], -1.0, None, ALU.mult)
                dve.tensor_scalar(nrm[:, m, 0:1], mv[:, m, 1:2], EPS, None, ALU.add).then_inc(var_ok, 1)

            def norm(k):
                ln, m = divmod(k, MT)
                n = nrm[:, m, :]
                dve.wait_ge(sq_ok, k + 1)
                step(dve.reciprocal(n[:, 2:3], n[:, 1:2]))
                step(dve.scalar_tensor_tensor(out=n[:, 3:4], in0=n[:, 2:3], scalar=n[:, 0:1], in1=n[:, 2:3],
                                              op0=ALU.mult, op1=ALU.mult))
                step(dve.tensor_scalar(n[:, 3:4], n[:, 3:4], -0.5, 1.5, ALU.mult, ALU.add))
                step(dve.tensor_tensor(n[:, 3:4], n[:, 3:4], n[:, 2:3], ALU.mult))
                dve.wait_ge(centred, k + 1)
                dve.scalar_tensor_tensor(out=y[:, m, :], in0=y[:, m, :], scalar=n[:, 3:4], in1=lng[:, ln, :],
                                         op0=ALU.mult, op1=ALU.mult).then_inc(scaled, 1)
                dve.wait_ge(scaled, k + 1)
                dve.tensor_tensor(y[:, m, 0:BIAS_COLS], y[:, m, 0:BIAS_COLS], lnb[:, ln, 0:BIAS_COLS],
                                  ALU.add).then_inc(h_ok[0], 1)

            def ht_lo_of(m):
                dve.wait_ge(ht_hi, m + 1)
                lo(htl[:, :, P * m:P * m + P],
                   ps[:, 4 + 2 * (m % 2):6 + 2 * (m % 2), :].rearrange("p b (k t) -> p (b k) t", k=4),
                   hth[:, :, P * m:P * m + P]).then_inc(ht_lo, 1)

            dve.wait_ge(x2_arrived, 16)
            split(U_OUT + 2, 0)
            for m in range(MT):
                if m < 3:
                    dve.wait_ge(rows_done, 15 + m + 1)
                else:
                    dve.wait_ge(w_used, U_OUT + 2)
                add_rows(m, 0, m).then_inc(mg_lo, 1)
            split(U_OUT + 3, 1)
            dve.wait_ge(mg_lo, KD + MT)
            for m in range(MT):
                moments(m, 0)
            split_to(first_l[:, :], first_h[:, :], U_FFN, 0)
            dve.wait_ge(ln_arrived, 64)
            for m in range(MT):
                if m < 3:
                    dve.wait_ge(rows_done, 18 + m + 1)
                else:
                    ht_lo_of(0)
                    ht_lo_of(1)
                    dve.wait_ge(w_used, U_FFN)
                add_rows(m, 1, m).then_inc(mg_lo, 1)
                dve.wait_ge(mg_lo, KD + MT + m + 1)
                step(moments(m, 1))
                variance(m)
                if m == 3:
                    split(U_FFN + 1, 1)
                norm(m)
            ht_lo_of(2)
            ht_lo_of(3)

            def ffn(i):
                u = 2 * i + U_FFN
                split(u + 2, 0)
                for f in range(2):
                    dve.wait_ge(silu_ok, 2 * i + f + 1)
                    if f == 0:
                        dve.wait_ge(ffn_half, 2 * i + 2)
                    else:
                        dve.wait_ge(w_used, u + 2)
                    dve.tensor_tensor(fact[:, ds(2 * i + f, 1), :], hid_sg[:, f:f + 1, :], ps[:, 2 + f:3 + f, :],
                                      ALU.mult).then_inc(fact_ok, 1)
                split(u + 3, 1)

            def tiles_lo(j, slot):
                dve.wait_ge(a_hi, j + 1)
                dve.tensor_tensor(al[:, slot, :, :], fact[:, ds(2 * j, 2), :], ah[:, slot, :, :].bitcast(fp32),
                                  ALU.subtract).then_inc(a_lo, 1)

            with dve.Fori(0, FT // 2 - 1) as i:
                ffn(i)
            tiles_lo(0, 0)
            tiles_lo(1, 1)
            ffn(FT // 2 - 1)
            with dve.Fori(0, (N_DOWN - 5) // 2) as i:
                for b in range(2):
                    split(2 * i + U_DOWN + b + 2, b)
                    tiles_lo(2 * i + b + 2, b)
            split(U_DOWN + N_DOWN - 3, 0)
            tiles_lo(N_DOWN - 3, 0)
            split_to(late_l, late_h, U_DOWN + N_DOWN - 2, 1)
            tiles_lo(N_DOWN - 2, 2)
            tiles_lo(N_DOWN - 1, 3)
            split_to(wl[:, 1, :], wh[:, 1, :], U_DOWN + N_DOWN - 1, 0)
            for m in range(MT):
                for half in range(2):
                    dve.wait_ge(rows_out, 2 * m + half + 1)
                    step(add_rows(m, half, 2 * m + half))
                    step(moments(m, half))
                variance(m)
                norm(MT + m)

        @block.tensor
        def _(pe):
            def mm3(out, sh, sl, mh, ml, start, stop):
                pe.matmul(out, sh, mh, start=start, stop=False)
                pe.matmul(out, sh, ml, start=False, stop=False)
                return pe.matmul(out, sl, mh, start=False, stop=stop)

            def transpose(out, in_, k=P):
                return pe.transpose(out, in_, ident[0:k, 0:k])

            def x_tile(k):
                pe.wait_ge(x_arrived[k // 4], 16)
                if k >= 2:
                    pe.wait_ge(xt_lo, k - 1)
                for m in range(MT):
                    last = transpose(ps[:, 4 + k % 2, P * m:P * m + P], x_sb[:, m, P * k:P * k + P])
                last.then_inc(xt_done, 1)

            pe.wait_ge(masks_ready, 1)
            for k in range(4):
                x_tile(k)

            def tokens(u, lh, ll, n, before):
                for kh in range(2):
                    pe.wait_ge(w_lo, u + kh + 1)
                    before(kh, None)
                    for m in range(MT):
                        before(kh, m)
                        for k in range(4):
                            kk = 4 * kh + k
                            tok = slice(P * m, P * m + P)
                            last = mm3(ps[:, m, 0:n], lh[:, kk, tok], ll[:, kk, tok], w4(wh, kh, n)[:, k, :],
                                       w4(wl, kh, n)[:, k, :], kk == 0, kk == KD - 1)
                        if kh == 1 and m < MT - 1:
                            last.then_inc(rows_done, 1)
                    last.then_inc(w_used, 1)

            def bank_free(c):
                def before(kh, m):
                    if kh == 0 and m is not None:
                        pe.wait_ge(raw_dve if m % 2 else raw_act, 2 * (c - 1) + m // 2 + 1)
                return before

            def first_chunk(kh, m):
                if m is None and kh == 0:
                    pe.wait_ge(xt_lo, 4)
                if m is None and kh == 1:
                    for k in range(4, KD):
                        x_tile(k)
                    pe.wait_ge(xt_lo, KD)

            tokens(U_Q, xh, xl, 512, first_chunk)
            tokens(U_KVA, xh, xl, 512, bank_free(1))
            tokens(U_KVB, xh, xl, N_KVB, bank_free(2))
            with pe.Fori(0, 2) as c:
                tokens(2 * c + U_V, xh, xl, SG, bank_free(c + 3))

            pe.wait_ge(small_arrived, 160)
            pe.wait_ge(raw_act, 9)
            for c in range(2):
                last = transpose(ps[:, 0, 16 * c:16 * c + 16], pe_in[:, c, :], 16)
            last.then_inc(pe_tr, 1)
            pe.wait_ge(roped, 1)
            for t in range(8):
                if t == 4:
                    pe.wait_ge(tok_k, 4)
                if t == 5:
                    pe.wait_ge(tok_v, 4)
                if t >= 6:
                    pe.wait_ge(op_lo, t - 5)
                for m in range(MT):
                    src = (kva[:, m, P * t:P * t + P] if t < 3 else
                           kvb[:, m, 0:P] if t == 3 else q_perm[:, m, P * (t - 4):P * (t - 4) + P])
                    last = transpose(ps[:, 4 + t % 4, P * m:P * m + P], src)
                last.then_inc(tr_done, 1)

            def merge_piece(u, piece, f):
                half, k = piece // KD, piece % KD
                if piece == 0:
                    pe.wait_ge(w_lo, u + 1)
                if k == 0 and f >= 2:
                    pe.wait_ge(merge_out, f - 1)
                col = slice(P * half, P * half + P)
                last = mm3(ps[:, M0 + half, :], w8(wh, u % 2)[:, k, col], w8(wl, u % 2)[:, k, col],
                           xh[:, k, :], xl[:, k, :], k == 0, k == KD - 1)
                if k == KD - 1:
                    last.then_inc(w_used if half else merge_half, 1)

            pe.wait_ge(op_lo, 6)
            for piece in range(2 * KD):
                merge_piece(U_MERGE0, piece, piece // KD)

            for c, u in enumerate((U_CK, U_CV)):
                pe.wait_ge(w_lo, u + 1)
                pe.wait_ge(flat_ok, c + 1)
                for j in range(16):
                    cols = slice(G * NB * j, G * NB * (j + 1))
                    last = mm3(ps[:, 4 + c, 0:G * NB], w16(wh, u % 2)[:, j, :], w16(wl, u % 2)[:, j, :],
                               flath[:, c, cols], flatl[:, c, cols], j == 0, j == 15)
                last.then_inc(w_used, 1)
            for piece in range(LATE_PIECE):
                merge_piece(U_MERGE, piece, 2 + piece // KD)

            pe.wait_ge(w2_lo, 1)
            pe.wait_ge(hid_lo, 1)
            dup = slice(0, 2 * DH)
            k2h, k2l = [t[:, :, :].rearrange("p a b -> p (a b)")[:, dup] for t in (w2h, w2l)]
            mm3(ps[:, 2, 0:G * NB], k2h, k2l, hidh[:, 0, :], hidl[:, 0, :], True, True).then_inc(cmp_done, 1)
            pe.wait_ge(hid_lo, 2)
            for g in range(G):
                n = slice(NB * g, NB * g + NB)
                last = mm3(ps[0:NB, 3, DH * g:DH * g + DH], hidh[:, 1, n], hidl[:, 1, n], w2h[:, 2, :], w2l[:, 2, :],
                           True, True)
            last.then_inc(cmp_done, 1)
            pe.wait_ge(masks_ready, 4)
            pe.wait_ge(hid_ok, 1)
            for gs in range(4):
                last = transpose(ps[:, 4, P * gs:P * gs + P], wsp[:, gs, :])
            last.then_inc(wt_done, 1)
            for piece in range(LATE_PIECE, 2 * KD):
                merge_piece(U_MERGE, piece, 2 + piece // KD)
            pe.wait_ge(cmp_lo, 2)
            pe.wait_ge(pe_ok, 1)
            for g in range(G):
                r = slice(DH * g, DH * g + DH)
                for m in range(MT):
                    for pp in range(PAIRS):
                        at = NB * (PAIRS * m + pp)
                        tok = slice(P * m, P * m + P)
                        last = mm3(ps[:, g, at:at + NB], q_t(ath)[r, pp, tok], q_t(atl)[r, pp, tok], kch[r, :],
                                   kcl[r, :], True, True)
                last.then_inc(sc_done, 1)
            pe.wait_ge(vl_ok, 1)
            pe.wait_ge(wt_lo, 1)
            pe.wait_ge(cmp_lo, 3)
            for gs in range(4):
                cols = slice(P * gs, P * gs + P)
                mm3(ps[:, 2 + gs, :], wth[:, gs, :], wtl[:, gs, :], oth[:, :, cols], otl[:, :, cols],
                    True, True).then_inc(mix_done, 1)

            piece = 0

            def fill(until):
                nonlocal piece
                while piece < until:
                    merge_piece(U_FILL0 + piece // (2 * KD), piece % (2 * KD), 4 + piece // KD)
                    piece += 1

            fill(FILL_AT[0])
            for i in range(N_STEPS + 3):
                if i >= 3:
                    a = i - 3
                    qt, pp, br = STEPS[a]
                    w = a // 3
                    pe.wait_ge(pt_lo, a + 1)
                    if br == 0 and w >= 2:
                        pe.wait_ge(o_lo, w - 1)
                    out = ps[:, O0 + w % 2, 0:G * P]
                    if br < 2:
                        for kt in range(qt + 1):
                            c = slice(G * P * kt, G * P * (kt + 1))
                            last = mm3(out, v_t(ath, br)[:, kt, :], v_t(atl, br)[:, kt, :], pth[:, c], ptl[:, c],
                                       br == 0 and kt == 0, False)
                    else:
                        last = mm3(out, vch[:, :], vcl[:, :], pth[0:NB, 0:G * P], ptl[0:NB, 0:G * P], False, True)
                    last.then_inc(pv_done, 1)
                if 2 <= i < N_STEPS + 2:
                    a = i - 2
                    qt, pp, br = STEPS[a]
                    if a == 0:
                        pe.wait_ge(sgu_ok, 4)
                        pe.wait_ge(roped, 3)
                    if br < 2:
                        s = SOFT[a]
                        for g in range(G):
                            pe.wait_ge(p_ok[g], s + 1)
                            for kt in range(qt + 1):
                                last = transpose(ps[:, PT0 + kt // 2, G * P * (kt % 2) + P * g:G * P * (kt % 2) + P * g + P],
                                                 prob[:, s % 2, g, P * kt:P * kt + P])
                    else:
                        if a == 2:
                            pe.wait_ge(pcmp_ok, 1)
                        for g in range(G):
                            last = transpose(ps[0:NB, PT0, P * g:P * g + P], pcmp[:, g, qt, pp, :])
                    last.then_inc(pt_done, 1)
                if i in SOFT:
                    qt, pp, br = STEPS[i]
                    if i == 0:
                        pe.wait_ge(sc_max, 1)
                    else:
                        pe.wait_ge(s_exp, 2 * SOFT[i])
                    n = P * (qt + 1)
                    for g in range(G):
                        r = slice(DH * g, DH * g + DH)
                        tok = slice(P * qt, P * qt + P)
                        mm3(ps[:, g, 0:n], q_t(ath)[r, pp, tok], q_t(atl)[r, pp, tok], k_t(ath, br)[r, 0:n],
                            k_t(atl, br)[r, 0:n], True, False)
                        last = pe.matmul(ps[:, g, n - P:n], ident_r[:, :], causal[:, :], start=False, stop=True)
                    last.then_inc(s_done, 1)
                fill(FILL_AT[i + 1])

            for k in range(4):
                if k == 0:
                    pe.wait_ge(o_lo, MT * PAIRS)
                if k == 2:
                    pe.wait_ge(merge_out, 2 * N_MERGE)
                for m in range(MT):
                    last = transpose(ps[:, 4 + k, P * m:P * m + P], u_raw[:, m, P * k:P * k + P])
                last.then_inc(st_done, 1)

            with pe.Fori(0, 2) as c:
                for b, (oh, ol) in enumerate(((oth, otl), (sgh, sgl))):
                    pe.wait_ge(w_lo, 2 * c + U_BRANCH + b + 1)
                    if b:
                        pe.wait_ge(st_lo, 4)
                        pe.wait_ge(br_prod, 8 * c + 1)
                    for f in range(4):
                        for k in range(4):
                            col = slice(P * f, P * f + P)
                            last = mm3(ps[:, 4 * b + f, :], w4(wh, b)[:, k, col], w4(wl, b)[:, k, col], oh[:, k, :],
                                       ol[:, k, :], k == 0, k == 3)
                        if f < 3:
                            last.then_inc(br_done, 1)
                    last.then_inc(w_used, 1)
                pe.wait_ge(br_prod, 8 * c + 4)

            def before(kh, m):
                if m is None:
                    pe.wait_ge(mg_lo, 4 * kh + 4)
            tokens(U_OUT, xh, xl, 512, before)

            def h_transposed(m):
                for h in h_ok:
                    pe.wait_ge(h, m + 1)
                if m >= 2:
                    pe.wait_ge(ht_lo, m - 1)
                for k in range(KD):
                    last = transpose(ps[:, 4 + 2 * (m % 2) + k // 4, P * (k % 4):P * (k % 4) + P],
                                     y[:, m, P * k:P * k + P])
                last.then_inc(ht_done, 1)

            pe.wait_ge(w_lo, U_OUT + 4)
            for m in range(MT):
                pe.wait_ge(mg_lo, KD + m + 1)
                tok = slice(P * m, P * m + P)
                for k in range(KD):
                    last = mm3(ps[:, m, :], xh[:, k, tok], xl[:, k, tok], w4(wh, k // 4)[:, k % 4, :],
                               w4(wl, k // 4)[:, k % 4, :], k == 0, k == KD - 1)
                    if m == MT - 1 and k == 3:
                        last.then_inc(w_used, 1)
                last.then_inc(rows_done if m < MT - 1 else w_used, 1)
                if m == 2:
                    h_transposed(0)
                    h_transposed(1)

            def ffn_tile(b, f, gh, gl, tok=slice(0, SEQ)):
                for k in range(KD):
                    col = slice(P * f, P * f + P)
                    last = mm3(ps[:, 2 * b + f, tok], gh[:, k, col], gl[:, k, col], hth[:, k, tok], htl[:, k, tok],
                               k == 0, k == KD - 1)
                return last

            views = [(first_h[:, :].rearrange("p (k n) -> p k n", k=8), first_l[:, :].rearrange("p (k n) -> p k n", k=8)),
                     (w8(wh, 1), w8(wl, 1))]
            h_transposed_at = {(0, 0): 2, (1, 1): 3}
            pe.wait_ge(ht_lo, 2)
            for half in range(2):
                tok = slice(SEQ // 2 * half, SEQ // 2 * half + SEQ // 2)
                for b, (gh, gl) in enumerate(views):
                    if half == 0:
                        pe.wait_ge(w_lo, U_FFN + b + 1)
                        pe.wait_ge(mg_lo, KD + MT + 2 * b + 2)
                    elif b == 0:
                        pe.wait_ge(ht_lo, MT)
                    for f in range(2):
                        if half == 0 and (b, f) in h_transposed_at:
                            h_transposed(h_transposed_at[b, f])
                        last = ffn_tile(b, f, gh, gl, tok)
                        if half == 1:
                            last.then_inc(w_used if f else ffn_half, 1)
            pe.wait_ge(silu_ok, 2)
            with pe.Fori(1, FT // 2) as i:
                for b in range(2):
                    pe.wait_ge(w_lo, 2 * i + U_FFN + b + 1)
                    for f in range(2):
                        ffn_tile(b, f, w8(wh, b), w8(wl, b)).then_inc(w_used if f else ffn_half, 1)
                pe.wait_ge(silu_ok, 2 * i + 2)

            def down(m, half, f, ring, dh, dl, start, stop):
                tok = slice(P * m, P * m + P)
                c = slice(512 * half, 512 * half + 512)
                return mm3(ps[:, 2 * m + half, :], ah[:, ring, f, tok], al[:, ring, f, tok], dh[:, f, c], dl[:, f, c],
                           start, stop)

            def down_unit(j, slot, start=False):
                pe.wait_ge(w_lo, U_DOWN + 1 + j)
                pe.wait_ge(a_lo, j + 1)
                for m in ((2, 3, 0, 1) if start else range(MT)):
                    if start and m == 0:
                        pe.wait_ge(fact_ok, FT)
                    for f in range(2):
                        for half in range(2):
                            last = down(m, half, f, slot, w2d(wh, slot), w2d(wl, slot), start and f == 0, False)
                last.then_inc(w_used, 1)

            down_unit(0, 0, True)
            down_unit(1, 1)
            with pe.Fori(1, (N_DOWN - 3) // 2) as i:
                for b in range(2):
                    down_unit(2 * i + b, b)
            late = ((0, w2d(wh, 0), w2d(wl, 0)),
                    (2, late_h.rearrange("p (f n) -> p f n", f=2), late_l.rearrange("p (f n) -> p f n", f=2)),
                    (3, w2d(wh, 1), w2d(wl, 1)))
            for m in range(MT):
                for half in range(2):
                    for j, (ring, dh, dl) in enumerate(late):
                        if m == 0 and half == 0:
                            pe.wait_ge(w_lo, U_DOWN + N_DOWN - 2 + j)
                            pe.wait_ge(a_lo, N_DOWN - 2 + j)
                        for f in range(2):
                            last = down(m, half, f, ring, dh, dl, False, j == 2 and f == 1)
                    last.then_inc(rows_out, 1)


_INS = ["x", "positions", "w_in", "pe_ck", "w_ck1", "w_ck2", "pe_cv", "w_cv1", "w_cv2", "ln_sgu_g", "ln_sgu_b",
        "w_spatial", "b_spatial", "w_branch_nsa", "w_branch_sgu", "w_out", "ln1_g", "ln1_b", "w_ffn_gate",
        "w_ffn_up", "w_ffn_down", "ln2_g", "ln2_b"]


def kernel(**inputs):
    import numpy as np
    import concourse.bacc as bacc
    from concourse import mybir
    from concourse.bass_utils import run_bass_kernel_spmd

    nc = bacc.Bacc("TRN2", target_bir_lowering=False, num_devices=1)
    arrays, tensors = {}, {}
    for name in _INS:
        a = np.ascontiguousarray(inputs[name])
        arrays[f"in_{name}"] = a
        tensors[name] = nc.dram_tensor(f"in_{name}", a.shape, mybir.dt.from_np(a.dtype), kind="ExternalInput").ap()
    tensors["out"] = nc.dram_tensor("out", inputs["x"].shape, mybir.dt.float32, kind="ExternalOutput").ap()
    build_layer(nc, tensors)
    result = run_bass_kernel_spmd(nc, [arrays], core_ids=[0])
    return result.results[0]["out"]
```

```python
def build_layer(nc, T):
    import math
    from contextlib import ExitStack

    import numpy as np

    import concourse.bass as bass
    from concourse import mybir

    fp32 = mybir.dt.float32
    f32r = mybir.dt.float32r
    i32 = mybir.dt.int32
    ALU = mybir.AluOpType
    ACT = mybir.ActivationFunctionType
    AX = mybir.AxisListType
    ds = bass.ds

    P = 128
    SEQ, D = T["x"].shape[1:]
    MT = SEQ // P
    KD = D // P
    DH = 64
    G, R = 2, 4
    PAIRS = R
    NCB = 31
    NB = 32
    STRIDE, BLOCK = 16, 32
    SG = 512
    F = T["w_ffn_gate"].shape[2]
    FT = F // P
    HALF = 8
    SCALE = DH ** -0.5
    NEG = -1e30
    ALPHA = 2.0 ** 0.25
    EPS = 1e-5
    GATE_W = 3 * G * R

    C_Q, C_KVA, C_KVB = 0, 512, 1024
    N_KVB = 2 * P + GATE_W
    C_U = C_KVB + N_KVB
    C_V = C_U + SG
    C_MERGE = C_V + SG

    U_Q, U_KVA, U_KVB, U_V, U_U = 0, 2, 4, 6, 8
    U_CK, U_MERGE0, U_CV, U_MERGE1 = 10, 11, 12, 13
    U_FILL0 = 14
    N_MERGE = 2 * D // 256
    U_BRANCH = U_FILL0 + N_MERGE - 2
    U_OUT = U_BRANCH + 4
    U_FFN = U_OUT + 4
    U_DOWN = U_FFN + FT
    N_DOWN = FT // 2

    TILE_ORDER = (0, 1, 3, 2)
    FILL_SHARE = {0: 1.15, 1: 1.0, 2: 0.95, 3: 0.9, -1: 0.8}
    FILL_BRANCH = (2.0, 1.0, 2.7)
    FILL_FIRST = 6
    BIAS_COLS = 704

    x_d = T["x"][0].rearrange("(m p) c -> p m c", p=P)
    out_d = T["out"][0].rearrange("(m p) c -> p m c", p=P)
    w_in_d = T["w_in"][0].rearrange("(k p) n -> p k n", p=P)
    ck1_d = T["w_ck1"][0].rearrange("(j p) h -> p j h", p=P)
    cv1_d = T["w_cv1"][0].rearrange("(j p) h -> p j h", p=P)
    nsa_d = T["w_branch_nsa"][0].rearrange("(g k d) n -> g d k n", g=G, k=PAIRS)
    sgu_d = T["w_branch_sgu"][0].rearrange("(k p) n -> p k n", p=P)
    wout_d = T["w_out"][0].rearrange("(k p) n -> p k n", p=P)
    gate_d = T["w_ffn_gate"][0].rearrange("(k p) n -> p k n", p=P)
    up_d = T["w_ffn_up"][0].rearrange("(k p) n -> p k n", p=P)
    down_d = T["w_ffn_down"][0].rearrange("(f p) n -> p f n", p=P)

    def as_rows(v):
        return v.rearrange("n -> () n").broadcast_to([P, v.shape[0]])

    FREQ = [float(np.float32(500000.0 ** (-j / HALF))) for j in range(HALF)]
    MAGIC = 1.5 * 2.0 ** 23
    PI_1 = 6.28125
    PI_2 = round((2 * math.pi - PI_1) * 2.0 ** 20) / 2.0 ** 20
    PI_3 = 2 * math.pi - PI_1 - PI_2
    PI_IN = 3.1415925

    with ExitStack() as ctx:
        def sb(name, shape, dt, scope=ctx):
            return scope.enter_context(nc.sbuf_tensor(name, shape, dt))

        def sem(name):
            return ctx.enter_context(nc.semaphore(name))

        stage = sb("stage", [P, 2, 2048], fp32)
        wh = sb("wh", [P, 2, 2048], f32r)
        wl = sb("wl", [P, 2, 2048], f32r)
        xh = sb("xh", [P, KD, SEQ], f32r)
        xl = sb("xl", [P, KD, SEQ], f32r)
        ath = sb("ath", [P, 4096], f32r)
        atl = sb("atl", [P, 4096], f32r)
        ident = sb("ident", [P, P], fp32)

        first = ExitStack()
        prob = sb("prob", [P, 2, G, SEQ], fp32, first)
        pcmp = sb("pcmp", [P, G, MT, PAIRS, NB], fp32, first)
        pth = sb("pth", [P, 1024], f32r, first)
        ptl = sb("ptl", [P, 1024], f32r, first)
        arena = sb("arena", [P, 10240], fp32, first)
        oth = sb("oth", [P, PAIRS, SEQ], f32r, first)
        otl = sb("otl", [P, PAIRS, SEQ], f32r, first)
        ln_g = sb("ln_g", [P, SG], fp32, first)
        ln_b = sb("ln_b", [P, SG], fp32, first)
        wsp = sb("wsp", [P, 4, P], fp32, first)
        wth = sb("wth", [P, 4, P], f32r, first)
        wtl = sb("wtl", [P, 4, P], f32r, first)
        bsp = sb("bsp", [P, 4], fp32, first)
        causal = sb("causal", [P, P], f32r, first)
        ident_r = sb("ident_r", [P, P], f32r, first)
        cbias = sb("cbias", [P, MT, NB], fp32, first)
        any_block = sb("any_block", [P, MT], fp32, first)
        pos_i = sb("pos_i", [P, MT], i32, first)
        pos_f = sb("pos_f", [P, MT], fp32, first)
        freq = sb("freq", [P, HALF], fp32, first)
        ang = sb("ang", [P, 2, MT, HALF], fp32, first)
        trig = sb("trig", [P, 2, MT, HALF], fp32, first)
        gates = sb("gates", [P, MT, G, R, 3], fp32, first)
        pe_in = sb("pe_in", [16, 2, P], fp32, first)
        pe_t = sb("pe_t", [P, 2, 16], fp32, first)
        w2 = sb("w2", [P, 3, DH], fp32, first)
        w2h = sb("w2h", [P, 3, DH], f32r, first)
        w2l = sb("w2l", [P, 3, DH], f32r, first)
        hidh = sb("hidh", [P, 2, G * NB], f32r, first)
        hidl = sb("hidl", [P, 2, G * NB], f32r, first)
        vch = sb("vch", [NB, P], f32r, first)
        vcl = sb("vcl", [NB, P], f32r, first)
        nmax = sb("nmax", [P, 2, G], fp32, first)
        rsum = sb("rsum", [P, 2, G], fp32, first)
        rinv = sb("rinv", [P, 2, G], fp32, first)
        vstat = sb("vstat", [P, MT, 6], fp32, first)
        vmv = sb("vmv", [P, MT, 2], fp32, first)
        vrs = sb("vrs", [P, 4, MT], fp32, first)
        first.close()

        second = ExitStack()
        hid_sg = sb("hid_sg", [P, 2, SEQ], fp32, second)
        y = sb("y", [P, MT, D], fp32, second)
        lng = sb("lng", [P, 2, D], fp32, second)
        lnb = sb("lnb", [P, 2, D], fp32, second)
        stat = sb("stat", [P, MT, 2, 6], fp32, second)
        mv = sb("mv", [P, MT, 2], fp32, second)
        nrm = sb("nrm", [P, MT, 5], fp32, second)
        early = ExitStack()
        sb("fact_before", [P, FT - 8, SEQ], fp32, early)
        first_h = sb("first_h", [P, 2048], f32r, early)
        first_l = sb("first_l", [P, 2048], f32r, early)
        early.close()
        fact = sb("fact", [P, FT, SEQ], fp32, second)
        second.close()

        raw = arena[:, :].rearrange("p (c m n) -> p c m n", c=5, m=MT)
        q_raw, kva, v_raw, u_raw = raw[:, 0], raw[:, 1], raw[:, 2], raw[:, 4]
        kvb = arena[:, 6144:6144 + MT * N_KVB].rearrange("p (m n) -> p m n", m=MT)
        kvb_end = 6144 + MT * N_KVB
        hid = arena[0:G * NB, kvb_end:kvb_end + 256].rearrange("p (c h) -> p c h", c=2)
        cmax = arena[:, kvb_end + 256:kvb_end + 288]
        csum_f = arena[:, kvb_end + 288:kvb_end + 320]
        csum = csum_f.rearrange("p (g m k) -> p g m k", g=G, m=MT)
        x_sb = arena[:, 4096:8192].rearrange("p (m c) -> p m c", m=MT)
        merge = arena[:, 0:16 * SEQ].rearrange("p (f t) -> p f t", f=16)
        q_perm = prob[:, :, :, :].rearrange("p a b c -> p (a b c)").rearrange("p (m n) -> p m n", m=MT)
        q_view = q_perm.rearrange("p m (k g d) -> p m g k d", k=PAIRS, g=G)
        pc_flat = pcmp[:, :, :, :, :].rearrange("p a b c d -> p (a b c d)")
        turns, tmp_b = [pc_flat[:, P + 64 * i:P + 64 * i + 64].rearrange("p (a m j) -> p a m j", a=2, m=MT)
                        for i in range(2)]
        rope_t = pc_flat.rearrange("p (t m h j) -> p t m h j", t=4, m=MT, h=8)
        tok2 = pc_flat.rearrange("p (c g t) -> p c g t", c=2, g=G)
        flat = prob[:, :, :, :].rearrange("p a b c -> p a (b c)").rearrange(
            "p c (j g n) -> p c j g n", j=16, g=G)
        sct = pc_flat.rearrange("p (g t) -> p g t", g=G)
        kz = [t[:, 0:PAIRS * P].rearrange("p (k n) -> p k n", k=PAIRS) for t in (pth, ptl)]
        kz_diag = [t[:, 0:PAIRS * (P + NB)].rearrange("p (k n) -> p k n", k=PAIRS)[:, :, 0:NB] for t in (pth, ptl)]
        flath = oth[:, :, :].rearrange("p a b -> p (a b)").rearrange("p (c e) -> p c e", c=2)
        flatl = otl[:, :, :].rearrange("p a b -> p (a b)").rearrange("p (c e) -> p c e", c=2)

        def att(t, off, n):
            return t[:, off:off + n]

        def q_t(t):
            return att(t, 0, 2048).rearrange("p (k s) -> p k s", k=PAIRS)

        def k_t(t, br):
            return att(t, 2048 + 512 * br, 512)

        def v_t(t, br):
            return att(t, 3072 + 512 * br, 512).rearrange("p (m n) -> p m n", m=MT)

        sgh = att(ath, 0, 2048).rearrange("p (k s) -> p k s", k=4)
        sgl = att(atl, 0, 2048).rearrange("p (k s) -> p k s", k=4)
        hth = ath[:, :].rearrange("p (k s) -> p k s", k=KD)
        htl = atl[:, :].rearrange("p (k s) -> p k s", k=KD)
        late_h, late_l = ath[:, 0:2048], atl[:, 0:2048]
        ah = xh[:, :, :].rearrange("p (r f) s -> p r f s", f=2)
        al = xl[:, :, :].rearrange("p (r f) s -> p r f s", f=2)

        ps = ctx.enter_context(nc.psum_tensor("ps", [P, 8, 512], fp32))
        PT0, O0, M0 = 2, 4, 6

        def w4(t, slot, n=512):
            return t[:, slot, 0:4 * n].rearrange("p (k n) -> p k n", k=4)

        def w8(t, slot):
            return t[:, slot, :].rearrange("p (k n) -> p k n", k=8)

        def w2d(t, slot):
            return t[:, slot, :].rearrange("p (f n) -> p f n", f=2)

        def w16(t, slot):
            return t[:, slot, :].rearrange("p (j h) -> p j h", j=16)

        w_arrived = [sem("w_arrived0"), sem("w_arrived1")]
        w_hi, w_lo, w_used = sem("w_hi"), sem("w_lo"), sem("w_used")
        quarter_hi, quarter_lo = sem("quarter_hi"), sem("quarter_lo")
        x_arrived = [sem(f"x_arrived{k}") for k in range(KD)]
        q_arrived = [sem(f"q_arrived{k}") for k in range(KD)]
        ident_ready = sem("ident_ready")
        small_arrived = sem("small_arrived")
        xt_done, xt_hi, xt_lo = sem("xt_done"), sem("xt_hi"), sem("xt_lo")
        rows_done = sem("rows_done")
        raw_act, raw_dve = sem("raw_act"), sem("raw_dve")
        pool_step, dve_step = sem("pool_step"), sem("dve_step")
        masks_ready, ang_ready, trig_ready = sem("masks_ready"), sem("ang_ready"), sem("trig_ready")
        roped = sem("roped")
        tr_done = sem("tr_done")
        tok_k, tok_v = sem("tok_k"), sem("tok_v")
        op_hi, op_lo = sem("op_hi"), sem("op_lo")
        pe_tr, pe_ok = sem("pe_tr"), sem("pe_ok")
        flat_ok = sem("flat_ok")
        w2_hi, w2_lo = sem("w2_hi"), sem("w2_lo")
        hid_ok, hid_tr, hid_hi, hid_lo = sem("hid_ok"), sem("hid_tr"), sem("hid_hi"), sem("hid_lo")
        kz_zero, sct_done = sem("kz_zero"), sem("sct_done")
        sct_out = [sem("sct_out0"), sem("sct_out1")]
        cmp_done, cmp_hi, cmp_lo = sem("cmp_done"), sem("cmp_hi"), sem("cmp_lo")
        sc_done, sc_max, sc_exp, pcmp_ok = sem("sc_done"), sem("sc_max"), sem("sc_exp"), sem("pcmp_ok")
        gates_ok = sem("gates_ok")
        gelu_ok, vsq_in, vsq_ok, vln_ok = sem("gelu_ok"), sem("vsq_in"), sem("vsq_ok"), sem("vln_ok")
        vh_ok, vl_ok = sem("vh_ok"), sem("vl_ok")
        wt_done, wt_hi, wt_lo = sem("wt_done"), sem("wt_hi"), sem("wt_lo")
        mix_done, sgu_ok = sem("mix_done"), sem("sgu_ok")
        merge_half = sem("merge_half")
        merge_out = sem("merge_out")
        s_done, s_max, s_exp, rinv_ok = sem("s_done"), sem("s_max"), sem("s_exp"), sem("rinv_ok")
        p_ok = [sem("p_ok0"), sem("p_ok1")]
        pt_done, pt_hi, pt_lo = sem("pt_done"), sem("pt_hi"), sem("pt_lo")
        pv_done, o_hi, o_lo = sem("pv_done"), sem("o_hi"), sem("o_lo")
        st_done, st_hi, st_lo = sem("st_done"), sem("st_hi"), sem("st_lo")
        sig_ok = sem("sig_ok")
        br_done, br_prod = sem("br_done"), sem("br_prod")
        mg_ok, mg_hi, mg_lo = sem("mg_ok"), sem("mg_hi"), sem("mg_lo")
        x2_arrived, ln_arrived = sem("x2_arrived"), sem("ln_arrived")
        var_ok, sq_ok, centred, scaled = sem("var_ok"), sem("sq_ok"), sem("centred"), sem("scaled")
        h_ok = [sem("h_ok0"), sem("h_ok1")]
        ht_done, ht_hi, ht_lo = sem("ht_done"), sem("ht_hi"), sem("ht_lo")
        ffn_half, silu_ok, fact_ok = sem("ffn_half"), sem("silu_ok"), sem("fact_ok")
        a_hi, a_lo = sem("a_hi"), sem("a_lo")
        rows_out = sem("rows_out")
        stored = sem("stored")

        block = ctx.enter_context(nc.Block())

        STEPS = [(qt, pp, br) for qt in TILE_ORDER for pp in range(PAIRS) for br in range(3)]
        N_STEPS = len(STEPS)
        SOFT_STEPS = [a for a in range(N_STEPS) if STEPS[a][2] < 2]
        SOFT = {a: s for s, a in enumerate(SOFT_STEPS)}
        PT_BANKS = [1 if br == 2 else (qt + 2) // 2 for qt, pp, br in STEPS]
        PT_BEFORE = [sum(PT_BANKS[:a]) for a in range(N_STEPS + 1)]
        N_FILL = N_MERGE - 2
        PIECES = N_FILL * 2 * KD
        share = [FILL_SHARE[STEPS[i][0] if i < N_STEPS else -1] * FILL_BRANCH[i % 3] for i in range(N_STEPS + 3)]
        FILL_AT = [FILL_FIRST + round((PIECES - FILL_FIRST) * sum(share[:i]) / sum(share)) for i in range(N_STEPS + 4)]

        def fills_done(i):
            return FILL_AT[i] // KD

        QUARTERS = [[] for _ in range(N_STEPS + 3)]
        for v in range(N_FILL):
            end = next(i for i in range(N_STEPS + 3) if fills_done(i + 1) >= 2 * v + 2)
            for quarter in range(4):
                at = end - end % 3 + 2 + 3 * (quarter // 2)
                QUARTERS[min(at, N_STEPS + 2)].append((U_FILL0 + v + 2, quarter))

        class Steps:

            def __init__(self, eng, s):
                self.eng, self.s, self.n = eng, s, 0

            def __call__(self, ins):
                ins.then_inc(self.s, 1)
                self.n = self.n + 1
                self.eng.wait_ge(self.s, self.n)

        @block.sync
        def _(sp):
            def load(u, slot, parts):
                sp.wait_ge(w_lo, u - 1)
                for dst, src in parts:
                    sp.dma_start(dst, src).then_inc(w_arrived[slot], 16)

            def rows4(d, slot, kh, col, n):
                s = w4(stage, slot, n)
                return [(s[:, 2 * i:2 * i + 2, :], d[:, 4 * kh + 2 * i:4 * kh + 2 * i + 2, ds(col, n)])
                        for i in range(2)]

            def rows8(d, slot, col):
                s = w8(stage, slot)
                return [(s[:, 4 * i:4 * i + 4, :], d[:, 4 * i:4 * i + 4, ds(col, 256)]) for i in range(2)]

            for k in range(KD):
                sp.dma_start(x_sb[:, :, P * k:P * k + P], x_d[:, :, P * k:P * k + P]).then_inc(x_arrived[k], 16)
                sp.dma_start(w4(stage, k // 4)[:, k % 4, :], w_in_d[:, k, C_Q:C_Q + 512]).then_inc(q_arrived[k], 16)
            smalls = [(pos_i[:, :], T["positions"][0].rearrange("(m p) -> p m", p=P)),
                      (pe_in[:, 0, :], T["pe_ck"][0].rearrange("(j a) d -> j (a d)", a=2)),
                      (pe_in[:, 1, :], T["pe_cv"][0].rearrange("(j a) d -> j (a d)", a=2)),
                      (w2[:, 0, :], T["w_ck2"][0]), (w2[:, 1, :], T["w_ck2"][0]), (w2[:, 2, :], T["w_cv2"][0]),
                      (ln_g[:, :], as_rows(T["ln_sgu_g"][0])), (ln_b[:, :], as_rows(T["ln_sgu_b"][0])),
                      (wsp[:, :, :], T["w_spatial"][0].rearrange("g t s -> t g s")),
                      (bsp[:, :], T["b_spatial"][0].rearrange("g t -> t g"))]
            for dst, src in smalls:
                sp.dma_start(dst, src, allow_slow_non_contiguous=True).then_inc(small_arrived, 16)
            for kh in range(2):
                load(U_KVA + kh, kh, rows4(w_in_d, kh, kh, C_KVA, 512))
            for kh in range(2):
                load(U_KVB + kh, kh, rows4(w_in_d, kh, kh, C_KVB, N_KVB))
            for u, col in ((U_V, C_V), (U_U, C_U)):
                for kh in range(2):
                    load(u + kh, kh, rows4(w_in_d, kh, kh, col, SG))
            def rows16(d, slot):
                s = w16(stage, slot)
                return [(s[:, 8 * i:8 * i + 8, :], d[:, 8 * i:8 * i + 8, :]) for i in range(2)]

            load(U_CK, 0, rows16(ck1_d, 0))
            load(U_MERGE0, 1, rows8(w_in_d, 1, C_MERGE))
            load(U_CV, 0, rows16(cv1_d, 0))
            load(U_MERGE1, 1, rows8(w_in_d, 1, C_MERGE + 256))
            with sp.Fori(0, (N_MERGE - 2) // 2) as i:
                for b in range(2):
                    load(2 * i + U_FILL0 + b, b, rows8(w_in_d, b, 512 * i + C_MERGE + 256 * (2 + b)))
            with sp.Fori(0, 2) as c:
                s = w4(stage, 0)
                load(2 * c + U_BRANCH, 0,
                     [(s[DH * g:DH * g + DH, :, :], nsa_d[g][:, :, ds(512 * c, 512)]) for g in range(G)])
                load(2 * c + U_BRANCH + 1, 1, rows4(sgu_d, 1, 0, 512 * c, 512))
            sp.wait_ge(o_lo, MT * PAIRS)
            sp.dma_start(y[:, :, :], x_d).then_inc(x2_arrived, 16)
            with sp.Fori(0, 2) as c:
                for kh in range(2):
                    load(2 * c + U_OUT + kh, kh, rows4(wout_d, kh, kh, 512 * c, 512))
            sp.wait_ge(mg_lo, KD)
            for i, (g_, b_) in enumerate((("ln1_g", "ln1_b"), ("ln2_g", "ln2_b"))):
                sp.dma_start(lng[:, i, :], as_rows(T[g_][0])).then_inc(ln_arrived, 16)
                sp.dma_start(lnb[:, i, :], as_rows(T[b_][0])).then_inc(ln_arrived, 16)
            with sp.Fori(0, FT // 2) as i:
                load(2 * i + U_FFN, 0, rows8(gate_d, 0, 256 * i))
                load(2 * i + U_FFN + 1, 1, rows8(up_d, 1, 256 * i))

            def down(j, slot):
                s = w2d(stage, slot)
                load(U_DOWN + j, slot, [(s[:, f:f + 1, :], down_d[:, ds(2 * j + f, 1), :]) for f in range(2)])

            with sp.Fori(0, N_DOWN // 2) as i:
                for b in range(2):
                    down(2 * i + b, b)
            if N_DOWN % 2:
                down(N_DOWN - 1, (N_DOWN - 1) % 2)
            for m in range(MT):
                for h in h_ok:
                    sp.wait_ge(h, MT + m + 1)
                sp.dma_start(out_d[:, m, :], y[:, m, :]).then_inc(stored, 16)
            sp.wait_ge(stored, 16 * MT)

        @block.gpsimd
        def _(pool):
            step = Steps(pool, pool_step)
            step(pool.memset(ident[:, :], 0.0))
            pool.affine_select(out=ident[:, :], in_=ident[:, :], compare_op=ALU.not_equal, fill=1.0, base=0,
                               pattern=[[-1, P]], channel_multiplier=1).then_inc(ident_ready, 1)
            pool.wait_ge(ident_ready, 1)
            step(pool.tensor_copy(ident_r[:, :], ident[:, :]))
            step(pool.memset(pc_flat[:, 0:P], 0.0))
            step(pool.memset(cbias[:, :, :], 0.0))
            step(pool.memset(any_block[:, :], 1.0))
            step(pool.affine_select(out=pc_flat[:, 0:P], in_=pc_flat[:, 0:P], compare_op=ALU.is_ge, fill=NEG, base=0,
                                    pattern=[[-1, P]], channel_multiplier=1))
            pool.tensor_copy(causal[:, :], pc_flat[:, 0:P]).then_inc(masks_ready, 1)
            pool.affine_select(out=cbias[:, :, :], in_=cbias[:, :, :], compare_op=ALU.is_ge, fill=NEG,
                               base=-(BLOCK - 1), pattern=[[P, MT], [-STRIDE, NB]],
                               channel_multiplier=1).then_inc(masks_ready, 1)
            pool.affine_select(out=any_block[:, :], in_=any_block[:, :], compare_op=ALU.is_ge, fill=0.0,
                               base=-(BLOCK - 1), pattern=[[P, MT]], channel_multiplier=1).then_inc(masks_ready, 1)
            step(pool.memset(prob[:, 0, 0, :], 0.0))
            for t in (pth, ptl):
                pool.tensor_copy(t[:, 0:PAIRS * P], prob[:, 0, 0, :]).then_inc(kz_zero, 1)
            for j in range(HALF):
                step(pool.memset(freq[:, j:j + 1], FREQ[j]))
            pool.wait_ge(small_arrived, 160)
            step(pool.tensor_copy(pos_f[:, :], pos_i[:, :]))
            for i in range(2):
                for m in range(MT):
                    step(pool.tensor_scalar(ang[:, i, m, :], freq[:, :], pos_f[:, m:m + 1], None, ALU.mult))
                step(pool.tensor_scalar(turns[:, i], ang[:, i], 1.0 / (2 * math.pi), 0.25 * i, ALU.mult, ALU.add))
            step(pool.tensor_scalar(turns[:, :], turns[:, :], MAGIC, None, ALU.add))
            step(pool.tensor_scalar(turns[:, :], turns[:, :], -MAGIC, None, ALU.add))
            for part in (PI_1, PI_2, PI_3):
                step(pool.tensor_scalar(tmp_b[:, :], turns[:, :], -part, None, ALU.mult))
                step(pool.tensor_tensor(ang[:, :], ang[:, :], tmp_b[:, :], ALU.add))
            step(pool.tensor_scalar(ang[:, 1], ang[:, 1], math.pi / 2, None, ALU.add))
            pool.tensor_scalar(ang[:, :], ang[:, :], PI_IN, -PI_IN, ALU.min, ALU.max).then_inc(ang_ready, 1)
            pool.affine_select(out=wsp[:, :, :], in_=wsp[:, :, :], compare_op=ALU.is_ge, fill=0.0, base=0,
                               pattern=[[0, 4], [-1, P]], channel_multiplier=1).then_inc(masks_ready, 1)

            pool.wait_ge(trig_ready, 1)

            def rotate(src, dst, heads):
                t = [rope_t[:, i, :, 0:heads, :] for i in range(4)]
                x1, x2 = src[..., 0:HALF], src[..., HALF:2 * HALF]
                sn, cs = [trig[:, i, :, :].rearrange("p m (h j) -> p m h j", h=1).broadcast_to([P, MT, heads, HALF])
                          for i in range(2)]
                pool.tensor_tensor(t[0], x1, cs, ALU.mult).then_inc(pool_step, 1)
                pool.tensor_tensor(t[1], x2, sn, ALU.mult).then_inc(pool_step, 1)
                pool.tensor_tensor(t[2], x2, cs, ALU.mult).then_inc(pool_step, 1)
                pool.tensor_tensor(t[3], x1, sn, ALU.mult).then_inc(pool_step, 1)
                step.n += 4
                pool.wait_ge(pool_step, step.n)
                return t

            pool.wait_ge(raw_act, 4)
            pool.wait_ge(raw_dve, 4)
            for col in (0, 2 * P):
                k = kva[:, :, col:col + P].rearrange("p m (g d) -> p m g d", g=G)
                t = rotate(k, k, G)
                step(pool.tensor_tensor(k[..., 0:HALF], t[0], t[1], ALU.subtract))
                step(pool.tensor_tensor(k[..., HALF:2 * HALF], t[2], t[3], ALU.add))
            for m in range(MT):
                step(pool.tensor_copy(q_view[:, m], q_raw[:, m, :].rearrange("p (g k d) -> p g k d", g=G, k=PAIRS)))
            q_heads = q_raw[:, :, :].rearrange("p m (h d) -> p m h d", h=G * R)
            t = rotate(q_heads, None, G * R)
            for m in range(MT):
                tv = [t_[:, m].rearrange("p (g k) j -> p g k j", g=G) for t_ in t]
                step(pool.tensor_tensor(q_view[:, m][..., 0:HALF], tv[0], tv[1], ALU.subtract))
                step(pool.tensor_tensor(q_view[:, m][..., HALF:2 * HALF], tv[2], tv[3], ALU.add))
            pool.wait_ge(raw_act, 6)
            pool.wait_ge(raw_dve, 6)
            k = kvb[:, :, 0:P].rearrange("p m (g d) -> p m g d", g=G)
            t = rotate(k, k, G)
            step(pool.tensor_tensor(k[..., 0:HALF], t[0], t[1], ALU.subtract))
            pool.tensor_tensor(k[..., HALF:2 * HALF], t[2], t[3], ALU.add).then_inc(roped, 1)
            for br, v in ((0, kva[:, :, 3 * P:4 * P]), (1, kvb[:, :, P:2 * P])):
                step(pool.tensor_copy(v_t(ath, br), v))
                pool.tensor_tensor(v_t(atl, br), v, v_t(ath, br).bitcast(fp32), ALU.subtract).then_inc(roped, 1)
            pool.wait_ge(pe_ok, 1)
            pool.wait_ge(tr_done, 8)
            for c, tok in ((0, tok_k), (1, tok_v)):
                step(pool.memset(flat[:, c, :, :, NCB:NB], 0.0))
                pool.wait_ge(tok, 4)
                for g in range(G):
                    src = tok2[:, c, g, :].rearrange("p (n j) -> p j n", j=8)
                    for jh in range(2):
                        step(pool.tensor_tensor(
                            flat[:, c, 8 * jh:8 * jh + 8, g, 0:NCB], src[:, :, jh:jh + NCB],
                            pe_t[:, c, 8 * jh:8 * jh + 8].rearrange("p (j n) -> p j n", n=1).broadcast_to([P, 8, NCB]),
                            ALU.add))
                src = flat[:, c].rearrange("p j g n -> p (j g n)")
                step(pool.tensor_copy(flath[:, c, :], src))
                pool.tensor_tensor(flatl[:, c, :], src, flath[:, c, :].bitcast(fp32),
                                   ALU.subtract).then_inc(flat_ok, 1)
            for a, i in enumerate(SOFT_STEPS):
                n = P * (STEPS[i][0] + 1)
                pool.wait_ge(rinv_ok, a + 1)
                pool.tensor_scalar(prob[:, a % 2, 1, 0:n], prob[:, a % 2, 1, 0:n], rinv[:, a % 2, 1:2], None,
                                   ALU.mult).then_inc(p_ok[1], 1)
            for k in range(2 * MT):
                ln, m = divmod(k, MT)
                pool.wait_ge(scaled, k + 1)
                pool.tensor_tensor(y[:, m, BIAS_COLS:D], y[:, m, BIAS_COLS:D], lnb[:, ln, BIAS_COLS:D],
                                   ALU.add).then_inc(h_ok[1], 1)

        @block.scalar
        def _(act):
            def split(u, slot, n=2048):
                act.wait_ge(w_arrived[slot], 16 * (u - slot))
                act.wait_ge(w_used, u - 1)
                act.copy(wh[:, slot, 0:n], stage[:, slot, 0:n]).then_inc(w_hi, 1)

            def hi(dst, src):
                return act.copy(dst, src)

            for k in range(KD):
                act.wait_ge(xt_done, k + 1)
                hi(xh[:, k, :], ps[:, 4 + k % 4, :]).then_inc(xt_hi, 1)
                act.wait_ge(q_arrived[k], 16)
                hi(w4(wh, k // 4)[:, k % 4, :], w4(stage, k // 4)[:, k % 4, :]).then_inc(
                    quarter_hi if k % 4 < 3 else w_hi, 1)

            def chunk(u, c, dst, n, n_next=2048, both=True):
                split(u + 2, 0, n_next)
                for m in (0, 2):
                    act.wait_ge(rows_done, 3 * c + m + 1)
                    act.copy(dst[:, m, :], ps[:, m, 0:n]).then_inc(raw_act, 1)
                if both:
                    split(u + 3, 1, n_next)

            chunk(U_Q, 0, q_raw, 512)
            act.wait_ge(ang_ready, 1)
            act.activation(trig[:, :, :, :], ang[:, :, :, :], ACT.Sin).then_inc(trig_ready, 1)
            chunk(U_KVA, 1, kva, 512, 4 * N_KVB)
            chunk(U_KVB, 2, kvb, N_KVB)
            act.wait_ge(pe_tr, 1)
            act.copy(pe_t[:, :, :], ps[:, 7, 0:32].rearrange("p (c j) -> p c j", c=2)).then_inc(pe_ok, 1)
            chunk(U_V, 3, v_raw, SG, both=False)
            act.wait_ge(tr_done, 1)
            for g in range(G):
                for par in range(2):
                    act.copy(tok2[DH * par:DH * par + DH, 0, g, :],
                             ps[DH * g:DH * g + DH, 4, par:SEQ:2]).then_inc(tok_k, 1)
            for t in range(2, 8):
                act.wait_ge(tr_done, t + 1)
                if t < 4:
                    hi(k_t(ath, t - 2), ps[:, 4 + t % 4, :]).then_inc(op_hi, 1)
                else:
                    act.mul(q_t(ath)[:, t - 4, :], ps[:, t - 4, :], SCALE).then_inc(op_hi, 1)
            split(U_U + 1, 1)
            act.wait_ge(small_arrived, 160)
            hi(w2h[:, :, :], w2[:, :, :]).then_inc(w2_hi, 1)
            act.wait_ge(raw_dve, 8)
            act.wait_ge(raw_act, 8)
            act.activation(gates[:, :, :, :, :].rearrange("p m g r b -> p m (g r b)"),
                           kvb[:, :, 2 * P:2 * P + GATE_W], ACT.Sigmoid).then_inc(gates_ok, 1)
            act.activation(v_raw, v_raw, ACT.Gelu_apprx_tanh).then_inc(gelu_ok, 1)
            act.wait_ge(vsq_in, 1)
            act.activation(vrs[:, 1, :], vrs[:, 0, :], ACT.Sqrt).then_inc(vsq_ok, 1)
            chunk(U_U, 4, u_raw, SG)
            act.wait_ge(raw_dve, 10)
            act.wait_ge(raw_act, 10)
            act.activation(u_raw, u_raw, ACT.Gelu_apprx_tanh).then_inc(gelu_ok, 1)

            def take_merge(f, u, second):
                if second:
                    act.wait_ge(w_used, u + 1)
                else:
                    act.wait_ge(merge_half, f // 2 + 1)
                act.copy(merge[:, f, :], ps[:, M0 + f % 2, :]).then_inc(merge_out, 1)

            def hidden(c, u):
                act.wait_ge(w_used, u + 1)
                act.activation(hid[:, c, :], ps[0:G * NB, 4 + c, 0:P], ACT.Silu).then_inc(hid_ok, 1)

            def hidden_hi(c):
                act.wait_ge(hid_tr, c + 1)
                hi(hidh[:, c, :], ps[:, 2 + c, 256:256 + G * NB]).then_inc(hid_hi, 1)

            hidden(0, U_CK)
            split(U_CV, 0)
            act.wait_ge(wt_done, 1)
            hi(wth[:, :, :].rearrange("p g t -> p (g t)"), ps[:, 5, :]).then_inc(wt_hi, 1)
            hidden_hi(0)
            act.wait_ge(kz_zero, 2)
            act.wait_ge(cmp_done, 1)
            for g in range(G):
                r = slice(DH * g, DH * g + DH)
                hi(kz_diag[0][r], ps[r, 2, NB * g:NB * g + NB].rearrange("p (k n) -> p k n", k=1).broadcast_to(
                    [DH, PAIRS, NB])).then_inc(cmp_hi, 1)
            take_merge(0, U_MERGE0, False)
            split(U_MERGE1, 1)
            take_merge(1, U_MERGE0, True)
            hidden(1, U_CV)
            act.wait_ge(vln_ok, MT)
            hi(oth[:, :, :], v_raw).then_inc(vh_ok, 1)
            act.wait_ge(sct_done, 1)
            act.copy(sct[:, 0, :], ps[:, 0, :]).then_inc(sct_out[0], 1)
            split(U_FILL0, 0)
            hidden_hi(1)
            act.wait_ge(cmp_done, 2)
            hi(vch[:, :], ps[0:NB, 3, 0:P]).then_inc(cmp_hi, 1)
            take_merge(2, U_MERGE1, False)
            split(U_FILL0 + 1, 1)
            take_merge(3, U_MERGE1, True)
            act.wait_ge(sc_max, 1)
            act.activation(pc_flat, pc_flat, ACT.Exp).then_inc(sc_exp, 1)

            def take_o(w):
                qt, pp, _ = STEPS[3 * w]
                act.wait_ge(pv_done, 3 * w + 3)
                for g in range(G):
                    hi(oth[DH * g:DH * g + DH, pp, P * qt:P * qt + P],
                       ps[DH * g:DH * g + DH, O0 + w % 2, P * g:P * g + P]).then_inc(o_hi, 1)

            f_out = 0
            act.wait_ge(mix_done, 4)
            for i in range(N_STEPS + 3):
                if 2 <= i < N_STEPS + 2:
                    a = i - 2
                    n = G * P * (STEPS[a][0] + 1) if STEPS[a][2] < 2 else G * P
                    rows = P if STEPS[a][2] < 2 else NB
                    if a >= 1:
                        act.wait_ge(pv_done, a)
                    for b in range(PT_BANKS[a]):
                        act.wait_ge(pt_done, PT_BEFORE[a] + b + 1)
                        w = min(512, n - 512 * b)
                        hi(pth[0:rows, 512 * b:512 * b + w], ps[0:rows, PT0 + b, 0:w]).then_inc(pt_hi, 1)
                if i in SOFT:
                    a = SOFT[i]
                    if a >= 2:
                        act.wait_ge(pt_done, PT_BEFORE[SOFT_STEPS[a - 2] + 1])
                    n = P * (STEPS[i][0] + 1)
                    for g in range(G):
                        act.wait_ge(s_max, 2 * a + g + 1)
                        act.activation(prob[:, a % 2, g, 0:n], ps[:, g, 0:n], ACT.Exp, bias=nmax[:, a % 2, g:g + 1],
                                       accum_out=rsum[:, a % 2, g:g + 1]).then_inc(s_exp, 1)
                if i >= 5 and i % 3 == 2:
                    take_o((i - 5) // 3)
                while f_out < fills_done(i + 1):
                    u = U_FILL0 + f_out // 2
                    take_merge(4 + f_out, u, f_out % 2 == 1)
                    f_out += 1
                for u, quarter in QUARTERS[i]:
                    if quarter == 0:
                        act.wait_ge(w_arrived[u % 2], 32 * (u // 2))
                        act.wait_ge(w_used, u - 1)
                    part = slice(512 * quarter, 512 * quarter + 512)
                    last = act.copy(wh[:, u % 2, part], stage[:, u % 2, part])
                    last.then_inc(quarter_hi if quarter < 3 else w_hi, 1)

            for k in range(4):
                act.wait_ge(st_done, k + 1)
                hi(sgh[:, k, :], ps[:, 4 + k, :]).then_inc(st_hi, 1)
            act.wait_ge(merge_out, 16)
            for f in (0, 8, 4, 12):
                act.activation(merge[:, f:f + 4, :], merge[:, f:f + 4, :], ACT.Sigmoid).then_inc(sig_ok, 1)
            with act.Fori(0, 2) as c:
                split(2 * c + U_BRANCH + 2, 0)
                for f in range(4):
                    act.wait_ge(mg_ok, 4 * c + f + 1)
                    act.copy(xh[:, ds(4 * c + f, 1), :], merge[:, ds(4 * c + f, 1), :]).then_inc(mg_hi, 1)
                split(2 * c + U_BRANCH + 3, 1)
            def split_to(dst, u, slot, used):
                act.wait_ge(w_arrived[slot], 32 * (u // 2))
                act.wait_ge(w_used, used)
                act.copy(dst, stage[:, slot, :]).then_inc(w_hi, 1)

            split(U_OUT + 2, 0)
            split(U_OUT + 3, 1)
            split_to(first_h[:, :], U_FFN, 0, U_BRANCH)

            def root(k):
                m = k % MT
                act.wait_ge(var_ok, k + 1)
                act.activation(nrm[:, m, 1:2], nrm[:, m, 0:1], ACT.Sqrt).then_inc(sq_ok, 1)
                act.activation(y[:, m, :], y[:, m, :], ACT.Identity, bias=nrm[:, m, 4:5]).then_inc(centred, 1)

            def ht_hi_of(m):
                act.wait_ge(ht_done, m + 1)
                hi(hth[:, :, P * m:P * m + P],
                   ps[:, 4 + 2 * (m % 2):6 + 2 * (m % 2), :].rearrange("p b (k t) -> p (b k) t", k=4)).then_inc(ht_hi, 1)

            root(0)
            root(1)
            ht_hi_of(0)
            root(2)
            ht_hi_of(1)
            split(U_FFN + 1, 1)
            root(3)
            ht_hi_of(2)
            ht_hi_of(3)

            def ffn(i):
                u = 2 * i + U_FFN
                for f in range(2):
                    if f == 0:
                        act.wait_ge(ffn_half, 2 * i + 1)
                    else:
                        act.wait_ge(w_used, u + 1)
                    act.activation(hid_sg[:, f, :], ps[:, f, :], ACT.Silu).then_inc(silu_ok, 1)
                split(u + 2, 0)
                split(u + 3, 1)
                act.wait_ge(fact_ok, 2 * i + 2)

            def tiles_hi(j, slot):
                act.copy(ah[:, slot, :, :], fact[:, ds(2 * j, 2), :]).then_inc(a_hi, 1)

            with act.Fori(0, FT // 2 - 1) as i:
                ffn(i)
            tiles_hi(0, 0)
            tiles_hi(1, 1)
            ffn(FT // 2 - 1)
            with act.Fori(0, (N_DOWN - 5) // 2) as i:
                for b in range(2):
                    split(2 * i + U_DOWN + b + 2, b)
                    tiles_hi(2 * i + b + 2, b)
            split(U_DOWN + N_DOWN - 3, 0)
            tiles_hi(N_DOWN - 3, 0)
            split_to(late_h, U_DOWN + N_DOWN - 2, 1, U_DOWN)
            tiles_hi(N_DOWN - 2, 2)
            tiles_hi(N_DOWN - 1, 3)
            split_to(wh[:, 1, :], U_DOWN + N_DOWN - 1, 0, U_DOWN + N_DOWN - 3)
            for m in range(MT):
                root(MT + m)

        @block.vector
        def _(dve):
            step = Steps(dve, dve_step)

            def split(u, slot, n=2048):
                dve.wait_ge(w_hi, u + 1)
                dve.tensor_tensor(wl[:, slot, 0:n], stage[:, slot, 0:n], wh[:, slot, 0:n].bitcast(fp32),
                                  ALU.subtract).then_inc(w_lo, 1)

            def lo(dst, src, h):
                return dve.tensor_tensor(dst, src, h.bitcast(fp32), ALU.subtract)

            for k in range(KD):
                dve.wait_ge(xt_hi, k + 1)
                lo(xl[:, k, :], ps[:, 4 + k % 4, :], xh[:, k, :]).then_inc(xt_lo, 1)
                if k % 4 < 3:
                    dve.wait_ge(quarter_hi, 3 * (k // 4) + k % 4 + 1)
                else:
                    dve.wait_ge(w_hi, k // 4 + 1)
                lo(w4(wl, k // 4)[:, k % 4, :], w4(stage, k // 4)[:, k % 4, :], w4(wh, k // 4)[:, k % 4, :]).then_inc(
                    quarter_lo if k % 4 < 3 else w_lo, 1)

            def chunk(u, c, dst, n, n_next=2048, both=True):
                split(u + 2, 0, n_next)
                dve.wait_ge(rows_done, 3 * c + 2)
                dve.tensor_copy(dst[:, 1, :], ps[:, 1, 0:n]).then_inc(raw_dve, 1)
                dve.wait_ge(w_used, u + 2)
                dve.tensor_copy(dst[:, 3, :], ps[:, 3, 0:n]).then_inc(raw_dve, 1)
                if both:
                    split(u + 3, 1, n_next)

            chunk(U_Q, 0, q_raw, 512)
            chunk(U_KVA, 1, kva, 512, 4 * N_KVB)
            chunk(U_KVB, 2, kvb, N_KVB)
            chunk(U_V, 3, v_raw, SG, both=False)

            dve.wait_ge(tr_done, 2)
            for g in range(G):
                for par in range(2):
                    dve.tensor_copy(tok2[DH * par:DH * par + DH, 1, g, :],
                                    ps[DH * g:DH * g + DH, 5, par:SEQ:2]).then_inc(tok_v, 1)
            for t in range(2, 8):
                dve.wait_ge(op_hi, t - 1)
                if t < 4:
                    lo(k_t(atl, t - 2), ps[:, 4 + t % 4, :], k_t(ath, t - 2)).then_inc(op_lo, 1)
                else:
                    dve.scalar_tensor_tensor(out=q_t(atl)[:, t - 4, :], in0=ps[:, t - 4, :], scalar=SCALE,
                                             in1=q_t(ath)[:, t - 4, :].bitcast(fp32), op0=ALU.mult,
                                             op1=ALU.subtract).then_inc(op_lo, 1)
            split(U_U + 1, 1)
            dve.wait_ge(w2_hi, 1)
            lo(w2l[:, :, :], w2[:, :, :], w2h[:, :, :]).then_inc(w2_lo, 1)
            dve.wait_ge(gelu_ok, 1)
            for m in range(MT):
                step(dve.bn_stats(vstat[:, m, :], v_raw[:, m, :]))
                step(dve.bn_aggr(vmv[:, m, :], vstat[:, m, :]))
            dve.tensor_scalar(vrs[:, 0, :], vmv[:, :, 1], EPS, None, ALU.add).then_inc(vsq_in, 1)
            dve.wait_ge(vsq_ok, 1)
            step(dve.reciprocal(vrs[:, 2, :], vrs[:, 1, :]))
            step(dve.tensor_tensor(vrs[:, 3, :], vrs[:, 2, :], vrs[:, 2, :], ALU.mult))
            step(dve.tensor_tensor(vrs[:, 3, :], vrs[:, 3, :], vrs[:, 0, :], ALU.mult))
            step(dve.tensor_scalar(vrs[:, 3, :], vrs[:, 3, :], -0.5, 1.5, ALU.mult, ALU.add))
            step(dve.tensor_tensor(vrs[:, 3, :], vrs[:, 3, :], vrs[:, 2, :], ALU.mult))
            for m in range(MT):
                step(dve.scalar_tensor_tensor(out=v_raw[:, m, :], in0=v_raw[:, m, :], scalar=vmv[:, m, 0:1],
                                              in1=ln_g[:, :], op0=ALU.subtract, op1=ALU.mult))
                dve.scalar_tensor_tensor(out=v_raw[:, m, :], in0=v_raw[:, m, :], scalar=vrs[:, 3, m:m + 1],
                                         in1=ln_b[:, :], op0=ALU.mult, op1=ALU.add).then_inc(vln_ok, 1)
            chunk(U_U, 4, u_raw, SG)

            def hidden_lo(c):
                dve.wait_ge(hid_hi, c + 1)
                lo(hidl[:, c, :], ps[:, 2 + c, 256:256 + G * NB], hidh[:, c, :]).then_inc(hid_lo, 1)

            split(U_CV, 0)
            dve.wait_ge(wt_hi, 1)
            lo(wtl[:, :, :].rearrange("p g t -> p (g t)"), ps[:, 5, :],
               wth[:, :, :].rearrange("p g t -> p (g t)")).then_inc(wt_lo, 1)
            hidden_lo(0)
            for g in range(G):
                r = slice(DH * g, DH * g + DH)
                dve.wait_ge(cmp_hi, g + 1)
                lo(kz_diag[1][r], ps[r, 2, NB * g:NB * g + NB].rearrange("p (k n) -> p k n", k=1).broadcast_to(
                    [DH, PAIRS, NB]), kz_diag[0][r]).then_inc(cmp_lo, 1)
            split(U_MERGE1, 1)
            dve.wait_ge(vh_ok, 1)
            lo(otl[:, :, :], v_raw, oth[:, :, :]).then_inc(vl_ok, 1)
            dve.wait_ge(sct_done, 2)
            dve.tensor_copy(sct[:, 1, :], ps[:, 1, :]).then_inc(sct_out[1], 1)
            split(U_FILL0, 0)
            hidden_lo(1)
            dve.wait_ge(cmp_hi, 3)
            lo(vcl[:, :], ps[0:NB, 3, 0:P], vch[:, :]).then_inc(cmp_lo, 1)

            dve.wait_ge(masks_ready, 4)
            for g in range(G):
                dve.wait_ge(sc_done, g + 1)
                step(dve.tensor_tensor(pcmp[:, g], ps[:, g, :].rearrange("p (m k n) -> p m k n", m=MT, k=PAIRS),
                                       cbias[:, :, :].rearrange("p m (k n) -> p m k n", k=1).broadcast_to(
                                           [P, MT, PAIRS, NB]), ALU.add))
            rows = pc_flat.rearrange("p (r n) -> p r n", n=NB)

            def per_row(v):
                return v.rearrange("p (r n) -> p r n", n=1).broadcast_to([P, G * MT * PAIRS, NB])

            step(dve.tensor_reduce(cmax, rows, AX.X, ALU.max))
            dve.tensor_tensor(rows, rows, per_row(cmax), ALU.subtract).then_inc(sc_max, 1)
            split(U_FILL0 + 1, 1)
            dve.wait_ge(gelu_ok, 2)
            for gs in range(4):
                dve.wait_ge(mix_done, gs + 1)
                uv = u_raw[:, :, P * gs:P * gs + P]
                dve.scalar_tensor_tensor(out=uv, in0=ps[:, 2 + gs, :].rearrange("p (n c) -> p n c", n=MT),
                                         scalar=bsp[:, gs:gs + 1], in1=uv, op0=ALU.add,
                                         op1=ALU.mult).then_inc(sgu_ok, 1)

            def weigh_cmp():
                dve.wait_ge(sc_exp, 1)
                step(dve.tensor_reduce(csum_f, rows, AX.X, ALU.add))
                step(dve.reciprocal(csum_f, csum_f))
                step(dve.tensor_tensor(csum, csum, any_block[:, :].rearrange(
                    "p (g m k) -> p g m k", g=1, k=1).broadcast_to([P, G, MT, PAIRS]), ALU.mult))
                dve.wait_ge(gates_ok, 1)
                for g in range(G):
                    step(dve.tensor_tensor(csum[:, g], csum[:, g], gates[:, :, g, :, 0], ALU.mult))
                dve.tensor_tensor(rows, rows, per_row(csum_f), ALU.mult).then_inc(pcmp_ok, 1)

            def norm_prob(i):
                a = SOFT[i]
                qt, pp, br = STEPS[i]
                n = P * (qt + 1)
                dve.wait_ge(s_exp, 2 * a + 2)
                step(dve.reciprocal(rinv[:, a % 2, :], rsum[:, a % 2, :]))
                dve.tensor_tensor(rinv[:, a % 2, :], rinv[:, a % 2, :], gates[:, qt, :, pp, 1 + br],
                                  ALU.mult).then_inc(rinv_ok, 1)
                dve.wait_ge(rinv_ok, a + 1)
                dve.tensor_scalar(prob[:, a % 2, 0, 0:n], prob[:, a % 2, 0, 0:n], rinv[:, a % 2, 0:1],
                                  None, ALU.mult).then_inc(p_ok[0], 1)

            def lo_prob(a):
                n = G * P * (STEPS[a][0] + 1) if STEPS[a][2] < 2 else G * P
                rws = P if STEPS[a][2] < 2 else NB
                for b in range(PT_BANKS[a]):
                    dve.wait_ge(pt_hi, PT_BEFORE[a] + b + 1)
                    part = slice(512 * b, min(512 * b + 512, n))
                    lo(ptl[0:rws, part], ps[0:rws, PT0 + b, 0:part.stop - part.start],
                       pth[0:rws, part]).then_inc(pt_lo, 1)

            def lo_quarter(u, quarter):
                if quarter < 3:
                    dve.wait_ge(quarter_hi, 6 + 3 * (u - U_FILL0 - 2) + quarter + 1)
                else:
                    dve.wait_ge(w_hi, u + 1)
                part = slice(512 * quarter, 512 * quarter + 512)
                last = lo(wl[:, u % 2, part], stage[:, u % 2, part], wh[:, u % 2, part])
                if quarter == 3:
                    last.then_inc(w_lo, 1)

            for i in range(N_STEPS + 3):
                if i - 1 in SOFT:
                    norm_prob(i - 1)
                if 2 <= i < N_STEPS + 2:
                    lo_prob(i - 2)
                if i in SOFT:
                    a = SOFT[i]
                    for g in range(G):
                        dve.wait_ge(s_done, 2 * a + g + 1)
                        dve.tensor_reduce(nmax[:, a % 2, g:g + 1], ps[:, g, 0:P * (STEPS[i][0] + 1)], AX.X, ALU.max,
                                          negate=True).then_inc(s_max, 1)
                if i == 2:
                    weigh_cmp()
                if i >= 5 and i % 3 == 2:
                    w = (i - 5) // 3
                    qt, pp, _ = STEPS[3 * w]
                    dve.wait_ge(o_hi, 2 * w + 2)
                    for g in range(G):
                        o = lo(otl[DH * g:DH * g + DH, pp, P * qt:P * qt + P],
                               ps[DH * g:DH * g + DH, O0 + w % 2, P * g:P * g + P],
                               oth[DH * g:DH * g + DH, pp, P * qt:P * qt + P])
                        if g == G - 1:
                            o.then_inc(o_lo, 1)
                if i >= 1:
                    for u, quarter in QUARTERS[i - 1]:
                        lo_quarter(u, quarter)
            for u, quarter in QUARTERS[N_STEPS + 2]:
                lo_quarter(u, quarter)

            for k in range(4):
                dve.wait_ge(st_hi, k + 1)
                lo(sgl[:, k, :], ps[:, 4 + k, :], sgh[:, k, :]).then_inc(st_lo, 1)

            with dve.Fori(0, 2) as c:
                dve.wait_ge(sig_ok, 2 * c + 2)
                for f in range(4):
                    if f < 3:
                        dve.wait_ge(br_done, 6 * c + f + 1)
                    else:
                        dve.wait_ge(w_used, 2 * c + U_BRANCH + 1)
                    gt = merge[:, ds(4 * c + f, 1), :]
                    dve.tensor_tensor(gt, gt, ps[:, f:f + 1, :], ALU.mult).then_inc(br_prod, 1)
                split(2 * c + U_BRANCH + 2, 0)
                for f in range(4):
                    if f < 3:
                        dve.wait_ge(br_done, 6 * c + 3 + f + 1)
                    else:
                        dve.wait_ge(w_used, 2 * c + U_BRANCH + 2)
                    gn, gt = merge[:, ds(4 * c + f, 1), :], merge[:, ds(4 * c + f + 8, 1), :]
                    dve.tensor_tensor(gt, gt, ps[:, 4 + f:5 + f, :], ALU.mult).then_inc(br_prod, 1)
                    dve.wait_ge(br_prod, 8 * c + 4 + f + 1)
                    dve.tensor_tensor(gn, gn, gt, ALU.add).then_inc(mg_ok, 1)
                    dve.wait_ge(mg_hi, 4 * c + f + 1)
                    dve.tensor_tensor(xl[:, ds(4 * c + f, 1), :], gn, xh[:, ds(4 * c + f, 1), :].bitcast(fp32),
                                      ALU.subtract).then_inc(mg_lo, 1)
                split(2 * c + U_BRANCH + 3, 1)

            def split_to(dst, src_h, u, slot):
                dve.wait_ge(w_hi, u + 1)
                lo(dst, stage[:, slot, :], src_h).then_inc(w_lo, 1)

            def moments(m, half):
                return dve.bn_stats(stat[:, m, half, :], y[:, m, 512 * half:512 * half + 512])

            def add_rows(m, half, bank):
                ym = y[:, m, 512 * half:512 * half + 512]
                return dve.scalar_tensor_tensor(out=ym, in0=ym, scalar=ALPHA, in1=ps[:, bank, :], op0=ALU.mult,
                                                op1=ALU.add)

            def variance(m):
                step(dve.bn_aggr(mv[:, m, :], stat[:, m, :, :].rearrange("p a b -> p (a b)")))
                dve.tensor_scalar(nrm[:, m, 4:5], mv[:, m, 0:1], -1.0, None, ALU.mult)
                dve.tensor_scalar(nrm[:, m, 0:1], mv[:, m, 1:2], EPS, None, ALU.add).then_inc(var_ok, 1)

            def norm(k):
                ln, m = divmod(k, MT)
                n = nrm[:, m, :]
                dve.wait_ge(sq_ok, k + 1)
                step(dve.reciprocal(n[:, 2:3], n[:, 1:2]))
                step(dve.scalar_tensor_tensor(out=n[:, 3:4], in0=n[:, 2:3], scalar=n[:, 0:1], in1=n[:, 2:3],
                                              op0=ALU.mult, op1=ALU.mult))
                step(dve.tensor_scalar(n[:, 3:4], n[:, 3:4], -0.5, 1.5, ALU.mult, ALU.add))
                step(dve.tensor_tensor(n[:, 3:4], n[:, 3:4], n[:, 2:3], ALU.mult))
                dve.wait_ge(centred, k + 1)
                dve.scalar_tensor_tensor(out=y[:, m, :], in0=y[:, m, :], scalar=n[:, 3:4], in1=lng[:, ln, :],
                                         op0=ALU.mult, op1=ALU.mult).then_inc(scaled, 1)
                dve.wait_ge(scaled, k + 1)
                dve.tensor_tensor(y[:, m, 0:BIAS_COLS], y[:, m, 0:BIAS_COLS], lnb[:, ln, 0:BIAS_COLS],
                                  ALU.add).then_inc(h_ok[0], 1)

            def ht_lo_of(m):
                dve.wait_ge(ht_hi, m + 1)
                lo(htl[:, :, P * m:P * m + P],
                   ps[:, 4 + 2 * (m % 2):6 + 2 * (m % 2), :].rearrange("p b (k t) -> p (b k) t", k=4),
                   hth[:, :, P * m:P * m + P]).then_inc(ht_lo, 1)

            dve.wait_ge(x2_arrived, 16)
            split(U_OUT + 2, 0)
            for m in range(MT):
                if m < 3:
                    dve.wait_ge(rows_done, 15 + m + 1)
                else:
                    dve.wait_ge(w_used, U_OUT + 2)
                add_rows(m, 0, m).then_inc(mg_lo, 1)
            split(U_OUT + 3, 1)
            dve.wait_ge(mg_lo, KD + MT)
            for m in range(MT):
                moments(m, 0)
            split_to(first_l[:, :], first_h[:, :], U_FFN, 0)
            dve.wait_ge(ln_arrived, 64)
            for m in range(MT):
                if m < 3:
                    dve.wait_ge(rows_done, 18 + m + 1)
                else:
                    dve.wait_ge(w_used, U_FFN)
                add_rows(m, 1, m).then_inc(mg_lo, 1)
                dve.wait_ge(mg_lo, KD + MT + m + 1)
                step(moments(m, 1))
                variance(m)
                if m == 2:
                    ht_lo_of(0)
                    ht_lo_of(1)
                if m == 3:
                    split(U_FFN + 1, 1)
                norm(m)
            ht_lo_of(2)
            ht_lo_of(3)

            def ffn(i):
                u = 2 * i + U_FFN
                split(u + 2, 0)
                for f in range(2):
                    dve.wait_ge(silu_ok, 2 * i + f + 1)
                    if f == 0:
                        dve.wait_ge(ffn_half, 2 * i + 2)
                    else:
                        dve.wait_ge(w_used, u + 2)
                    dve.tensor_tensor(fact[:, ds(2 * i + f, 1), :], hid_sg[:, f:f + 1, :], ps[:, 2 + f:3 + f, :],
                                      ALU.mult).then_inc(fact_ok, 1)
                split(u + 3, 1)

            def tiles_lo(j, slot):
                dve.wait_ge(a_hi, j + 1)
                dve.tensor_tensor(al[:, slot, :, :], fact[:, ds(2 * j, 2), :], ah[:, slot, :, :].bitcast(fp32),
                                  ALU.subtract).then_inc(a_lo, 1)

            with dve.Fori(0, FT // 2 - 1) as i:
                ffn(i)
            tiles_lo(0, 0)
            tiles_lo(1, 1)
            ffn(FT // 2 - 1)
            with dve.Fori(0, (N_DOWN - 5) // 2) as i:
                for b in range(2):
                    split(2 * i + U_DOWN + b + 2, b)
                    tiles_lo(2 * i + b + 2, b)
            split(U_DOWN + N_DOWN - 3, 0)
            tiles_lo(N_DOWN - 3, 0)
            split_to(late_l, late_h, U_DOWN + N_DOWN - 2, 1)
            tiles_lo(N_DOWN - 2, 2)
            tiles_lo(N_DOWN - 1, 3)
            split_to(wl[:, 1, :], wh[:, 1, :], U_DOWN + N_DOWN - 1, 0)
            for m in range(MT):
                for half in range(2):
                    dve.wait_ge(rows_out, 2 * m + half + 1)
                    step(add_rows(m, half, 2 * m + half))
                    step(moments(m, half))
                variance(m)
                norm(MT + m)

        @block.tensor
        def _(pe):
            def one_pass(i, out, sh, sl, mh, ml, start, stop):
                return pe.matmul(out, (sh, sh, sl)[i], (mh, ml, mh)[i], start=start and i == 0, stop=stop and i == 2)

            def mm3(*product):
                return [one_pass(i, *product) for i in range(3)][-1]

            def transpose(out, in_, k=P):
                return pe.transpose(out, in_, ident[0:k, 0:k])

            def x_tile(k):
                pe.wait_ge(x_arrived[k], 16)
                if k >= 4:
                    pe.wait_ge(xt_lo, k - 3)
                for m in range(MT):
                    last = transpose(ps[:, 4 + k % 4, P * m:P * m + P], x_sb[:, m, P * k:P * k + P])
                last.then_inc(xt_done, 1)

            pe.wait_ge(ident_ready, 1)
            x_tile(0)
            for k in range(KD):
                if k + 1 < KD:
                    x_tile(k + 1)
                pe.wait_ge(xt_lo, k + 1)
                if k % 4 < 3:
                    pe.wait_ge(quarter_lo, 3 * (k // 4) + k % 4 + 1)
                else:
                    pe.wait_ge(w_lo, k // 4 + 1)
                for m in range(MT):
                    tok = slice(P * m, P * m + P)
                    last = mm3(ps[:, m, :], xh[:, k, tok], xl[:, k, tok], w4(wh, k // 4)[:, k % 4, :],
                               w4(wl, k // 4)[:, k % 4, :], k == 0, k == KD - 1)
                    if k == KD - 1 and m < MT - 1:
                        last.then_inc(rows_done, 1)
                if k % 4 == 3:
                    last.then_inc(w_used, 1)

            def tokens(u, lh, ll, n, before):
                for kh in range(2):
                    pe.wait_ge(w_lo, u + kh + 1)
                    before(kh, None)
                    for m in range(MT):
                        before(kh, m)
                        for k in range(4):
                            kk = 4 * kh + k
                            tok = slice(P * m, P * m + P)
                            last = mm3(ps[:, m, 0:n], lh[:, kk, tok], ll[:, kk, tok], w4(wh, kh, n)[:, k, :],
                                       w4(wl, kh, n)[:, k, :], kk == 0, kk == KD - 1)
                        if kh == 1 and m < MT - 1:
                            last.then_inc(rows_done, 1)
                    last.then_inc(w_used, 1)

            def bank_free(c):
                def before(kh, m):
                    if kh == 0 and m is not None:
                        pe.wait_ge(raw_dve if m % 2 else raw_act, 2 * (c - 1) + m // 2 + 1)
                return before

            tokens(U_KVA, xh, xl, 512, bank_free(1))
            tokens(U_KVB, xh, xl, N_KVB, bank_free(2))
            pe.wait_ge(small_arrived, 160)
            pe.wait_ge(xt_lo, KD)
            for c in range(2):
                last = transpose(ps[:, 7, 16 * c:16 * c + 16], pe_in[:, c, :], 16)
            last.then_inc(pe_tr, 1)
            tokens(U_V, xh, xl, SG, bank_free(3))

            pe.wait_ge(roped, 1)
            for t in range(8):
                if t == 3:
                    pe.wait_ge(pe_ok, 1)
                if t >= 4:
                    bank_free(4)(0, t - 4)
                for m in range(MT):
                    src = (kva[:, m, P * t:P * t + P] if t < 3 else
                           kvb[:, m, 0:P] if t == 3 else q_perm[:, m, P * (t - 4):P * (t - 4) + P])
                    last = transpose(ps[:, (4 + t) % 8, P * m:P * m + P], src)
                last.then_inc(tr_done, 1)

            def queries_out(kh, m):
                if kh == 0 and m is not None:
                    pe.wait_ge(op_lo, 3 + m)
            tokens(U_U, xh, xl, SG, queries_out)

            def merge_piece(u, piece, f):
                half, k = piece // KD, piece % KD
                if piece == 0:
                    pe.wait_ge(w_lo, u + 1)
                if k == 0 and f >= 2:
                    pe.wait_ge(merge_out, f - 1)
                col = slice(P * half, P * half + P)
                last = mm3(ps[:, M0 + half, :], w8(wh, u % 2)[:, k, col], w8(wl, u % 2)[:, k, col],
                           xh[:, k, :], xl[:, k, :], k == 0, k == KD - 1)
                if k == KD - 1:
                    last.then_inc(w_used if half else merge_half, 1)

            def compress(c, u):
                pe.wait_ge(w_lo, u + 1)
                pe.wait_ge(flat_ok, c + 1)
                for j in range(16):
                    cols = slice(G * NB * j, G * NB * (j + 1))
                    last = mm3(ps[0:G * NB, 4 + c, 0:P], flath[:, c, cols], flatl[:, c, cols],
                               w16(wh, u % 2)[:, j, :], w16(wl, u % 2)[:, j, :], j == 0, j == 15)
                last.then_inc(w_used, 1)

            def hidden_transposed(c):
                pe.wait_ge(hid_ok, c + 1)
                transpose(ps[:, 2 + c, 256:256 + G * NB], hid[:, c, :], G * NB).then_inc(hid_tr, 1)

            pe.wait_ge(tok_k, 4)
            compress(0, U_CK)
            pe.wait_ge(masks_ready, 4)
            pe.wait_ge(tok_v, 4)
            for gs in range(4):
                last = transpose(ps[:, 5, P * gs:P * gs + P], wsp[:, gs, :])
            last.then_inc(wt_done, 1)
            pe.wait_ge(op_lo, 2)
            pe.wait_ge(raw_dve, 10)
            pe.wait_ge(raw_act, 10)
            for piece in range(2 * KD):
                merge_piece(U_MERGE0, piece, piece // KD)
                if piece == 5:
                    hidden_transposed(0)
                if piece == 9:
                    pe.wait_ge(w2_lo, 1)
                    pe.wait_ge(hid_lo, 1)
                    dup = slice(0, 2 * DH)
                    k2h, k2l = [t[:, :, :].rearrange("p a b -> p (a b)")[:, dup] for t in (w2h, w2l)]
                    mm3(ps[:, 2, 0:G * NB], k2h, k2l, hidh[:, 0, :], hidl[:, 0, :], True, True).then_inc(cmp_done, 1)
            pe.wait_ge(wt_lo, 1)
            compress(1, U_CV)
            pe.wait_ge(cmp_lo, 2)
            for g in range(G):
                r = slice(DH * g, DH * g + DH)
                for pp in range(PAIRS):
                    last = mm3(ps[:, g, :], kz[0][r, pp, :], kz[1][r, pp, :], q_t(ath)[r, pp, :], q_t(atl)[r, pp, :],
                               pp == 0, pp == PAIRS - 1)
                last.then_inc(sct_done, 1)
            for piece in range(2 * KD):
                merge_piece(U_MERGE1, piece, 2 + piece // KD)
                if piece == 2:
                    hidden_transposed(1)
                if piece == 4:
                    for g in range(G):
                        pe.wait_ge(sct_out[g], 1)
                        for m in range(MT):
                            last = transpose(ps[:, g, P * m:P * m + P], sct[:, g, P * m:P * m + P])
                        last.then_inc(sc_done, 1)
                if piece == 9:
                    pe.wait_ge(hid_lo, 2)
                    for g in range(G):
                        n = slice(NB * g, NB * g + NB)
                        last = mm3(ps[0:NB, 3, DH * g:DH * g + DH], hidh[:, 1, n], hidl[:, 1, n], w2h[:, 2, :],
                                   w2l[:, 2, :], True, True)
                    last.then_inc(cmp_done, 1)
            pe.wait_ge(vl_ok, 1)
            pe.wait_ge(cmp_lo, 3)
            pe.wait_ge(hid_ok, 2)
            for gs in range(4):
                cols = slice(P * gs, P * gs + P)
                mm3(ps[:, 2 + gs, :], wth[:, gs, :], wtl[:, gs, :], oth[:, :, cols], otl[:, :, cols],
                    True, True).then_inc(mix_done, 1)

            piece = 0

            def fill(until):
                nonlocal piece
                while piece < until:
                    merge_piece(U_FILL0 + piece // (2 * KD), piece % (2 * KD), 4 + piece // KD)
                    piece += 1

            fill(FILL_AT[0])
            for i in range(N_STEPS + 3):
                if i >= 3:
                    a = i - 3
                    qt, pp, br = STEPS[a]
                    w = a // 3
                    if br == 0 and w >= 2:
                        pe.wait_ge(o_lo, w - 1)
                    out = ps[:, O0 + w % 2, 0:G * P]
                    if br < 2:
                        for kt in range(qt + 1):
                            if kt % 2 == 0:
                                pe.wait_ge(pt_lo, PT_BEFORE[a] + kt // 2 + 1)
                            c = slice(G * P * kt, G * P * (kt + 1))
                            last = mm3(out, v_t(ath, br)[:, kt, :], v_t(atl, br)[:, kt, :], pth[:, c], ptl[:, c],
                                       br == 0 and kt == 0, False)
                    else:
                        pe.wait_ge(pt_lo, PT_BEFORE[a] + 1)
                        last = mm3(out, vch[:, :], vcl[:, :], pth[0:NB, 0:G * P], ptl[0:NB, 0:G * P], False, True)
                    last.then_inc(pv_done, 1)
                if 2 <= i < N_STEPS + 2:
                    a = i - 2
                    qt, pp, br = STEPS[a]
                    if a == 0:
                        pe.wait_ge(sgu_ok, 4)
                        pe.wait_ge(roped, 3)
                    if br < 2:
                        s = SOFT[a]
                        for b in range(PT_BANKS[a]):
                            for g in range(G):
                                if b == 0:
                                    pe.wait_ge(p_ok[g], s + 1)
                                for kt in range(2 * b, min(2 * b + 2, qt + 1)):
                                    at = G * P * (kt % 2) + P * g
                                    last = transpose(ps[:, PT0 + b, at:at + P], prob[:, s % 2, g, P * kt:P * kt + P])
                            last.then_inc(pt_done, 1)
                    else:
                        if a == 2:
                            pe.wait_ge(pcmp_ok, 1)
                        for g in range(G):
                            last = transpose(ps[0:NB, PT0, P * g:P * g + P], pcmp[:, g, qt, pp, :])
                        last.then_inc(pt_done, 1)
                if i in SOFT:
                    qt, pp, br = STEPS[i]
                    n = P * (qt + 1)
                    for g in range(G):
                        if i == 0:
                            pe.wait_ge(sc_max, 1)
                        else:
                            pe.wait_ge(s_exp, 2 * SOFT[i] - 1 + g)
                        r = slice(DH * g, DH * g + DH)
                        tok = slice(P * qt, P * qt + P)
                        mm3(ps[:, g, 0:n], q_t(ath)[r, pp, tok], q_t(atl)[r, pp, tok], k_t(ath, br)[r, 0:n],
                            k_t(atl, br)[r, 0:n], True, False)
                        pe.matmul(ps[:, g, n - P:n], ident_r[:, :], causal[:, :], start=False,
                                  stop=True).then_inc(s_done, 1)
                fill(FILL_AT[i + 1])

            for k in range(4):
                if k == 0:
                    pe.wait_ge(o_lo, MT * PAIRS)
                if k == 2:
                    pe.wait_ge(merge_out, 2 * N_MERGE)
                for m in range(MT):
                    last = transpose(ps[:, 4 + k, P * m:P * m + P], u_raw[:, m, P * k:P * k + P])
                last.then_inc(st_done, 1)

            with pe.Fori(0, 2) as c:
                for b, (oh, ol) in enumerate(((oth, otl), (sgh, sgl))):
                    pe.wait_ge(w_lo, 2 * c + U_BRANCH + b + 1)
                    if b:
                        pe.wait_ge(st_lo, 4)
                        pe.wait_ge(br_prod, 8 * c + 1)
                    for f in range(4):
                        for k in range(4):
                            col = slice(P * f, P * f + P)
                            last = mm3(ps[:, 4 * b + f, :], w4(wh, b)[:, k, col], w4(wl, b)[:, k, col], oh[:, k, :],
                                       ol[:, k, :], k == 0, k == 3)
                        if f < 3:
                            last.then_inc(br_done, 1)
                    last.then_inc(w_used, 1)
                pe.wait_ge(br_prod, 8 * c + 4)

            def before(kh, m):
                if m is None:
                    pe.wait_ge(mg_lo, 4 * kh + 4)
            tokens(U_OUT, xh, xl, 512, before)

            def h_transposed(m):
                for h in h_ok:
                    pe.wait_ge(h, m + 1)
                if m >= 2:
                    pe.wait_ge(ht_lo, m - 1)
                for k in range(KD):
                    last = transpose(ps[:, 4 + 2 * (m % 2) + k // 4, P * (k % 4):P * (k % 4) + P],
                                     y[:, m, P * k:P * k + P])
                last.then_inc(ht_done, 1)

            def last_rows(m, kh):
                tok = slice(P * m, P * m + P)
                if kh == 0:
                    pe.wait_ge(mg_lo, KD + m + 1)
                for k in range(4):
                    last = mm3(ps[:, m, :], xh[:, 4 * kh + k, tok], xl[:, 4 * kh + k, tok], w4(wh, kh)[:, k, :],
                               w4(wl, kh)[:, k, :], kh == 0 and k == 0, kh == 1 and k == 3)
                if m == MT - 1:
                    last.then_inc(w_used, 1)
                elif kh == 1:
                    last.then_inc(rows_done, 1)

            pe.wait_ge(w_lo, U_OUT + 3)
            last_rows(0, 0)
            last_rows(1, 0)
            pe.wait_ge(w_lo, U_OUT + 4)
            last_rows(0, 1)
            last_rows(1, 1)
            last_rows(2, 0)
            h_transposed(0)
            last_rows(2, 1)
            last_rows(3, 0)
            h_transposed(1)
            last_rows(3, 1)

            def ffn_tile(b, f, gh, gl, tok=slice(0, SEQ)):
                for k in range(KD):
                    col = slice(P * f, P * f + P)
                    last = mm3(ps[:, 2 * b + f, tok], gh[:, k, col], gl[:, k, col], hth[:, k, tok], htl[:, k, tok],
                               k == 0, k == KD - 1)
                return last

            views = [tuple(t[:, :].rearrange("p (k n) -> p k n", k=8) for t in (first_h, first_l)),
                     (w8(wh, 1), w8(wl, 1))]
            h_transposed_at = {(0, 1): 2, (1, 1): 3}
            pe.wait_ge(ht_lo, 2)
            for half in range(2):
                tok = slice(SEQ // 2 * half, SEQ // 2 * half + SEQ // 2)
                for b, (gh, gl) in enumerate(views):
                    if half == 0:
                        pe.wait_ge(w_lo, U_FFN + b + 1)
                        pe.wait_ge(mg_lo, KD + MT + 2 * b + 2)
                    elif b == 0:
                        pe.wait_ge(ht_lo, MT)
                    for f in range(2):
                        if half == 0 and (b, f) in h_transposed_at:
                            h_transposed(h_transposed_at[b, f])
                        last = ffn_tile(b, f, gh, gl, tok)
                        if half == 1:
                            last.then_inc(w_used if f else ffn_half, 1)
            pe.wait_ge(silu_ok, 2)
            with pe.Fori(1, FT // 2) as i:
                for b in range(2):
                    pe.wait_ge(w_lo, 2 * i + U_FFN + b + 1)
                    for f in range(2):
                        ffn_tile(b, f, w8(wh, b), w8(wl, b)).then_inc(w_used if f else ffn_half, 1)
                pe.wait_ge(silu_ok, 2 * i + 2)

            def down(m, half, f, ring, dh, dl, start, stop):
                tok = slice(P * m, P * m + P)
                c = slice(512 * half, 512 * half + 512)
                return mm3(ps[:, 2 * m + half, :], ah[:, ring, f, tok], al[:, ring, f, tok], dh[:, f, c], dl[:, f, c],
                           start, stop)

            def down_unit(j, slot, start=False):
                pe.wait_ge(w_lo, U_DOWN + 1 + j)
                pe.wait_ge(a_lo, j + 1)
                for m in ((2, 3, 0, 1) if start else range(MT)):
                    if start and m == 0:
                        pe.wait_ge(fact_ok, FT)
                    for f in range(2):
                        for half in range(2):
                            last = down(m, half, f, slot, w2d(wh, slot), w2d(wl, slot), start and f == 0, False)
                last.then_inc(w_used, 1)

            down_unit(0, 0, True)
            down_unit(1, 1)
            with pe.Fori(1, (N_DOWN - 3) // 2) as i:
                for b in range(2):
                    down_unit(2 * i + b, b)
            late = ((0, w2d(wh, 0), w2d(wl, 0)),
                    (2, late_h.rearrange("p (f n) -> p f n", f=2), late_l.rearrange("p (f n) -> p f n", f=2)),
                    (3, w2d(wh, 1), w2d(wl, 1)))
            for m in range(MT):
                order = ([(half, j) for half in range(2) for j in range(3)] if m else
                         [(half, j) for j in range(3) for half in range(2)])
                for half, j in order:
                    ring, dh, dl = late[j]
                    if m == 0 and half == 0:
                        pe.wait_ge(w_lo, U_DOWN + N_DOWN - 2 + j)
                        pe.wait_ge(a_lo, N_DOWN - 2 + j)
                    for f in range(2):
                        last = down(m, half, f, ring, dh, dl, False, j == 2 and f == 1)
                    if j == 2:
                        last.then_inc(rows_out, 1)


_INS = ["x", "positions", "w_in", "pe_ck", "w_ck1", "w_ck2", "pe_cv", "w_cv1", "w_cv2", "ln_sgu_g", "ln_sgu_b",
        "w_spatial", "b_spatial", "w_branch_nsa", "w_branch_sgu", "w_out", "ln1_g", "ln1_b", "w_ffn_gate",
        "w_ffn_up", "w_ffn_down", "ln2_g", "ln2_b"]


def kernel(**inputs):
    import numpy as np
    import concourse.bacc as bacc
    from concourse import mybir
    from concourse.bass_utils import run_bass_kernel_spmd

    nc = bacc.Bacc("TRN2", target_bir_lowering=False, num_devices=1)
    arrays, tensors = {}, {}
    for name in _INS:
        a = np.ascontiguousarray(inputs[name])
        arrays[f"in_{name}"] = a
        tensors[name] = nc.dram_tensor(f"in_{name}", a.shape, mybir.dt.from_np(a.dtype), kind="ExternalInput").ap()
    tensors["out"] = nc.dram_tensor("out", inputs["x"].shape, mybir.dt.float32, kind="ExternalOutput").ap()
    build_layer(nc, tensors)
    result = run_bass_kernel_spmd(nc, [arrays], core_ids=[0])
    return result.results[0]["out"]
```
